# Optimizing a Trainium2 kernel written in Bass

```python
import jax
import jax.numpy as jnp
from jax import lax
import numpy as np

D_MODEL = 1024
BATCH = 1
SEQ = 512
DEPTH = 2
DEC_BATCH = 1
DEC_SEQ = 64
PAST_LEN = 1024

CHUNK = 64
HEAD_DIM = 64
A_HEADS = 4
A_WIDTH = A_HEADS * HEAD_DIM
A_BAND_CHUNKS = 8
A_WINDOW = A_BAND_CHUNKS * CHUNK
REL_MAX = 128
REL_SIZE = REL_MAX + CHUNK
B_HEADS = 8
B_WIDTH = B_HEADS * HEAD_DIM
Q_BLOCK = 128
C_GROUPS = 4
C_GROUP_W = 64
C_WIDTH = C_GROUPS * C_GROUP_W
C_CHUNK = 128
N_BRANCH = 3
P_TOTAL = 3 * A_WIDTH + 3 * B_WIDTH + B_HEADS + 2 * C_WIDTH + N_BRANCH * D_MODEL
D_FF = 2752
FFN_RES = 0.5
N_MOD = 9
RMS_EPS = 1e-6
NEG_INF = -1e30
FORGET_BIAS_INIT = 3.0

kernel_name = "hybrid_streaming_encoder_step"

def rmsnorm(x, g):
    xf = x.astype(jnp.float32)
    y = xf * lax.rsqrt(jnp.mean(xf * xf, axis=-1, keepdims=True) + RMS_EPS)
    return (y * g.astype(jnp.float32)).astype(x.dtype)

def adaln(c, w_ada, b_ada):
    return jnp.split(jax.nn.silu(c) @ w_ada + b_ada, N_MOD, axis=-1)

def pre_mod(h, g_pre, shift, scale):
    return rmsnorm(h, g_pre) * (1 + scale[:, None, :]) + shift[:, None, :]

def post_add(h, y, g_post, gate, weight):
    return h + weight * gate[:, None, :] * rmsnorm(y, g_post)

def swiglu(x, w1, w2):
    g, u = jnp.split(x @ w1, 2, axis=-1)
    return (jax.nn.silu(g) * u) @ w2

def in_proj_split(x, w_in, b_forget, c_vnorm_g):
    B, T, _ = x.shape
    sizes = [A_WIDTH] * 3 + [B_WIDTH] * 3 + [B_HEADS] + [C_WIDTH] * 2
    cuts = [int(i) for i in np.cumsum(sizes)]
    qa, ka, va, qb, kb, vb, fb, uc, vc, gl = jnp.split(x @ w_in, cuts, axis=-1)
    def heads(t, h):
        return t.reshape(B, T, h, HEAD_DIM)
    logf = jax.nn.log_sigmoid(fb.astype(jnp.float32) + b_forget.astype(jnp.float32))
    vc = rmsnorm(vc, c_vnorm_g)
    return (heads(qa, A_HEADS), heads(ka, A_HEADS), heads(va, A_HEADS),
            heads(qb, B_HEADS), heads(kb, B_HEADS), heads(vb, B_HEADS), logf, uc, vc, gl)

def band_attention(q, k, v, q_pos, k_pos, rel_bias):
    s = jnp.einsum('bqhd,bkhd->bhqk', q, k).astype(jnp.float32) * (HEAD_DIM ** -0.5)
    rel = jnp.clip(q_pos[:, None] - k_pos[None, :], -(CHUNK - 1), REL_MAX) + (CHUNK - 1)
    s = s + rel_bias.astype(jnp.float32)[:, rel][None]
    qc = q_pos[:, None] // CHUNK
    kc = k_pos[None, :] // CHUNK
    mask = (kc <= qc) & (kc >= qc - A_BAND_CHUNKS) & (k_pos[None, :] >= 0)
    s = jnp.where(mask[None, None], s, NEG_INF)
    p = jax.nn.softmax(s, axis=-1).astype(v.dtype)
    return jnp.einsum('bhqk,bkhd->bqhd', p, v)

def band_attention_prompt(q, k, v, rel_bias):
    B, T = q.shape[:2]
    pad = ((0, 0), (A_WINDOW, 0), (0, 0), (0, 0))
    kp = jnp.pad(k, pad)
    vp = jnp.pad(v, pad)
    band = A_WINDOW + CHUNK
    def one_chunk(c):
        start = c * CHUNK
        qc = lax.dynamic_slice_in_dim(q, start, CHUNK, axis=1)
        kc = lax.dynamic_slice_in_dim(kp, start, band, axis=1)
        vc = lax.dynamic_slice_in_dim(vp, start, band, axis=1)
        q_pos = start + jnp.arange(CHUNK)
        k_pos = start - A_WINDOW + jnp.arange(band)
        return band_attention(qc, kc, vc, q_pos, k_pos, rel_bias)
    out = lax.map(one_chunk, jnp.arange(T // CHUNK))
    return jnp.moveaxis(out, 0, 1).reshape(B, T, A_HEADS, HEAD_DIM)

def fox_block(q, k, v, f_q, f_k, q_pos, k_pos):
    s = jnp.einsum('bqhd,bkhd->bhqk', q, k).astype(jnp.float32) * (HEAD_DIM ** -0.5)
    s = s + jnp.swapaxes(f_q, 1, 2)[..., :, None] - jnp.swapaxes(f_k, 1, 2)[..., None, :]
    mask = k_pos[None, :] <= q_pos[:, None]
    s = jnp.where(mask[None, None], s, NEG_INF)
    p = jax.nn.softmax(s, axis=-1).astype(v.dtype)
    return jnp.einsum('bhqk,bkhd->bqhd', p, v)

def fox_prompt(q, k, v, logf):
    B, T = q.shape[:2]
    F = jnp.cumsum(logf, axis=1)
    pos = jnp.arange(T)
    def one_block(i):
        start = i * Q_BLOCK
        qb = lax.dynamic_slice_in_dim(q, start, Q_BLOCK, axis=1)
        fq = lax.dynamic_slice_in_dim(F, start, Q_BLOCK, axis=1)
        return fox_block(qb, k, v, fq, F, start + jnp.arange(Q_BLOCK), pos)
    out = lax.map(one_block, jnp.arange(T // Q_BLOCK))
    return jnp.moveaxis(out, 0, 1).reshape(B, T, B_HEADS, HEAD_DIM)

def spatial_gating(u, v, w_s, b_s):
    B, T, _ = u.shape
    L = min(T, C_CHUNK)
    tri = jnp.tril(jnp.ones((L, L), w_s.dtype))
    wm = w_s[:, :L, :L] * tri
    vr = v.reshape(B, T // L, L, C_GROUPS, C_GROUP_W)
    mixed = jnp.einsum('gij,bnjgc->bnigc', wm, vr) + jnp.swapaxes(b_s[:, :L], 0, 1)[None, None, :, :, None]
    return u * mixed.reshape(B, T, C_WIDTH)

def merge_branches(oa, ob, oc, gl, b_gate, w_br_a, w_br_b, w_br_c, w_out):
    B, T = oa.shape[:2]
    ga, gb, gc = jnp.split(jax.nn.sigmoid(gl + b_gate), N_BRANCH, axis=-1)
    m = (ga * (oa.reshape(B, T, A_WIDTH) @ w_br_a)
         + gb * (ob.reshape(B, T, B_WIDTH) @ w_br_b)
         + gc * (oc @ w_br_c))
    return m @ w_out

def mixer_prompt(x, w_in, b_forget, a_rel_bias, c_vnorm_g, c_spatial_w, c_spatial_b,
                 b_gate, w_br_a, w_br_b, w_br_c, w_out):
    T = x.shape[1]
    qa, ka, va, qb, kb, vb, logf, uc, vc, gl = in_proj_split(x, w_in, b_forget, c_vnorm_g)
    oa = band_attention_prompt(qa, ka, va, a_rel_bias)
    ob = fox_prompt(qb, kb, vb, logf)
    oc = spatial_gating(uc, vc, c_spatial_w, c_spatial_b)
    y = merge_branches(oa, ob, oc, gl, b_gate, w_br_a, w_br_b, w_br_c, w_out)
    rows = min(A_WINDOW, T)
    return y, (ka[:, T - rows:], va[:, T - rows:], kb, vb, logf)

def mixer_sample(x, a_k, a_v, b_k, b_v, b_logf, w_in, b_forget, a_rel_bias, c_vnorm_g,
                 c_spatial_w, c_spatial_b, b_gate, w_br_a, w_br_b, w_br_c, w_out):
    Tn = x.shape[1]
    past = b_k.shape[1]
    rows = a_k.shape[1]
    qa, ka, va, qb, kb, vb, logf, uc, vc, gl = in_proj_split(x, w_in, b_forget, c_vnorm_g)
    q_pos = past + jnp.arange(Tn)
    ka_all = jnp.concatenate([a_k, ka], axis=1)
    va_all = jnp.concatenate([a_v, va], axis=1)
    oa = band_attention(qa, ka_all, va_all, q_pos, past - rows + jnp.arange(rows + Tn), a_rel_bias)
    kb_all = jnp.concatenate([b_k, kb], axis=1)
    vb_all = jnp.concatenate([b_v, vb], axis=1)
    F = jnp.cumsum(jnp.concatenate([b_logf.astype(jnp.float32), logf], axis=1), axis=1)
    ob = fox_block(qb, kb_all, vb_all, F[:, past:], F, q_pos, jnp.arange(past + Tn))
    oc = spatial_gating(uc, vc, c_spatial_w, c_spatial_b)
    y = merge_branches(oa, ob, oc, gl, b_gate, w_br_a, w_br_b, w_br_c, w_out)
    return y, (ka_all[:, Tn:], va_all[:, Tn:], kb, vb, logf, vc)

def setup_inputs(seed: int = 0) -> dict:
    key = jax.random.key(seed)
    ks = jax.random.split(key, 26)
    def nrm(k, shape, s=1.0):
        return jax.random.normal(k, shape, jnp.float32) * s
    a_rows = min(A_WINDOW, PAST_LEN)
    return {
        "x_prompt": nrm(ks[0], (BATCH, SEQ, D_MODEL)),
        "x_sample": nrm(ks[1], (DEC_BATCH, DEC_SEQ, D_MODEL)),
        "c_prompt": nrm(ks[2], (BATCH, D_MODEL)),
        "c_sample": nrm(ks[3], (DEC_BATCH, D_MODEL)),
        "cache_a_k": nrm(ks[4], (DEPTH, DEC_BATCH, a_rows, A_HEADS, HEAD_DIM)),
        "cache_a_v": nrm(ks[5], (DEPTH, DEC_BATCH, a_rows, A_HEADS, HEAD_DIM)),
        "cache_b_k": nrm(ks[6], (DEPTH, DEC_BATCH, PAST_LEN, B_HEADS, HEAD_DIM)),
        "cache_b_v": nrm(ks[7], (DEPTH, DEC_BATCH, PAST_LEN, B_HEADS, HEAD_DIM)),
        "cache_b_logf": jax.nn.log_sigmoid(FORGET_BIAS_INIT + nrm(ks[8], (DEPTH, DEC_BATCH, PAST_LEN, B_HEADS))),
        "w_ada": nrm(ks[9], (DEPTH, D_MODEL, N_MOD * D_MODEL), 0.5 * D_MODEL ** -0.5),
        "b_ada": nrm(ks[10], (DEPTH, N_MOD * D_MODEL), 0.02),
        "norm_g": 1.0 + nrm(ks[11], (DEPTH, 6, D_MODEL), 0.01),
        "ffn_w1": nrm(ks[12], (DEPTH, 2, D_MODEL, 2 * D_FF), D_MODEL ** -0.5),
        "ffn_w2": nrm(ks[13], (DEPTH, 2, D_FF, D_MODEL), D_FF ** -0.5),
        "w_in": nrm(ks[14], (DEPTH, D_MODEL, P_TOTAL), D_MODEL ** -0.5),
        "b_forget": FORGET_BIAS_INIT + nrm(ks[15], (DEPTH, B_HEADS), 0.1),
        "b_gate": nrm(ks[16], (DEPTH, N_BRANCH * D_MODEL), 0.02),
        "a_rel_bias": nrm(ks[17], (DEPTH, A_HEADS, REL_SIZE), 0.5),
        "c_vnorm_g": 1.0 + nrm(ks[18], (DEPTH, C_WIDTH), 0.01),
        "c_spatial_w": nrm(ks[19], (DEPTH, C_GROUPS, C_CHUNK, C_CHUNK), C_CHUNK ** -0.5),
        "c_spatial_b": 1.0 + nrm(ks[20], (DEPTH, C_GROUPS, C_CHUNK), 0.1),
        "w_br_a": nrm(ks[21], (DEPTH, A_WIDTH, D_MODEL), A_WIDTH ** -0.5),
        "w_br_b": nrm(ks[22], (DEPTH, B_WIDTH, D_MODEL), B_WIDTH ** -0.5),
        "w_br_c": nrm(ks[23], (DEPTH, C_WIDTH, D_MODEL), C_WIDTH ** -0.5),
        "w_out": nrm(ks[24], (DEPTH, D_MODEL, D_MODEL), D_MODEL ** -0.5),
    }

def reference(x_prompt, x_sample, c_prompt, c_sample, cache_a_k, cache_a_v, cache_b_k, cache_b_v,
              cache_b_logf, w_ada, b_ada, norm_g, ffn_w1, ffn_w2, w_in, b_forget, b_gate, a_rel_bias,
              c_vnorm_g, c_spatial_w, c_spatial_b, w_br_a, w_br_b, w_br_c, w_out):
    hp, hs = x_prompt, x_sample
    sp = [[] for _ in range(5)]
    ss = [[] for _ in range(6)]
    for l in range(DEPTH):
        mp = adaln(c_prompt, w_ada[l], b_ada[l])
        ms = adaln(c_sample, w_ada[l], b_ada[l])
        g = norm_g[l]
        mw = (w_in[l], b_forget[l], a_rel_bias[l], c_vnorm_g[l], c_spatial_w[l], c_spatial_b[l],
              b_gate[l], w_br_a[l], w_br_b[l], w_br_c[l], w_out[l])
        hp = post_add(hp, swiglu(pre_mod(hp, g[0], mp[0], mp[1]), ffn_w1[l, 0], ffn_w2[l, 0]), g[1], mp[2], FFN_RES)
        hs = post_add(hs, swiglu(pre_mod(hs, g[0], ms[0], ms[1]), ffn_w1[l, 0], ffn_w2[l, 0]), g[1], ms[2], FFN_RES)
        yp, st_p = mixer_prompt(pre_mod(hp, g[2], mp[3], mp[4]), *mw)
        hp = post_add(hp, yp, g[3], mp[5], 1.0)
        ys, st_s = mixer_sample(pre_mod(hs, g[2], ms[3], ms[4]), cache_a_k[l], cache_a_v[l], cache_b_k[l],
                                cache_b_v[l], cache_b_logf[l], *mw)
        hs = post_add(hs, ys, g[3], ms[5], 1.0)
        hp = post_add(hp, swiglu(pre_mod(hp, g[4], mp[6], mp[7]), ffn_w1[l, 1], ffn_w2[l, 1]), g[5], mp[8], FFN_RES)
        hs = post_add(hs, swiglu(pre_mod(hs, g[4], ms[6], ms[7]), ffn_w1[l, 1], ffn_w2[l, 1]), g[5], ms[8], FFN_RES)
        for lst, st in zip(sp, st_p):
            lst.append(st)
        for lst, st in zip(ss, st_s):
            lst.append(st)
    new_a_k_prompt, new_a_v_prompt, new_b_k_prompt, new_b_v_prompt, new_b_logf_prompt = [jnp.stack(s, 0) for s in sp]
    new_a_k_sample, new_a_v_sample, new_b_k_sample, new_b_v_sample, new_b_logf_sample, new_c_v_sample = [jnp.stack(s, 0) for s in ss]
    return (hp, hs, new_a_k_prompt, new_a_v_prompt, new_b_k_prompt, new_b_v_prompt, new_b_logf_prompt,
            new_a_k_sample, new_a_v_sample, new_b_k_sample, new_b_v_sample, new_b_logf_sample, new_c_v_sample)


_drawn_inputs = setup_inputs


def setup_inputs(seed=0):
    import zlib

    import numpy as np

    out = dict(_drawn_inputs(seed))
    spreads = {}
    factors = {'cache_b_logf': 46.388,
     'norm_g': 5.156,
     'b_gate': 8.0,
     'a_rel_bias': 3.011,
     'c_vnorm_g': 22.884,
     'cache_b_v': 3.444,
     'b_forget': 4.128}
    for name, (base, spread) in spreads.items():
        noise = np.random.default_rng([zlib.crc32(name.encode()), seed]).standard_normal(out[name].shape)
        drawn = base * np.exp(spread * noise) if base else spread * noise
        out[name] = jnp.asarray(drawn.astype(out[name].dtype))
    for name, factor in factors.items():
        out[name] = (out[name] * factor).astype(out[name].dtype)
    return out
```

```python
import numpy as np
import concourse.bass as bass
from concourse import mybir

F32 = mybir.dt.float32
F32R = mybir.dt.float32r
ACT = mybir.ActivationFunctionType
ALU = mybir.AluOpType
AXX = mybir.AxisListType.X

P = 128
D_MODEL = 1024
SEQ = 512
DEC = 64
TOK = SEQ + DEC
HALF = TOK // 2
DEPTH = 2
PAST = 1024
A_WIN = 512
HD = 64
A_HEADS, B_HEADS = 4, 8
CHUNK = 64
REL_MAX = 128
C_GROUPS = 4
D_FF = 2752
KD = D_MODEL // P
KF = -(-D_FF // P)
KF2 = KF // 2
N_MOD = 9
N_ADA = N_MOD * KD
NT = 5
EPS = 1e-6
NEG = -1e30

QA, KA, VA, QB, KB, VB, UC, VC, FB = 0, 2, 4, 6, 10, 14, 18, 20, 22
N_PROJ = 23
A_PAIRS, B_PAIRS = A_HEADS // 2, B_HEADS // 2
UNITS = 10
STRIP = 640
NCONST = 7
IDENT, ONES, NONES, TRI_LE, NTRI_LE, TRI_GT, CAUSAL = range(NCONST)

F1, F2, WIN, GATE, OUTP = KF, KD, 11, 3 * KD, KD // 2
PHASES = [("f1a", F1, F1), ("f2a", F2, F2), ("win", WIN, WIN), ("fb", 1, 0), ("gate", GATE, GATE),
          ("out", OUTP, OUTP), ("f1b", F1, F1), ("f2b", F2, F2)]
GROUPS = {"f1a": (KF, KF), "f2a": (4, 4), "win": (11, 11), "fb": (1, 0), "gate": (24, 24), "out": (4, 4),
          "f1b": (KF, KF), "f2b": (4, 4)}
ADA_PAIRS = N_ADA // 2


def running(counts):
    at, base = [0, 0], {}
    for name, a, b in counts:
        base[name] = tuple(at)
        at[0] += a
        at[1] += b
    return base, tuple(at)


SPLIT_AT, SPLIT_N = running(PHASES)
GROUP_AT, GROUP_N = running([(n, *GROUPS[n]) for n, _, _ in PHASES])
RAW_AT, RAW_N = running([("ada", ADA_PAIRS, ADA_PAIRS)] + PHASES[:4] + [("spatial", 0, 1)] + PHASES[4:])
WIDTH = {"f1a": KD * P, "f2a": KF2 * P, "win": KD * P, "fb": KD * P, "out": KD * P, "f1b": KD * P,
         "f2b": KF2 * P}


class Signal:

    def __init__(self, nc, name, per_layer, slots=0, step=1):
        self.sem = nc.alloc_semaphore(name)
        self.per_layer, self.slots, self.step = per_layer, slots, step

    def done(self, l, n):
        return (l * self.per_layer + n + 1) * self.step + self.slots

    def free(self, l, n):
        return l * self.per_layer + n + 1


def build_program(nc, ins, outs):
    arena = [(nc.sbuf_base + 31) // 32 * 32]

    def sb(name, shape, dt=F32, at=None):
        n = int(np.prod(shape[1:])) * 4
        if at is None:
            at = arena[0]
            arena[0] += (n + 31) // 32 * 32
        assert at + n <= nc.sbuf_usable_end, (name, at + n, nc.sbuf_usable_end)
        return nc.alloc_sbuf_tensor_at(name, shape, dt, offset=at), at

    h, _ = sb("h", [P, KD, TOK])
    x_hi, x_at = sb("x_hi", [P, KD, TOK], F32R)
    x_lo, _ = sb("x_lo", [P, KD, TOK], F32R)
    y, _ = sb("y", [P, KD, TOK], at=x_at)
    raw, _ = sb("w_raw", [P, 2, KF2 * P])
    w_hi, _ = sb("w_hi", [P, 2, KF2 * P], F32R)
    w_lo, _ = sb("w_lo", [P, 2, KF2 * P], F32R)
    const, _ = sb("const", [P, NCONST, P])
    cond, _ = sb("cond", [P, KD, 2])
    cond_s, _ = sb("cond_silu", [P, KD, 2])
    eps_t, _ = sb("eps", [P, 1])
    mods, _ = sb("mods", [P, N_MOD, KD, 2])
    b_ada, _ = sb("b_ada", [P, N_MOD, KD])
    norm_g, _ = sb("norm_g", [P, 6, KD])
    pre_scale, _ = sb("pre_scale", [P, 3, KD, 2])
    post_gate, _ = sb("post_gate", [P, 3, KD, 2])
    b_gate, _ = sb("b_gate", [P, 3, KD])
    b_forget, _ = sb("b_forget", [P, B_HEADS])
    c_gain, _ = sb("c_gain", [P, 256])
    c_bias, _ = sb("c_bias", [P, 2, P])
    cache_f, _ = sb("cache_f", [P, 8, B_HEADS])
    later_f, _ = sb("later_f", [P, 8, B_HEADS])
    earlier_f, _ = sb("earlier_f", [P, 4, B_HEADS])
    logf, _ = sb("logf", [P, NT, B_HEADS])
    fx, _ = sb("fx", [P, 6, NT, B_HEADS])
    f_query, _ = sb("f_query", [P, NT, B_HEADS])
    c_stat, _ = sb("c_stat", [P, 3, NT])
    row, _ = sb("row", [P, 4, 2])
    tmp_at = arena[0]
    sil, _ = sb("sil", [P, TOK])
    hid, _ = sb("hid", [P, TOK])
    sq, _ = sb("sq", [P, 2, TOK])
    acc, _ = sb("acc", [P, TOK])
    msum, _ = sb("msum", [P, TOK], at=tmp_at + 4 * TOK)
    mtmp, _ = sb("mtmp", [P, TOK], at=tmp_at + 8 * TOK)
    strip, _ = sb("strip", [P, 2, STRIP], at=tmp_at)
    big = arena[0]
    hid_hi, _ = sb("hid_hi", [P, KF, TOK], F32R, at=big)
    hid_lo, e = sb("hid_lo", [P, KF, TOK], F32R, at=big + KF * TOK * 4)
    rms, _ = sb("rms", [P, 4, TOK], at=big)
    nt, _ = sb("norm_t", [P, 2, TOK], at=big + 16 * TOK)
    nx, _ = sb("norm_x", [P, 2, TOK], at=big + 24 * TOK)
    proj, _ = sb("proj", [P, N_PROJ, TOK], at=big)
    m_hi, _ = sb("m_hi", [P, KD, TOK], F32R, at=big)
    m_lo, _ = sb("m_lo", [P, KD, TOK], F32R, at=big + KD * TOK * 4)
    att = big + N_PROJ * TOK * 4
    o_hi, _ = sb("o_hi", [P, KD, TOK], F32R, at=att)
    o_lo, _ = sb("o_lo", [P, KD, TOK], F32R, at=att + KD * TOK * 4)
    SC = PAST + DEC
    prob, _ = sb("prob", [P, 2, SC], at=att)
    a = att + 2 * SC * 4
    prob_t, _ = sb("prob_t", [P, 2, 9, P], at=a)
    a += 2 * 9 * P * 4
    decay_s, _ = sb("decay_s", [P, 2, SC], at=a)
    f_rows, _ = sb("f_rows", [B_HEADS, SEQ + SC], at=a)
    a += 2 * SC * 4
    decay_p, _ = sb("decay_p", [P, 2, SEQ], at=a)
    a += 2 * SEQ * 4
    cache_k, _ = sb("cache_k", [P, PAST], at=a)
    v_tok_c, _ = sb("v_tok_c", [P, NT, 256], at=a)
    a += PAST * 4
    cache_v, _ = sb("cache_v", [P, 8, P], at=a)
    a += 8 * P * 4
    q_st, _ = sb("q_stage", [P, TOK], at=a)
    w_mix, _ = sb("w_mix", [P, C_GROUPS, P], at=a)
    a += TOK * 4
    k_st, _ = sb("k_stage", [P, TOK], at=a)
    c_mix, _ = sb("c_mix", [P, TOK], at=a)
    a += TOK * 4
    v_st, _ = sb("v_stage", [P, TOK], at=a)
    a += TOK * 4
    v_tok, _ = sb("v_tok", [P, NT, P], at=a)

    ps = nc.alloc_psum_tensor("ps", [P, 8, 512], F32)
    pair = [ps[:, 0:2, 0:HALF], ps[:, 2:4, 0:HALF]]
    stat = ps[:, 4:6, 0:HALF]
    flat = ps[:, :, :].rearrange("p b n -> p (b n)")
    score = [flat[:, 0:3 * 512], flat[:, 4 * 512:7 * 512]]
    turned = ps[:, 3, :]
    att_out = ps[:, 7, :]
    scratch = nc.dram_tensor("f_scratch", (DEPTH, B_HEADS, SEQ + SC), F32, kind="Internal").ap()

    def two(ap):
        return ap.rearrange("p (b n) -> p b n", b=2)

    raw_full = [Signal(nc, f"raw_full{s}", RAW_N[s], step=16) for s in (0, 1)]
    raw_read = [Signal(nc, f"raw_read{s}", ADA_PAIRS + s, 1) for s in (0, 1)]
    hi_ready = [Signal(nc, f"hi_ready{s}", SPLIT_N[s]) for s in (0, 1)]
    lo_ready = [Signal(nc, f"lo_ready{s}", SPLIT_N[s], 1) for s in (0, 1)]
    chunk_done = [Signal(nc, f"chunk_done{s}", SPLIT_N[s], 1) for s in (0, 1)]
    acc_free = [Signal(nc, f"acc_free{s}", GROUP_N[s], 1) for s in (0, 1)]
    prod_hi = Signal(nc, "prod_hi", 2 * KF + KD)
    prod_lo = Signal(nc, "prod_lo", 2 * KF + KD, 1)
    sq_ready = Signal(nc, "sq_ready", 6 * KD)
    sq_added = Signal(nc, "sq_added", 6 * KD, 2)
    stat_ready = Signal(nc, "stat_ready", 6)
    ms_ready = Signal(nc, "ms_ready", 6)
    est_ready = Signal(nc, "est_ready", 6)
    t_ready = Signal(nc, "t_ready", 3 * KD)
    nx_ready = Signal(nc, "nx_ready", 3 * KD)
    x_ready = Signal(nc, "x_ready", 3 * KD, 2)
    h_ready = Signal(nc, "h_ready", 3 * KD)
    small_in = Signal(nc, "small_in", 9, step=16)
    small_used = Signal(nc, "small_used", 1, 1)
    start_in = Signal(nc, "start_in", 3, step=16)
    cond_ready = Signal(nc, "cond_ready", 1)
    eps_ready = Signal(nc, "eps_ready", 1)
    ada_ready = Signal(nc, "ada_ready", 1)
    mods_ready = Signal(nc, "mods_ready", 1)
    proj_ready = Signal(nc, "proj_ready", N_PROJ)
    f_turned = Signal(nc, "f_turned", 1)
    f_neg = Signal(nc, "f_neg", 1)
    f_exp = Signal(nc, "f_exp", 1)
    f_sums_in = Signal(nc, "f_sums_in", 1)
    f_sums = Signal(nc, "f_sums", 1)
    f_rows_ready = Signal(nc, "f_rows_ready", 1)
    vc_turned = Signal(nc, "vc_turned", 1)
    vc_copied = Signal(nc, "vc_copied", 1)
    vc_ready = Signal(nc, "vc_ready", 1)
    mixed = Signal(nc, "mixed", 2)
    mixer_begun = Signal(nc, "mixer_begun", 1)
    oc_ready = Signal(nc, "oc_ready", 1)
    NP = A_PAIRS + B_PAIRS
    NU = NP * UNITS
    strip_in = Signal(nc, "strip_in", A_PAIRS, step=16)
    ck_in = Signal(nc, "ck_in", NP, step=16)
    cv_in = Signal(nc, "cv_in", NP, step=16)
    decay_s_in = Signal(nc, "decay_s_in", B_PAIRS, step=16)
    decay_p_in = Signal(nc, "decay_p_in", B_PAIRS, step=16)
    rows_out = Signal(nc, "rows_out", 1, step=16)
    k_staged = Signal(nc, "k_staged", NP)
    q_staged = Signal(nc, "q_staged", NP)
    v_turned = Signal(nc, "v_turned", NP)
    v_staged = Signal(nc, "v_staged", NP)
    v_ready = Signal(nc, "v_ready", NP)
    scores_ready = Signal(nc, "scores_ready", NU)
    scores_taken = Signal(nc, "scores_taken", NU, 2)
    shift_ready = Signal(nc, "shift_ready", NU)
    exp_ready = Signal(nc, "exp_ready", NU)
    inv_ready = Signal(nc, "inv_ready", NU)
    prob_ready = Signal(nc, "prob_ready", NU)
    prob_turned = Signal(nc, "prob_turned", NU, 2)
    prob_t_ready = Signal(nc, "prob_t_ready", NU, 1)
    o_summed = Signal(nc, "o_summed", NU, 2)
    o_taken = Signal(nc, "o_taken", NU, 1)
    o_split_hi = Signal(nc, "o_split_hi", KD)
    o_ready = Signal(nc, "o_ready", KD)
    out_kv = Signal(nc, "out_kv", 4, step=16)
    out_small = Signal(nc, "out_small", 2, step=16)
    out_h = Signal(nc, "out_h", 1, step=16)

    passed = {e: nc.alloc_semaphore(f"passed_{e}") for e in ("sp", "pe", "act", "dve", "pool")}

    def hold(eng, e):
        eng.sem_inc(passed[e], 1)

    def credits(eng, signals):
        for s in signals:
            eng.sem_inc(s.sem, s.slots)

    units = [(0, 4), (1, 4)] + [(hh, i) for hh in (0, 1) for i in range(4)]

    def unit_shape(u, cached):
        hh, i = units[u]
        if i < 4:
            return hh, i, P, P * (i + 1), i + 1
        return hh, i, DEC, cached + DEC, cached // P + 1

    block_ctx = nc.Block()
    block = block_ctx.__enter__()

    @block.sync
    def _(sp):
        sp.dma_start(cond[:, :, :], ins["cond"]).then_inc(start_in.sem, 16)
        sp.dma_start(const[:, :, :], ins["const"]).then_inc(start_in.sem, 16)
        sp.dma_start(h[:, :, :], ins["x"]).then_inc(start_in.sem, 16)

        def load(l, ph, s, i, src, index, width):
            dst = raw[:, s, 0:width]
            src = src[bass.ds(index, 1), :, :].rearrange("a p n -> p (a n)")
            n_split = SPLIT_AT[ph][s] if ph in SPLIT_AT else (SPLIT_AT["gate"][1] if ph == "spatial" else 0)
            split_i = i if ph in SPLIT_AT else 0
            n_raw = i if ph == "ada" else ADA_PAIRS
            if s == 1 and SPLIT_AT.get(ph, (0, 0))[1] >= SPLIT_AT["gate"][1]:
                n_raw = ADA_PAIRS + 1
            sp.wait_ge(lo_ready[s].sem, lo_ready[s].free(l, n_split + split_i))
            hold(sp, "sp")
            sp.wait_ge(raw_read[s].sem, raw_read[s].free(l, n_raw))
            hold(sp, "sp")
            sp.dma_start(dst, src).then_inc(raw_full[s].sem, 16)

        def ffn_loads(l, ab, which):
            with sp.Fori(0, F1) as i:
                for s in (0, 1):
                    load(l, "f1" + ab, s, i, ins["f1"], (l * 2 + which) * 2 * F1 + i * 2 + s, KD * P)
            with sp.Fori(0, F2) as i:
                for s in (0, 1):
                    load(l, "f2" + ab, s, i, ins["f2"], (l * 2 + which) * 2 * F2 + i * 2 + s, KF2 * P)

        with sp.Fori(0, DEPTH) as l:
            sp.wait_ge(small_used.sem, small_used.free(l, 0))
            hold(sp, "sp")
            for dst, name in ((b_ada, "b_ada"), (norm_g, "norm_g"), (b_gate, "b_gate"), (b_forget, "b_forget"),
                              (c_gain, "c_gain"), (c_bias, "c_bias"), (cache_f, "cache_f")):
                src = ins[name][bass.ds(l, 1), :, :].rearrange("a p n -> p (a n)")
                flat_dst = dst[:, :] if len(dst.shape) == 2 else dst[:, :, :].rearrange("p a b -> p (a b)")
                sp.dma_start(flat_dst, src).then_inc(small_in.sem, 16)
            for name, out in (("cache_a_k", "roll_k"), ("cache_a_v", "roll_v")):
                sp.dma_start(outs[out][bass.ds(l, 1), :, :],
                             ins[name][bass.ds(l, 1), DEC:A_WIN, :]).then_inc(small_in.sem, 16)
            with sp.Fori(0, ADA_PAIRS) as i:
                for s in (0, 1):
                    load(l, "ada", s, i, ins["ada"], l * N_ADA + i * 2 + s, KD * P)
            ffn_loads(l, "a", 0)
            with sp.Fori(0, WIN) as i:
                for s in (0, 1):
                    load(l, "win", s, i, ins["win"], l * N_PROJ + i * 2 + s, KD * P)
            load(l, "fb", 0, 0, ins["win"], l * N_PROJ + FB, KD * P)
            load(l, "spatial", 1, 0, ins["c_spatial"], l, C_GROUPS * P)

            sp.wait_ge(oc_ready.sem, oc_ready.done(l, 0))
            hold(sp, "sp")
            with sp.Fori(0, A_PAIRS) as a:
                sp.wait_ge(o_summed.sem, l * NU + a * UNITS + 2)
                hold(sp, "sp")
                sp.dma_start(strip[:, :, :], ins["strip"][bass.ds(l * A_PAIRS + a, 1), :, :, :]
                             .rearrange("a p c n -> p (a c) n")).then_inc(strip_in.sem, 16)
                sp.dma_start(cache_k[:, 0:A_WIN], ins["ck_a"][bass.ds(l * A_PAIRS + a, 1), :, :]
                             .rearrange("a p n -> p (a n)")).then_inc(ck_in.sem, 16)
                sp.dma_start(cache_v[:, 0:A_WIN // P, :].rearrange("p t n -> p (t n)"),
                             ins["cv_a"][bass.ds(l * A_PAIRS + a, 1), :, :]
                             .rearrange("a p n -> p (a n)")).then_inc(cv_in.sem, 16)
            sp.wait_ge(rows_out.sem, rows_out.done(l, 0))
            hold(sp, "sp")
            with sp.Fori(0, B_PAIRS) as b:
                sp.wait_ge(o_summed.sem, l * NU + A_PAIRS * UNITS + b * UNITS + 2)
                hold(sp, "sp")
                sp.dma_start(cache_k[:, :], ins["ck_b"][bass.ds(l * B_PAIRS + b, 1), :, :]
                             .rearrange("a p n -> p (a n)")).then_inc(ck_in.sem, 16)
                sp.dma_start(cache_v[:, :, :].rearrange("p t n -> p (t n)"),
                             ins["cv_b"][bass.ds(l * B_PAIRS + b, 1), :, :]
                             .rearrange("a p n -> p (a n)")).then_inc(cv_in.sem, 16)
                rows = scratch[bass.ds(l, 1), bass.ds(b * 2, 2), :].rearrange("a h n -> (a h) n")
                sp.dma_start(decay_s[:, :, :], rows[:, SEQ:SEQ + SC].partition_broadcast(P)
                             ).then_inc(decay_s_in.sem, 16)
                sp.dma_start(decay_p[:, :, :], rows[:, 0:SEQ].partition_broadcast(P)
                             ).then_inc(decay_p_in.sem, 16)
            with sp.Fori(0, KD) as m:
                for br, k in enumerate((2, 4, 2)):
                    load(l, "gate", 0, m * 3 + br, ins["gate"], (l * KD + m) * 3 + br, KD * P)
                    load(l, "gate", 1, m * 3 + br, ins["br" + "abc"[br]], l * KD + m, k * P)
            with sp.Fori(0, OUTP) as i:
                for s in (0, 1):
                    load(l, "out", s, i, ins["wout"], l * KD + i * 2 + s, KD * P)
            ffn_loads(l, "b", 1)

    @block.tensor
    def _(pe):
        credits(pe, chunk_done + [raw_read[0], raw_read[1], prob_turned, o_summed])
        mm = nc.tensor.matmul

        def split_tile(out, s, t, hi, lo, first, last):
            wh, wl = w_hi[:, s, t * P:(t + 1) * P], w_lo[:, s, t * P:(t + 1) * P]
            for n, (w, xx) in enumerate(((wh, hi), (wh, lo), (wl, hi))):
                for b in (0, 1):
                    r = mm(out[:, b, :], w, xx[:, b * HALF:(b + 1) * HALF],
                           start=first and n == 0, stop=last and n == 2)
            return r

        def group_of_one(l, ph, p, i, hi, lo, tiles=KD, gate=None, done=True):
            pe.wait_ge(lo_ready[p].sem, lo_ready[p].done(l, SPLIT_AT[ph][p] + i))
            pe.wait_ge(acc_free[p].sem, acc_free[p].free(l, GROUP_AT[ph][p] + i))
            for t in range(tiles):
                if gate is not None:
                    gate(t)
                r = split_tile(pair[p], p, t, hi[:, t, :], lo[:, t, :], t == 0, t == tiles - 1)
            r.then_inc(chunk_done[p].sem, 1)

        def column_sums(l, n):
            pe.wait_ge(sq_added.sem, sq_added.done(l, n * KD + KD - 1))
            for b in (0, 1):
                r = mm(stat[:, b, :], const[:, ONES, :], acc[:, b * HALF:(b + 1) * HALF], start=True, stop=True)
            r.then_inc(stat_ready.sem, 1)

        def ffn(l, ab, n):
            column_sums(l, 2 * n)

            def x_tile(t):
                pe.wait_ge(x_ready.sem, x_ready.done(l, n * KD + t))
            with pe.Fori(0, F1) as i:
                for p in (0, 1):
                    group_of_one(l, "f1" + ab, p, i, x_hi, x_lo, gate=x_tile if p == 0 else None)
            with pe.Fori(0, F2 // 2) as i:
                for p in (0, 1):
                    pe.wait_ge(acc_free[p].sem, acc_free[p].free(l, GROUP_AT["f2" + ab][p] + i))
                    for s in (0, 1):
                        pe.wait_ge(lo_ready[s].sem, lo_ready[s].done(l, SPLIT_AT["f2" + ab][s] + 2 * i + p))
                        for t in range(KF2):
                            k = s * KF2 + t
                            if p == 0:
                                pe.wait_ge(prod_lo.sem, prod_lo.done(l, (0 if ab == "a" else KF + KD) + k))
                            r = split_tile(pair[p], s, t, hid_hi[:, k, :], hid_lo[:, k, :], k == 0, k == KF - 1)
                        r.then_inc(chunk_done[s].sem, 1)
            column_sums(l, 2 * n + 1)

        def projection(l):
            column_sums(l, 2)

            def x_tile(t):
                pe.wait_ge(x_ready.sem, x_ready.done(l, KD + t))
            with pe.Fori(0, WIN) as i:
                for p in (0, 1):
                    group_of_one(l, "win", p, i, x_hi, x_lo, gate=x_tile if p == 0 else None)
            group_of_one(l, "fb", 0, 0, x_hi, x_lo)

        def forget_and_spatial(l):
            pe.wait_ge(proj_ready.sem, proj_ready.done(l, N_PROJ - 1))
            hold(pe, "pe")
            for t in range(NT):
                m = P if t < 4 else DEC
                cols = slice(t * P, t * P + m)
                r = nc.tensor.transpose(ps[0:m, 4, t * 8:t * 8 + 8], proj[0:8, FB, cols], const[0:8, IDENT, 0:8])
            r.then_inc(f_turned.sem, 1)
            for t in range(NT):
                m = P if t < 4 else DEC
                cols = slice(t * P, t * P + m)
                for c in (0, 1):
                    r = nc.tensor.transpose(ps[0:m, 5 + t // 2, (t % 2) * 256 + c * P:(t % 2) * 256 + (c + 1) * P],
                                            proj[:, VC + c, cols], const[:, IDENT, :])
            r.then_inc(vc_turned.sem, 1)
            pe.wait_ge(f_sums_in.sem, f_sums_in.done(l, 0))
            for t in range(4):
                o = ps[:, 4, 64 + t * 8:72 + t * 8]
                mm(o, const[:, TRI_LE, :], logf[:, t, :], start=True, stop=t == 0)
                if t:
                    mm(o, const[:, ONES, :], earlier_f[:, t, :], start=False, stop=True)
            mm(ps[0:DEC, 4, 96:104], const[0:DEC, TRI_LE, 0:DEC], logf[0:DEC, 4, :], start=True, stop=True)
            for t in range(4):
                o = ps[0:B_HEADS, 0, t * P:(t + 1) * P]
                mm(o, logf[:, t, :], const[:, NTRI_LE, :], start=True, stop=t == 0)
                if t:
                    mm(o, earlier_f[:, t, :], const[:, NONES, :], start=False, stop=True)
            for t in range(8):
                o = ps[0:B_HEADS, 1 + t // 4, (t % 4) * P:(t % 4 + 1) * P]
                mm(o, cache_f[:, t, :], const[:, TRI_GT, :], start=True, stop=t == 7)
                if t < 7:
                    mm(o, later_f[:, t, :], const[:, ONES, :], start=False, stop=True)
            mm(ps[0:B_HEADS, 3, 0:DEC], logf[0:DEC, 4, :], const[0:DEC, NTRI_LE, 0:DEC], start=True,
               stop=True).then_inc(f_sums.sem, 1)
            pe.wait_ge(vc_ready.sem, vc_ready.done(l, 0))
            pe.wait_ge(f_rows_ready.sem, f_rows_ready.done(l, 0))
            for T in (0, 1):
                for hh in (0, 1):
                    g = 2 * T + hh
                    for n in range(4):
                        mm(ps[HD * hh:HD * hh + HD, 2 * T, n * P:(n + 1) * P], v_tok_c[:, n, g * HD:(g + 1) * HD],
                           w_mix[:, g, :], start=True, stop=True)
                    r = mm(ps[HD * hh:HD * hh + HD, 2 * T + 1, 0:DEC], v_tok_c[0:DEC, 4, g * HD:(g + 1) * HD],
                           w_mix[0:DEC, g, 0:DEC], start=True, stop=True)
                r.then_inc(mixed.sem, 1)

        def pair_units(l, pr, cached):
            base = pr * UNITS

            def scores(u):
                hh, i, m, nk, _ = unit_shape(u, cached)
                n, rows = base + u, slice(hh * HD, hh * HD + HD)
                pe.wait_ge(scores_taken.sem, scores_taken.free(l, n))
                q = q_st[rows, i * P:i * P + m]
                out = score[u % 2]
                if i < 4:
                    r = mm(out[:, 0:nk], q, k_st[rows, 0:nk], start=True, stop=True)
                else:
                    if u == 0:
                        pe.wait_ge(ck_in.sem, ck_in.done(l, pr))
                    hold(pe, "pe")
                    for c in range(0, cached, 512):
                        mm(out[0:m, c:c + 512], q, cache_k[rows, c:c + 512], start=True, stop=True)
                    r = mm(out[0:m, cached:nk], q, k_st[rows, SEQ:TOK], start=True, stop=True)
                r.then_inc(scores_ready.sem, 1)

            def turn(u):
                hh, i, m, nk, nb = unit_shape(u, cached)
                n = base + u
                pe.wait_ge(prob_ready.sem, prob_ready.done(l, n))
                pe.wait_ge(prob_t_ready.sem, prob_t_ready.free(l, n))
                if i == 4:
                    hold(pe, "pe")
                for b in range(nb):
                    w = min(P, nk - b * P)
                    out = turned[0:w, b * m:(b + 1) * m] if b < 8 else score[u % 2][0:w, nk:nk + m]
                    r = nc.tensor.transpose(out, prob[0:m, u % 2, b * P:b * P + w], const[0:m, IDENT, 0:m])
                r.then_inc(prob_turned.sem, 1)

            def weigh(u):
                hh, i, m, nk, nb = unit_shape(u, cached)
                n = base + u
                pe.wait_ge(prob_t_ready.sem, prob_t_ready.done(l, n))
                pe.wait_ge(o_taken.sem, o_taken.free(l, n))
                if u == 0:
                    pe.wait_ge(cv_in.sem, cv_in.done(l, pr))
                    pe.wait_ge(v_ready.sem, v_ready.done(l, pr))
                if i == 4:
                    hold(pe, "pe")
                for b in range(nb):
                    w = min(P, nk - b * P)
                    cols = slice(hh * HD, hh * HD + HD)
                    if i < 4:
                        v = v_tok[:, b, cols]
                    else:
                        v = cache_v[:, b, cols] if b < nb - 1 else v_tok[0:w, 4, cols]
                    r = mm(att_out[hh * HD:hh * HD + HD, 0:m], v, prob_t[0:w, u % 2, b, 0:m],
                           start=b == 0, stop=b == nb - 1)
                r.then_inc(o_summed.sem, 1)

            pe.wait_ge(v_staged.sem, v_staged.done(l, pr))
            pe.wait_ge(o_taken.sem, o_taken.free(l, base))
            pe.wait_ge(prob_t_ready.sem, prob_t_ready.free(l, base))
            for t in range(NT):
                m = P if t < 4 else DEC
                out = turned[:, t * P:(t + 1) * P] if t < 4 else att_out[0:m, 0:P]
                r = nc.tensor.transpose(out, v_st[:, t * P:t * P + m], const[:, IDENT, :])
            r.then_inc(v_turned.sem, 1)
            pe.wait_ge(k_staged.sem, k_staged.done(l, pr))
            pe.wait_ge(v_ready.sem, v_ready.done(l, pr))
            scores(0)
            for u in range(UNITS):
                if u + 1 < UNITS:
                    scores(u + 1)
                turn(u)
                weigh(u)

        pe.wait_ge(start_in.sem, start_in.done(0, 2))
        pe.wait_ge(cond_ready.sem, cond_ready.done(0, 0))
        with pe.Fori(0, DEPTH) as l:
            with pe.Fori(0, ADA_PAIRS) as i:
                for s in (0, 1):
                    pe.wait_ge(raw_full[s].sem, raw_full[s].done(l, i))
                    for k in range(KD):
                        r = mm(ps[:, 6 + s, bass.ds(i * 2, 2)], raw[:, s, k * P:(k + 1) * P], cond_s[:, k, :],
                               start=k == 0, stop=k == KD - 1)
                    r.then_inc(raw_read[s].sem, 1)
            ffn(l, "a", 0)
            projection(l)
            forget_and_spatial(l)
            pe.wait_ge(oc_ready.sem, oc_ready.done(l, 0))
            hold(pe, "pe")
            with pe.Fori(0, A_PAIRS) as a:
                pair_units(l, a, A_WIN)
            with pe.Fori(0, B_PAIRS) as b:
                pair_units(l, b + A_PAIRS, PAST)
            pe.wait_ge(o_ready.sem, o_ready.done(l, KD - 1))
            hold(pe, "pe")
            with pe.Fori(0, KD) as m:
                for br, (t0, tiles) in enumerate(((0, 2), (2, 4), (6, 2))):
                    group_of_one(l, "gate", 0, m * 3 + br, x_hi, x_lo)
                    group_of_one(l, "gate", 1, m * 3 + br, o_hi[:, t0:t0 + tiles, :], o_lo[:, t0:t0 + tiles, :],
                                 tiles=tiles)

            def m_tile(t):
                pe.wait_ge(prod_lo.sem, prod_lo.done(l, KF + t))
            with pe.Fori(0, OUTP) as i:
                for p in (0, 1):
                    group_of_one(l, "out", p, i, m_hi, m_lo, gate=m_tile if p == 0 else None)
            column_sums(l, 3)
            ffn(l, "b", 2)

    @block.scalar
    def _(act):
        credits(act, [prob_t_ready, o_taken, acc_free[0]])
        A = nc.scalar.activation

        def split_hi(l, ph, s, i, width=None):
            w = width or WIDTH[ph]
            act.wait_ge(raw_full[s].sem, raw_full[s].done(l, RAW_AT[ph][s] + i))
            act.wait_ge(chunk_done[s].sem, chunk_done[s].free(l, SPLIT_AT[ph][s] + i))
            nc.scalar.copy(w_hi[:, s, 0:w], raw[:, s, 0:w]).then_inc(hi_ready[s].sem, 1)

        def pairs(n, l, body, following):
            with act.Fori(0, n - 1) as i:
                body(i, None)
            body(n - 1, following)

        def ffn_up(l, ab, following):
            ph = "f1" + ab
            act.preload_act_table(ACT.Silu)

            def body(i, nxt):
                split_hi(l, ph, 1, i)
                act.wait_ge(chunk_done[0].sem, chunk_done[0].done(l, SPLIT_AT[ph][0] + i))
                act.wait_ge(acc_free[1].sem, acc_free[1].free(l, GROUP_AT[ph][1] + i))
                A(two(sil[:, :]), pair[0], ACT.Silu).then_inc(acc_free[0].sem, 1)
                nxt() if nxt else split_hi(l, ph, 0, i + 1)
                act.wait_ge(acc_free[1].sem, acc_free[1].done(l, GROUP_AT[ph][1] + i))
                nc.scalar.copy(hid_hi[:, bass.ds(i, 1), :].rearrange("p a n -> p (a n)"), hid[:, :]
                               ).then_inc(prod_hi.sem, 1)
            pairs(F1, l, body, following)

        def keep_and_square(l, ph, n, p, i, m, k0, s):
            act.wait_ge(chunk_done[s].sem, chunk_done[s].done(l, SPLIT_AT[ph][s] + i))
            act.wait_ge(sq_added.sem, sq_added.free(l, n * KD + k0))
            A(two(sq[:, p, :]), pair[p], ACT.Square).then_inc(sq_ready.sem, 1)
            nc.scalar.copy(two(y[:, bass.ds(m, 1), :].rearrange("p a n -> p (a n)")), pair[p]
                           ).then_inc(acc_free[p].sem, 1)

        def ffn_down(l, ab, n, following):
            ph = "f2" + ab

            def body(i, nxt):
                for p in (0, 1):
                    split_hi(l, ph, 1, 2 * i + p)
                    if p == 0 or not nxt:
                        split_hi(l, ph, 0, 2 * i + p + 1)
                    else:
                        nxt()
                    keep_and_square(l, ph, n, p, 2 * i + p, 2 * i + p, 2 * i + p, 1)
            pairs(F2 // 2, l, body, following)

        def square_h(l, n, wait):
            for k in range(KD):
                wait(k)
                act.wait_ge(sq_added.sem, sq_added.free(l, n * KD + k))
                A(sq[:, k % 2, :], h[:, k, :], ACT.Square).then_inc(sq_ready.sem, 1)

        def estimate(l, n):
            act.wait_ge(ms_ready.sem, ms_ready.done(l, n))
            A(rms[:, 1, :], rms[:, 0, :], ACT.Ln)
            act.drain()
            A(rms[:, 1, :], rms[:, 1, :], ACT.Exp, scale=-0.5).then_inc(est_ready.sem, 1)

        def make_x(l, n):
            for k in range(KD):
                act.wait_ge(t_ready.sem, t_ready.done(l, n * KD + k))
                act.wait_ge(x_ready.sem, x_ready.free(l, n * KD + k))
                for g, cols in ((0, slice(0, SEQ)), (1, slice(SEQ, TOK))):
                    A(nx[:, k % 2, cols], nt[:, k % 2, cols], ACT.Identity,
                      bias=mods[:, 3 * n, k, g:g + 1], scale=pre_scale[:, n, k, g:g + 1])
                act.drain()
                nc.scalar.copy(x_hi[:, k, :], nx[:, k % 2, :]).then_inc(nx_ready.sem, 1)

        def h_tiles(l, n):
            return lambda k: act.wait_ge(h_ready.sem, h_ready.done(l, n * KD + k))

        def pair_units(l, pr, tile, first_q, first_k, first_v, cached, lag):
            base = pr * UNITS

            def one(t):
                return proj[:, bass.ds(t, 1), :].rearrange("p a n -> p (a n)")

            act.wait_ge(o_summed.sem, o_summed.free(l, base))
            nc.scalar.copy(v_st[:, :], one(first_v + tile)).then_inc(v_staged.sem, 1)
            nc.scalar.copy(k_st[:, :], one(first_k + tile))
            nc.scalar.mul(q_st[:, :], one(first_q + tile), HD ** -0.5).then_inc(k_staged.sem, 1)
            act.wait_ge(v_turned.sem, v_turned.done(l, pr))
            nc.scalar.copy(v_tok[:, 0:4, :].rearrange("p t n -> p (t n)"), turned)
            nc.scalar.copy(v_tok[0:DEC, 4, :], att_out[0:DEC, 0:P]).then_inc(v_ready.sem, 1)

            def expo(u):
                hh, i, m, nk, nb = unit_shape(u, cached)
                n = base + u
                act.wait_ge(shift_ready.sem, shift_ready.done(l, n))
                A(prob[0:m, u % 2, 0:nk], prob[0:m, u % 2, 0:nk], ACT.Exp, bias=row[0:m, 1, u % 2:u % 2 + 1],
                  accum_out=row[0:m, 2, u % 2:u % 2 + 1]).then_inc(exp_ready.sem, 1)

            def evacuate_turned(u):
                hh, i, m, nk, nb = unit_shape(u, cached)
                n = base + u
                act.wait_ge(prob_turned.sem, prob_turned.done(l, n))
                act.wait_ge(o_summed.sem, o_summed.free(l, n))
                last = nk - (nb - 1) * P
                full = nb if last == P else nb - 1
                r = nc.scalar.copy(prob_t[:, u % 2, 0:full, 0:m],
                                   turned[:, 0:full * m].rearrange("p (b n) -> p b n", b=full))
                if last != P:
                    src = turned[0:last, full * m:full * m + m] if full < 8 else score[u % 2][0:last, nk:nk + m]
                    r = nc.scalar.copy(prob_t[0:last, u % 2, full, 0:m], src)
                r.then_inc(prob_t_ready.sem, 1)

            def take_o(u):
                hh, i, m, nk, nb = unit_shape(u, cached)
                n = base + u
                act.wait_ge(o_summed.sem, o_summed.done(l, n))
                hold(act, "act")
                rows = slice(hh * HD, hh * HD + HD)
                nc.scalar.copy(proj[rows, bass.ds(first_q + tile, 1), i * P:i * P + m]
                               .rearrange("p a n -> p (a n)"), att_out[rows, 0:m]).then_inc(o_taken.sem, 1)

            expo(0)
            for u in range(UNITS):
                if u + 1 < UNITS:
                    expo(u + 1)
                evacuate_turned(u)
                take_o(u)

        act.wait_ge(start_in.sem, start_in.done(0, 2))
        A(cond_s[:, :, :], cond[:, :, :], ACT.Silu).then_inc(cond_ready.sem, 1)
        act.wait_ge(eps_ready.sem, eps_ready.done(0, 0))
        with act.Fori(0, DEPTH) as l:
            def h_complete(k):
                act.wait_ge(h_ready.sem, l * h_ready.per_layer + KD)
            square_h(l, 0, h_complete)
            split_hi(l, "f1a", 0, 0)
            estimate(l, 0)
            make_x(l, 0)
            ffn_up(l, "a", lambda: split_hi(l, "f2a", 0, 0))
            ffn_down(l, "a", 1, lambda: split_hi(l, "win", 0, 0))
            estimate(l, 1)
            square_h(l, 2, lambda k: act.wait_ge(h_ready.sem, h_ready.done(l, k) + KD))
            estimate(l, 2)
            make_x(l, 1)

            def proj_pair(i, nxt):
                split_hi(l, "win", 1, i)
                act.wait_ge(chunk_done[0].sem, chunk_done[0].done(l, SPLIT_AT["win"][0] + i))
                nc.scalar.copy(two(proj[:, bass.ds(i * 2, 1), :].rearrange("p a n -> p (a n)")), pair[0]
                               ).then_inc(acc_free[0].sem, 1)
                nxt() if nxt else split_hi(l, "win", 0, i + 1)
            pairs(WIN, l, proj_pair, lambda: split_hi(l, "fb", 0, 0))
            act.wait_ge(chunk_done[0].sem, chunk_done[0].done(l, SPLIT_AT["fb"][0]))
            nc.scalar.copy(two(proj[:, FB, :]), pair[0]).then_inc(acc_free[0].sem, 1)
            act.wait_ge(f_neg.sem, f_neg.done(l, 0))
            A(fx[:, 2, :, :], fx[:, 1, :, :], ACT.Exp).then_inc(f_exp.sem, 1)
            act.wait_ge(vc_turned.sem, vc_turned.done(l, 0))
            for t in range(NT):
                m = P if t < 4 else DEC
                src = ps[0:m, 5 + t // 2, (t % 2) * 256:(t % 2) * 256 + 256]
                A(v_tok_c[0:m, t, :], src, ACT.Square, accum_out=c_stat[0:m, 0, t:t + 1])
            act.drain()
            for t in range(NT):
                m = P if t < 4 else DEC
                src = ps[0:m, 5 + t // 2, (t % 2) * 256:(t % 2) * 256 + 256]
                nc.scalar.copy(v_tok_c[0:m, t, :], src)
            act.drain()
            A(c_stat[:, 1, :], c_stat[:, 0, :], ACT.Sqrt, scale=1.0 / 256, bias=eps_t[:, 0:1]
              ).then_inc(vc_copied.sem, 1)
            act.wait_ge(f_sums.sem, f_sums.done(l, 0))
            nc.scalar.copy(f_rows[:, 0:SEQ + PAST], flat[0:B_HEADS, 0:SEQ + PAST])
            nc.scalar.copy(f_rows[:, SEQ + PAST:SEQ + SC], ps[0:B_HEADS, 3, 0:DEC])
            nc.scalar.copy(f_query[:, 0:4, :].rearrange("p t h -> p (t h)"), ps[:, 4, 64:96])
            nc.scalar.copy(f_query[0:DEC, 4, :], ps[0:DEC, 4, 96:104]).then_inc(f_rows_ready.sem, 1)

            act.wait_ge(oc_ready.sem, oc_ready.done(l, 0))
            hold(act, "act")
            with act.Fori(0, A_PAIRS) as a:
                pair_units(l, a, a, QA, KA, VA, A_WIN, 0)
            with act.Fori(0, B_PAIRS) as b:
                pair_units(l, b + A_PAIRS, b, QB, KB, VB, PAST, 0)
            split_hi(l, "gate", 0, 0, KD * P)
            act.drain()
            for t, src in enumerate([QA, QA + 1, QB, QB + 1, QB + 2, QB + 3, UC, UC + 1]):
                nc.scalar.copy(o_hi[:, t, :], proj[:, src, :]).then_inc(o_split_hi.sem, 1)

            def gate_tile(m, nxt):
                for br, k in enumerate((2, 4, 2)):
                    n = m * 3 + br
                    split_hi(l, "gate", 1, n, k * P)
                    act.wait_ge(chunk_done[0].sem, chunk_done[0].done(l, SPLIT_AT["gate"][0] + n))
                    act.wait_ge(acc_free[1].sem, acc_free[1].free(l, GROUP_AT["gate"][1] + n))
                    A(two(sil[:, :]), pair[0], ACT.Sigmoid,
                      bias=b_gate[:, br, bass.ds(m, 1)]).then_inc(acc_free[0].sem, 1)
                    if br < 2 or not nxt:
                        split_hi(l, "gate", 0, n + 1, KD * P)
                    else:
                        nxt()
                act.wait_ge(acc_free[1].sem, acc_free[1].done(l, GROUP_AT["gate"][1] + m * 3 + 2) )
                act.wait_ge(mixer_begun.sem, l * KD + m + 1)
                nc.scalar.copy(m_hi[:, bass.ds(m, 1), :].rearrange("p a n -> p (a n)"), msum[:, :]
                               ).then_inc(prod_hi.sem, 1)
            act.wait_ge(out_kv.sem, out_kv.done(l, 3))
            act.wait_ge(o_ready.sem, o_ready.done(l, KD - 1))
            hold(act, "act")
            act.preload_act_table(ACT.Sigmoid)
            pairs(KD, l, gate_tile, lambda: split_hi(l, "out", 0, 0))

            def out_pair(i, nxt):
                split_hi(l, "out", 1, i)
                keep_and_square(l, "out", 3, 0, i, 2 * i, 2 * i, 0)
                nxt() if nxt else split_hi(l, "out", 0, i + 1)
                keep_and_square(l, "out", 3, 1, i, 2 * i + 1, 2 * i + 1, 1)
            pairs(OUTP, l, out_pair, lambda: split_hi(l, "f1b", 0, 0))
            estimate(l, 3)
            square_h(l, 4, lambda k: act.wait_ge(h_ready.sem, h_ready.done(l, KD + k) + KD))
            estimate(l, 4)
            make_x(l, 2)
            ffn_up(l, "b", lambda: split_hi(l, "f2b", 0, 0))
            ffn_down(l, "b", 5, lambda: None)
            estimate(l, 5)

    @block.vector
    def _(dve):
        credits(dve, lo_ready + [acc_free[1], prod_lo, sq_added, x_ready, scores_taken])
        V = nc.vector

        def split_lo(l, ph, s, i, width=None):
            w = width or WIDTH[ph]
            dve.wait_ge(hi_ready[s].sem, hi_ready[s].done(l, SPLIT_AT[ph][s] + i))
            V.tensor_tensor(w_lo[:, s, 0:w], raw[:, s, 0:w], w_hi[:, s, 0:w], ALU.subtract
                            ).then_inc(lo_ready[s].sem, 1)

        def pairs(n, l, body, following):
            with dve.Fori(0, n - 1) as i:
                body(i, None)
            body(n - 1, following)

        def ffn_up(l, ab, following):
            ph, at = "f1" + ab, (0 if ab == "a" else KF + KD)

            def body(i, nxt):
                split_lo(l, ph, 1, i)
                nxt() if nxt else split_lo(l, ph, 0, i + 1)
                dve.wait_ge(acc_free[0].sem, acc_free[0].done(l, GROUP_AT[ph][0] + i))
                dve.wait_ge(chunk_done[1].sem, chunk_done[1].done(l, SPLIT_AT[ph][1] + i))
                dve.wait_ge(prod_lo.sem, prod_lo.free(l, at + i))
                V.tensor_tensor(two(hid[:, :]), two(sil[:, :]), pair[1], ALU.mult).then_inc(acc_free[1].sem, 1)
                dve.wait_ge(prod_hi.sem, prod_hi.done(l, at + i))
                V.tensor_tensor(hid_lo[:, bass.ds(i, 1), :].rearrange("p a n -> p (a n)"), hid[:, :],
                                hid_hi[:, bass.ds(i, 1), :].rearrange("p a n -> p (a n)"), ALU.subtract
                                ).then_inc(prod_lo.sem, 1)
            pairs(F1, l, body, following)

        def add_square(l, n, p, k0):
            dve.wait_ge(sq_ready.sem, sq_ready.done(l, n * KD + k0))
            dve.wait_ge(sq_added.sem, sq_added.done(l, n * KD + k0 - 1))
            return V.tensor_tensor(acc[:, :], acc[:, :], sq[:, p, :], ALU.add)

        def clear_acc(l, n):
            if n:
                dve.wait_ge(stat_ready.sem, stat_ready.done(l, n - 1))
            V.memset(acc[:, :], 0.0)
            dve.drain()

        def ffn_down(l, ab, n, following):
            ph = "f2" + ab

            def body(i, nxt):
                for p in (0, 1):
                    split_lo(l, ph, 1, 2 * i + p)
                    if p == 0 or not nxt:
                        split_lo(l, ph, 0, 2 * i + p + 1)
                    else:
                        nxt()
                    tile_out(l, ph, n, p, i, 2 * i + p)
            clear_acc(l, n)
            pairs(F2 // 2, l, body, following)

        def tile_out(l, ph, n, p, i, m):
            r = add_square(l, n, p, m)
            r.then_inc(sq_added.sem, 1)

        def squares_of_h(l, n):
            clear_acc(l, n)
            for k in range(KD):
                add_square(l, n, k % 2, k).then_inc(sq_added.sem, 1)

        def inverse_rms(l, n):
            dve.wait_ge(stat_ready.sem, stat_ready.done(l, n))
            V.tensor_scalar(two(rms[:, 0, :]), stat, 1.0 / D_MODEL, EPS, ALU.mult, ALU.add
                            ).then_inc(ms_ready.sem, 1)
            dve.wait_ge(est_ready.sem, est_ready.done(l, n))
            V.scalar_tensor_tensor(out=rms[:, 2, :], in0=rms[:, 0, :], scalar=-0.5, in1=rms[:, 1, :],
                                   op0=ALU.mult, op1=ALU.mult)
            dve.drain()
            V.tensor_tensor(rms[:, 2, :], rms[:, 2, :], rms[:, 1, :], ALU.mult)
            dve.drain()
            V.scalar_tensor_tensor(out=rms[:, 3, :], in0=rms[:, 2, :], scalar=1.5, in1=rms[:, 1, :],
                                   op0=ALU.add, op1=ALU.mult)
            dve.drain()

        def make_x(l, n):
            for k in range(KD):
                if k >= 2:
                    dve.wait_ge(nx_ready.sem, nx_ready.done(l, n * KD + k - 2))
                V.tensor_tensor(nt[:, k % 2, :], h[:, k, :], rms[:, 3, :], ALU.mult).then_inc(t_ready.sem, 1)
                if k:
                    x_low(l, n, k - 1)
            x_low(l, n, KD - 1)

        def x_low(l, n, k):
            dve.wait_ge(nx_ready.sem, nx_ready.done(l, n * KD + k))
            V.tensor_tensor(x_lo[:, k, :], nx[:, k % 2, :], x_hi[:, k, :], ALU.subtract
                            ).then_inc(x_ready.sem, 1)

        def residual(l, n):
            for k in range(KD):
                V.tensor_tensor(nt[:, k % 2, :], y[:, k, :], rms[:, 3, :], ALU.mult)
                dve.drain()
                for g, cols in ((0, slice(0, SEQ)), (1, slice(SEQ, TOK))):
                    r = V.scalar_tensor_tensor(out=h[:, k, cols], in0=nt[:, k % 2, cols],
                                               scalar=post_gate[:, n, k, g:g + 1], in1=h[:, k, cols],
                                               op0=ALU.mult, op1=ALU.add)
                r.then_inc(h_ready.sem, 1)

        def step(ins):
            dve.drain()

        def forget(l):
            dve.wait_ge(f_turned.sem, f_turned.done(l, 0))
            V.memset(fx[:, 0, :, :], 0.0)
            dve.drain()
            V.tensor_copy(fx[:, 0, 0:4, :].rearrange("p t h -> p (t h)"), ps[:, 4, 0:32])
            V.tensor_copy(fx[0:DEC, 0, 4, :], ps[0:DEC, 4, 32:40])
            dve.drain()
            bias = b_forget[:, :].rearrange("p (a h) -> p a h", a=1).to_broadcast((P, NT, B_HEADS))
            x, na, e, z, z2, pl = (fx[:, k, :, :] for k in range(6))
            V.tensor_tensor(x, x, bias, ALU.add)
            dve.drain()
            V.tensor_scalar(z, x, -1.0, None, ALU.mult)
            dve.drain()
            V.tensor_tensor(na, x, z, ALU.min).then_inc(f_neg.sem, 1)
            dve.wait_ge(f_exp.sem, f_exp.done(l, 0))
            V.tensor_scalar(z2, e, 2.0, None, ALU.add)
            dve.drain()
            V.reciprocal(z2, z2)
            dve.drain()
            V.tensor_tensor(z, e, z2, ALU.mult)
            dve.drain()
            V.tensor_tensor(z2, z, z, ALU.mult)
            dve.drain()
            V.tensor_scalar(pl, z2, 1.0 / 17, None, ALU.mult)
            for odd in (15, 13, 11, 9, 7, 5, 3):
                dve.drain()
                V.scalar_tensor_tensor(out=pl, in0=pl, scalar=1.0 / odd, in1=z2, op0=ALU.add, op1=ALU.mult)
            dve.drain()
            V.scalar_tensor_tensor(out=pl, in0=pl, scalar=1.0, in1=z, op0=ALU.add, op1=ALU.mult)
            V.tensor_scalar(x, x, 0.0, None, ALU.min)
            dve.drain()
            V.scalar_tensor_tensor(out=logf[:, :, :], in0=pl, scalar=-2.0, in1=x, op0=ALU.mult, op1=ALU.add)
            dve.drain()
            V.tensor_copy(earlier_f[:, 1, :], logf[:, 0, :])
            V.tensor_copy(later_f[:, 6, :], cache_f[:, 7, :])
            for t in range(2, 4):
                dve.drain()
                V.tensor_tensor(earlier_f[:, t, :], earlier_f[:, t - 1, :], logf[:, t - 1, :], ALU.add)
            for t in range(5, -1, -1):
                dve.drain()
                r = V.tensor_tensor(later_f[:, t, :], later_f[:, t + 1, :], cache_f[:, t + 1, :], ALU.add)
            r.then_inc(f_sums_in.sem, 1)

        def spatial(l):
            dve.wait_ge(raw_full[1].sem, raw_full[1].done(l, RAW_AT["spatial"][1]))
            mask = const[:, TRI_LE:TRI_LE + 1, :].to_broadcast((P, C_GROUPS, P))
            V.tensor_tensor(w_mix[:, :, :], raw[:, 1, 0:C_GROUPS * P].rearrange("p (g n) -> p g n", g=C_GROUPS),
                            mask, ALU.mult).then_inc(raw_read[1].sem, 1)
            dve.wait_ge(vc_copied.sem, vc_copied.done(l, 0))
            V.reciprocal(c_stat[:, 2, :], c_stat[:, 1, :])
            dve.drain()
            for t in range(NT):
                m = P if t < 4 else DEC
                r = V.scalar_tensor_tensor(out=v_tok_c[0:m, t, :], in0=v_tok_c[0:m, t, :],
                                           scalar=c_stat[0:m, 2, t:t + 1], in1=c_gain[0:m, :],
                                           op0=ALU.mult, op1=ALU.mult)
            r.then_inc(vc_ready.sem, 1)
            for T in (0, 1):
                dve.wait_ge(mixed.sem, mixed.done(l, T))
                V.tensor_tensor(c_mix[:, 0:SEQ].rearrange("p (t n) -> p t n", t=4),
                                ps[:, 2 * T, :].rearrange("p (t n) -> p t n", t=4),
                                c_bias[:, T:T + 1, :].to_broadcast((P, 4, P)), ALU.add)
                V.tensor_tensor(c_mix[:, SEQ:TOK], ps[:, 2 * T + 1, 0:DEC], c_bias[:, T, 0:DEC], ALU.add)
                dve.drain()
                r = V.tensor_tensor(proj[:, UC + T, :], proj[:, UC + T, :], c_mix[:, :], ALU.mult)
                if T == 0:
                    dve.drain()
            dve.wait_ge(out_small.sem, out_small.done(l, 1))
            V.memset(c_stat[:, 0, :], 1.0).then_inc(oc_ready.sem, 1)

        def pair_units(l, pr, b, cached):
            base = pr * UNITS

            def logits(u):
                hh, i, m, nk, nb = unit_shape(u, cached)
                n = base + u
                s, s_ps = prob[0:m, u % 2, 0:nk], score[u % 2][0:m, 0:nk]
                dve.wait_ge(scores_ready.sem, scores_ready.done(l, n))
                dve.wait_ge(prob_turned.sem, prob_turned.free(l, n))
                if cached == A_WIN:
                    if u == 0:
                        dve.wait_ge(strip_in.sem, strip_in.done(l, pr))
                    c0 = 512 - P * i if i < 4 else 0
                    V.tensor_tensor(s, s_ps, strip[0:m, hh, c0:c0 + nk], ALU.add).then_inc(scores_taken.sem, 1)
                else:
                    if u == 0:
                        dve.wait_ge(decay_s_in.sem, decay_s_in.done(l, b))
                    if u == 2:
                        dve.wait_ge(decay_p_in.sem, decay_p_in.done(l, b))
                    d = decay_p[:, hh, 0:nk] if i < 4 else decay_s[0:m, hh, 0:nk]
                    fq = f_query[0:m, i, bass.ds(b * 2 + hh, 1)]
                    V.scalar_tensor_tensor(out=s, in0=d, scalar=fq, in1=s_ps, op0=ALU.add, op1=ALU.add
                                           ).then_inc(scores_taken.sem, 1)
                    dve.drain()
                    diag = prob[0:m, u % 2, nk - m:nk]
                    V.tensor_tensor(diag, diag, const[0:m, CAUSAL, 0:m], ALU.add)
                dve.drain()
                V.reduce_max(row[0:m, 0, u % 2:u % 2 + 1], s, AXX)
                dve.drain()
                V.tensor_scalar(row[0:m, 1, u % 2:u % 2 + 1], row[0:m, 0, u % 2:u % 2 + 1], -1.0, None, ALU.mult
                                ).then_inc(shift_ready.sem, 1)

            def inverse(u):
                hh, i, m, nk, nb = unit_shape(u, cached)
                n = base + u
                dve.wait_ge(exp_ready.sem, exp_ready.done(l, n))
                V.reciprocal(row[0:m, 3, u % 2:u % 2 + 1], row[0:m, 2, u % 2:u % 2 + 1]
                             ).then_inc(inv_ready.sem, 1)

            logits(0)
            for u in range(UNITS):
                if u + 1 < UNITS:
                    logits(u + 1)
                inverse(u)

        V.memset(c_stat[:, :, :], 1.0)
        dve.drain()
        V.memset(eps_t[:, :], EPS).then_inc(eps_ready.sem, 1)
        dve.wait_ge(start_in.sem, start_in.done(0, 2))
        dve.sem_inc(h_ready.sem, KD)
        with dve.Fori(0, DEPTH) as l:
            squares_of_h(l, 0)
            dve.wait_ge(small_in.sem, small_in.done(l, 8))
            for s in (0, 1):
                dve.wait_ge(raw_read[s].sem, l * (ADA_PAIRS + s) + ADA_PAIRS + 1)
            m5 = mods[:, :, :, :].rearrange("p m (k s) g -> p (m k) s g", s=2)
            for s in (0, 1):
                V.tensor_tensor(m5[:, :, s, :], ps[:, 6 + s, 0:N_ADA].rearrange("p (j g) -> p j g", g=2),
                                b_ada[:, :, :].rearrange("p m (k s) -> p (m k) s", s=2)[:, :, s:s + 1]
                                .to_broadcast((P, ADA_PAIRS, 2)), ALU.add)
            dve.drain()
            for n in range(3):
                for g in (0, 1):
                    V.scalar_tensor_tensor(out=pre_scale[:, n, :, g], in0=mods[:, 3 * n + 1, :, g], scalar=1.0,
                                           in1=norm_g[:, 2 * n, :], op0=ALU.add, op1=ALU.mult)
                    V.scalar_tensor_tensor(out=post_gate[:, n, :, g], in0=mods[:, 3 * n + 2, :, g],
                                           scalar=1.0 if n == 1 else 0.5,
                                           in1=norm_g[:, 2 * n + 1, :], op0=ALU.mult, op1=ALU.mult)
            dve.drain()
            inverse_rms(l, 0)
            split_lo(l, "f1a", 0, 0)
            make_x(l, 0)
            ffn_up(l, "a", lambda: split_lo(l, "f2a", 0, 0))
            ffn_down(l, "a", 1, lambda: split_lo(l, "win", 0, 0))
            inverse_rms(l, 1)
            residual(l, 0)
            squares_of_h(l, 2)
            inverse_rms(l, 2)
            make_x(l, 1)

            def proj_pair(i, nxt):
                split_lo(l, "win", 1, i)
                nxt() if nxt else split_lo(l, "win", 0, i + 1)
                dve.wait_ge(chunk_done[1].sem, chunk_done[1].done(l, SPLIT_AT["win"][1] + i))
                V.tensor_copy(two(proj[:, bass.ds(i * 2 + 1, 1), :].rearrange("p a n -> p (a n)")), pair[1]
                              ).then_inc(acc_free[1].sem, 1)
            pairs(WIN, l, proj_pair, lambda: split_lo(l, "fb", 0, 0))
            dve.wait_ge(acc_free[0].sem, acc_free[0].done(l, GROUP_AT["fb"][0]))
            hold(dve, "dve")
            dve.drain()
            dve.sem_inc(proj_ready.sem, N_PROJ)
            forget(l)
            spatial(l)
            dve.wait_ge(f_rows_ready.sem, f_rows_ready.done(l, 0))
            hold(dve, "dve")
            with dve.Fori(0, A_PAIRS) as a:
                pair_units(l, a, None, A_WIN)
            with dve.Fori(0, B_PAIRS) as b:
                pair_units(l, b + A_PAIRS, b, PAST)
            split_lo(l, "gate", 0, 0, KD * P)
            for t, src in enumerate([QA, QA + 1, QB, QB + 1, QB + 2, QB + 3, UC, UC + 1]):
                dve.wait_ge(o_split_hi.sem, o_split_hi.done(l, t))
                V.tensor_tensor(o_lo[:, t, :], proj[:, src, :], o_hi[:, t, :], ALU.subtract
                                ).then_inc(o_ready.sem, 1)

            def gate_tile(m, nxt):
                for br, k in enumerate((2, 4, 2)):
                    n = m * 3 + br
                    split_lo(l, "gate", 1, n, k * P)
                    if br < 2 or not nxt:
                        split_lo(l, "gate", 0, n + 1, KD * P)
                    else:
                        nxt()
                    dve.wait_ge(acc_free[0].sem, acc_free[0].done(l, GROUP_AT["gate"][0] + n))
                    dve.wait_ge(chunk_done[1].sem, chunk_done[1].done(l, SPLIT_AT["gate"][1] + n))
                    if br == 0:
                        dve.wait_ge(prod_lo.sem, prod_lo.free(l, KF + m))
                    V.tensor_tensor(two(mtmp[:, :] if br else msum[:, :]), two(sil[:, :]), pair[1], ALU.mult
                                    ).then_inc(acc_free[1].sem, 1)
                    dve.drain()
                    if br:
                        r = V.tensor_tensor(msum[:, :], msum[:, :], mtmp[:, :], ALU.add)
                        if br == 1:
                            dve.drain()
                r.then_inc(mixer_begun.sem, 1)
                dve.wait_ge(prod_hi.sem, prod_hi.done(l, KF + m))
                V.tensor_tensor(m_lo[:, bass.ds(m, 1), :].rearrange("p a n -> p (a n)"), msum[:, :],
                                m_hi[:, bass.ds(m, 1), :].rearrange("p a n -> p (a n)"), ALU.subtract
                                ).then_inc(prod_lo.sem, 1)
            pairs(KD, l, gate_tile, lambda: split_lo(l, "out", 0, 0))
            clear_acc(l, 3)

            def out_pair(i, nxt):
                split_lo(l, "out", 1, i)
                tile_out(l, "out", 3, 0, i, 2 * i)
                nxt() if nxt else split_lo(l, "out", 0, i + 1)
                tile_out(l, "out", 3, 1, i, 2 * i + 1)
            pairs(OUTP, l, out_pair, lambda: split_lo(l, "f1b", 0, 0))
            inverse_rms(l, 3)
            residual(l, 1)
            squares_of_h(l, 4)
            inverse_rms(l, 4)
            make_x(l, 2)
            ffn_up(l, "b", lambda: split_lo(l, "f2b", 0, 0))
            ffn_down(l, "b", 5, lambda: None)
            inverse_rms(l, 5)
            residual(l, 2)
            dve.drain()
            dve.sem_inc(small_used.sem, 1)

    @block.gpsimd
    def _(pool):
        credits(pool, [small_used])
        with pool.Fori(0, DEPTH) as l:
            pool.wait_ge(proj_ready.sem, proj_ready.done(l, N_PROJ - 1))
            for d0, p0, n in ((0, KA, 4), (4, KB, 8)):
                nc.gpsimd.dma_start(outs["kv"][bass.ds(l, 1), :, d0:d0 + n, :].rearrange("a p t n -> (a p) t n"),
                                    proj[:, p0:p0 + n, :]).then_inc(out_kv.sem, 32)
            pool.wait_ge(f_sums_in.sem, f_sums_in.done(l, 0))
            nc.gpsimd.dma_start(outs["logf"][bass.ds(l, 1), :, :].rearrange("a p n -> (a p) n"),
                                logf[:, :, :].rearrange("p t h -> p (t h)")).then_inc(out_small.sem, 16)
            pool.wait_ge(vc_ready.sem, vc_ready.done(l, 0))
            nc.gpsimd.dma_start(outs["vc"][bass.ds(l, 1), :, :].rearrange("a p n -> (a p) n"),
                                v_tok_c[0:DEC, 4, :]).then_inc(out_small.sem, 16)
            pool.wait_ge(f_rows_ready.sem, f_rows_ready.done(l, 0))
            nc.gpsimd.dma_start(scratch[bass.ds(l, 1), :, :].rearrange("a h n -> (a h) n"), f_rows[:, :]
                                ).then_inc(rows_out.sem, 16)

            def divide(pr, cached):
                for u in range(UNITS):
                    hh, i, m, nk, nb = unit_shape(u, cached)
                    pool.wait_ge(inv_ready.sem, inv_ready.done(l, pr * UNITS + u))
                    hold(pool, "pool")
                    s = prob[0:m, u % 2, 0:nk]
                    nc.gpsimd.tensor_scalar(s, s, row[0:m, 3, u % 2:u % 2 + 1], None, ALU.mult
                                            ).then_inc(prob_ready.sem, 1)
            with pool.Fori(0, A_PAIRS) as a:
                divide(a, A_WIN)
            with pool.Fori(0, B_PAIRS) as b:
                divide(b + A_PAIRS, PAST)
        pool.wait_ge(h_ready.sem, DEPTH * h_ready.per_layer + KD)
        nc.gpsimd.dma_start(outs["h"], h[:, :, :]).then_inc(out_h.sem, 16)
        pool.wait_ge(out_h.sem, 16)
        pool.wait_ge(out_kv.sem, out_kv.done(DEPTH - 1, 3))
        pool.wait_ge(out_small.sem, out_small.done(DEPTH - 1, 1))
        pool.wait_ge(small_in.sem, small_in.done(DEPTH - 1, 8))

    block_ctx.__exit__(None, None, None)


def constants():
    j, k = np.arange(P)[:, None], np.arange(P)[None, :]
    out = np.zeros((P, NCONST, P), np.float32)
    out[:, IDENT] = j == k
    out[:, ONES] = 1.0
    out[:, NONES] = -1.0
    out[:, TRI_LE] = j <= k
    out[:, NTRI_LE] = np.where(j <= k, np.float32(-1), np.float32(0))
    out[:, TRI_GT] = j > k
    out[:, CAUSAL] = np.where(k > j, np.float32(NEG), np.float32(0))
    return out


def tiles(w, k_tiles, chunks):
    n, rows, cols = w.shape
    kt = k_tiles // chunks
    w = w.reshape(n, chunks, kt, P, cols // P, P)
    return np.ascontiguousarray(w.transpose(0, 4, 1, 3, 2, 5)).reshape(n * (cols // P) * chunks, P, kt * P)


def layout(v):
    f = {k: np.asarray(x) for k, x in v.items()}
    g = {}
    x = np.concatenate([f["x_prompt"][0], f["x_sample"][0]], 0).T
    g["x"] = x.reshape(KD, P, TOK).transpose(1, 0, 2)
    c = np.concatenate([f["c_prompt"], f["c_sample"]], 0).T
    g["cond"] = c.reshape(KD, P, 2).transpose(1, 0, 2)
    g["const"] = constants()
    g["ada"] = tiles(f["w_ada"], KD, 1)
    g["b_ada"] = f["b_ada"].reshape(DEPTH, N_ADA, P).transpose(0, 2, 1)
    g["norm_g"] = f["norm_g"].reshape(DEPTH, 6 * KD, P).transpose(0, 2, 1)
    w1 = f["ffn_w1"].reshape(DEPTH * 2, D_MODEL, 2, D_FF)
    w1 = np.pad(w1, ((0, 0), (0, 0), (0, 0), (0, KF * P - D_FF)))
    w1 = w1.reshape(DEPTH * 2, D_MODEL, 2, KF, P).transpose(0, 1, 3, 2, 4).reshape(DEPTH * 2, D_MODEL, 2 * KF * P)
    g["f1"] = tiles(w1, KD, 1)
    w2 = f["ffn_w2"].reshape(DEPTH * 2, D_FF, D_MODEL)
    g["f2"] = tiles(np.pad(w2, ((0, 0), (0, KF * P - D_FF), (0, 0))), KF, 2)
    w = f["w_in"]
    fb0 = 3 * A_HEADS * HD + 3 * B_HEADS * HD
    uc0 = fb0 + B_HEADS
    gl0 = uc0 + 512
    fb = np.pad(w[:, :, fb0:uc0], ((0, 0), (0, 0), (0, P - B_HEADS)))
    g["win"] = tiles(np.concatenate([w[:, :, :fb0], w[:, :, uc0:gl0], fb], 2), KD, 1)
    gl = w[:, :, gl0:].reshape(DEPTH, D_MODEL, 3, KD, P).transpose(0, 1, 3, 2, 4).reshape(DEPTH, D_MODEL, -1)
    g["gate"] = tiles(gl, KD, 1)
    g["bra"] = tiles(f["w_br_a"], 2, 1)
    g["brb"] = tiles(f["w_br_b"], 4, 1)
    g["brc"] = tiles(f["w_br_c"], 2, 1)
    g["wout"] = tiles(f["w_out"], KD, 1)
    g["b_gate"] = f["b_gate"].reshape(DEPTH, 3 * KD, P).transpose(0, 2, 1)
    g["b_forget"] = np.broadcast_to(f["b_forget"][:, None, :], (DEPTH, P, B_HEADS))
    g["c_gain"] = np.broadcast_to(f["c_vnorm_g"][:, None, :], (DEPTH, P, 256))
    cb = f["c_spatial_b"].reshape(DEPTH, 2, 2, 1, P)
    g["c_bias"] = np.broadcast_to(cb, (DEPTH, 2, 2, HD, P)).transpose(0, 2, 3, 1, 4).reshape(DEPTH, P, 2 * P)
    g["cache_f"] = f["cache_b_logf"][:, 0].reshape(DEPTH, 8, P, B_HEADS).transpose(0, 2, 1, 3).reshape(DEPTH, P, 64)
    g["c_spatial"] = f["c_spatial_w"].transpose(0, 3, 1, 2).reshape(DEPTH, P, C_GROUPS * P)
    for name in ("cache_a_k", "cache_a_v"):
        g[name] = f[name].reshape(DEPTH, A_WIN, A_HEADS * HD)
    p, c = np.arange(P)[:, None], np.arange(STRIP)[None, :]
    rel = np.clip(p - (c - 512), -(CHUNK - 1), REL_MAX) + CHUNK - 1
    strip = f["a_rel_bias"][:, :, rel].transpose(0, 2, 1, 3)
    strip = np.where(((p < CHUNK) & (c >= 512 + CHUNK))[None, :, None, :], np.float32(NEG), strip)
    g["strip"] = strip.reshape(DEPTH, P, A_PAIRS, 2, STRIP).transpose(0, 2, 1, 3, 4).reshape(-1, P, 2, STRIP)
    for ab, heads, n in (("a", A_HEADS, A_WIN), ("b", B_HEADS, PAST)):
        k = f[f"cache_{ab}_k"][:, 0].reshape(DEPTH, n, heads // 2, P)
        g["ck_" + ab] = k.transpose(0, 2, 3, 1).reshape(-1, P, n)
        vv = f[f"cache_{ab}_v"][:, 0].reshape(DEPTH, n // P, P, heads // 2, P)
        g["cv_" + ab] = vv.transpose(0, 3, 2, 1, 4).reshape(-1, P, n)
    return {k: np.ascontiguousarray(x) for k, x in g.items()}


OUTS = {"h": (P, KD, TOK), "kv": (DEPTH, P, 12, TOK), "logf": (DEPTH, P, NT * B_HEADS), "vc": (DEPTH, DEC, 256),
        "roll_k": (DEPTH, A_WIN - DEC, A_HEADS * HD), "roll_v": (DEPTH, A_WIN - DEC, A_HEADS * HD)}


def kernel(**inputs):
    import concourse.bacc as bacc
    from concourse.bass_utils import run_bass_kernel_spmd

    nc = bacc.Bacc("TRN2", target_bir_lowering=False, num_devices=1)
    arrays = layout(inputs)
    ins = {k: nc.dram_tensor(f"in_{k}", a.shape, mybir.dt.from_np(a.dtype), kind="ExternalInput").ap()
           for k, a in arrays.items()}
    outs = {k: nc.dram_tensor(f"out_{k}", s, F32, kind="ExternalOutput").ap() for k, s in OUTS.items()}
    build_program(nc, ins, outs)
    r = run_bass_kernel_spmd(nc, [{f"in_{k}": a for k, a in arrays.items()}], core_ids=[0]).results[0]
    r = {k: np.asarray(r[f"out_{k}"]) for k in OUTS}

    h = r["h"].transpose(2, 1, 0).reshape(TOK, D_MODEL)
    kv = r["kv"].transpose(0, 3, 2, 1).reshape(DEPTH, TOK, 12 * P)
    ka, va, kb, vb = np.split(kv, [256, 512, 1024], axis=2)
    logf = r["logf"].reshape(DEPTH, P, NT, B_HEADS).transpose(0, 2, 1, 3).reshape(DEPTH, NT * P, B_HEADS)

    def prompt(t, heads):
        return np.ascontiguousarray(t[:, :SEQ]).reshape(DEPTH, 1, SEQ, heads, HD)

    def sample(t, heads, before=None):
        t = t[:, SEQ:TOK]
        if before is not None:
            t = np.concatenate([before, t], 1)
        return np.ascontiguousarray(t).reshape(DEPTH, 1, -1, heads, HD)

    return (np.ascontiguousarray(h[:SEQ])[None], np.ascontiguousarray(h[SEQ:])[None],
            prompt(ka, A_HEADS), prompt(va, A_HEADS), prompt(kb, B_HEADS), prompt(vb, B_HEADS),
            np.ascontiguousarray(logf[:, :SEQ])[:, None],
            sample(ka, A_HEADS, r["roll_k"]), sample(va, A_HEADS, r["roll_v"]),
            sample(kb, B_HEADS), sample(vb, B_HEADS),
            np.ascontiguousarray(logf[:, SEQ:TOK])[:, None], r["vc"][:, None])
```

```python
import numpy as np
import concourse.bass as bass
from concourse import mybir

F32 = mybir.dt.float32
F32R = mybir.dt.float32r
ACT = mybir.ActivationFunctionType
ALU = mybir.AluOpType
AXX = mybir.AxisListType.X

P = 128
D_MODEL = 1024
SEQ = 512
DEC = 64
TOK = SEQ + DEC
HALF = TOK // 2
DEPTH = 2
PAST = 1024
A_WIN = 512
HD = 64
A_HEADS, B_HEADS = 4, 8
CHUNK = 64
REL_MAX = 128
C_GROUPS = 4
D_FF = 2752
KD = D_MODEL // P
KF = -(-D_FF // P)
KF2 = KF // 2
N_MOD = 9
N_ADA = N_MOD * KD
NT = 5
EPS = 1e-6
NEG = -1e30

A_PAIRS, B_PAIRS = A_HEADS // 2, B_HEADS // 2
NP = A_PAIRS + B_PAIRS
UNITS = 10
SEGS_A, SEGS_B = 12, 14
NSEG = B_PAIRS * SEGS_B + A_PAIRS * SEGS_A
PROBS = 3
STRIP = 640
NCONST = 5
IDENT, ONES, TRI_LE, TRI_GT, CAUSAL = range(NCONST)
TRI = 3 * KD
KT = TRI // 2
SLOT = KT * P

ADA_FIRST, ADA_UP, ADA_DOWN = 32, 2, 3
ADA_LAYER = ADA_UP * KF + ADA_DOWN * (KD // 2)
ADA_N = (KF + KD, KF + KD // 2)
RING = 4
assert sum(ADA_N) == ADA_LAYER and ADA_FIRST % (2 * RING) == 0
assert ADA_FIRST + DEPTH * ADA_LAYER == DEPTH * N_ADA and ADA_FIRST + ADA_LAYER >= N_ADA + 2 * KD

PHASES = [("f1a", KF, KF), ("f2a", KD, KD), ("tri", NP + 1, NP + 1), ("uc", 1, 1), ("gate", 2 * KD, 2 * KD),
          ("out", KD // 2, KD // 2), ("f1b", KF, KF), ("f2b", KD, KD)]
GROUPS = [("f1a", KF, KF), ("f2a", KD // 2, KD // 2), ("tri", 2 * (NP + 1), NP + 1), ("uc", 1, 1),
          ("gate", 3 * KD, 3 * KD), ("out", KD // 2, KD // 2), ("f1b", KF, KF), ("f2b", KD // 2, KD // 2)]


def running(counts):
    at, base = [0, 0], {}
    for name, a, b in counts:
        base[name] = tuple(at)
        at[0] += a
        at[1] += b
    return base, tuple(at)


SPLIT_AT, SPLIT_N = running(PHASES)
GROUP_AT, GROUP_N = running(GROUPS)
WIDTH = {"f1a": KD * P, "f2a": KF2 * P, "tri": SLOT, "uc": KD * P, "gate": KD * P, "out": KD * P, "f1b": KD * P,
         "f2b": KF2 * P}


class Signal:

    def __init__(self, nc, name, per_layer, slots=0, step=1):
        self.sem = nc.alloc_semaphore(name)
        self.per_layer, self.slots, self.step = per_layer, slots, step

    def done(self, l, n):
        return (l * self.per_layer + n + 1) * self.step + self.slots

    def free(self, l, n):
        return l * self.per_layer + n + 1


UNIT = [(0, 4), (1, 4)] + [(hh, i) for i in range(4) for hh in (0, 1)]


def unit_shape(u, cached):
    hh, i = UNIT[u]
    if i < 4:
        return hh, i, P, P * (i + 1), i + 1, [(0, P * (i + 1))]
    nk = cached + DEC
    return hh, i, DEC, nk, cached // P + 1, [(c, min(c + 512, nk)) for c in range(0, nk, 512)]


def first_segment(u, cached):
    return sum(len(unit_shape(v, cached)[5]) for v in range(u))


def last_user(u):
    return u - PROBS if u >= PROBS else max(v for v in range(UNITS) if v % PROBS == u) - UNITS


def build_program(nc, ins, outs):
    arena = [(nc.sbuf_base + 31) // 32 * 32]

    def sb(name, shape, dt=F32, at=None):
        n = int(np.prod(shape[1:])) * 4
        if at is None:
            at = arena[0]
            arena[0] += (n + 31) // 32 * 32
        assert at + n <= nc.sbuf_usable_end, (name, at + n, nc.sbuf_usable_end)
        return nc.alloc_sbuf_tensor_at(name, shape, dt, offset=at)

    h = sb("h", [P, KD, TOK])
    x_at = arena[0]
    x_hi = sb("x_hi", [P, KD, TOK], F32R)
    x_lo = sb("x_lo", [P, KD, TOK], F32R)
    y = sb("y", [P, KD, TOK], at=x_at)
    acc = sb("acc", [P, TOK], at=x_at + KD * TOK * 4)
    raw = sb("w_raw", [P, 2, SLOT])
    w_hi = sb("w_hi", [P, 2, SLOT], F32R)
    w_lo = sb("w_lo", [P, 2, SLOT], F32R)
    ada_w = sb("ada_w", [P, 2, KD * P])
    const = sb("const", [P, NCONST, P])
    cond = sb("cond", [P, KD, 2])
    cond_s = sb("cond_silu", [P, KD, 2])
    eps_t = sb("eps", [P, 1])
    ada_all = sb("ada_all", [P, DEPTH * N_ADA, 2])
    b_ada = sb("b_ada", [P, DEPTH * N_ADA])
    mods = sb("mods", [P, N_MOD, KD, 2])
    norm_g = sb("norm_g", [P, 6, KD])
    pre_scale = sb("pre_scale", [P, 3, KD, 2])
    post_gate = sb("post_gate", [P, 3, KD, 2])
    b_gate = sb("b_gate", [P, 3, KD])
    f_query = sb("f_query", [P, NT, B_HEADS])
    c_stat = sb("c_stat", [P, 3, NT])
    row = sb("row", [P, 5, PROBS])
    seg_max = sb("seg_max", [P, 2])
    tmp_at = arena[0]
    sil = sb("sil", [P, TOK])
    hid = sb("hid", [P, TOK])
    sq = sb("sq", [P, 2, TOK], at=tmp_at)
    big = arena[0]
    hid_hi = sb("hid_hi", [P, KF, TOK], F32R, at=big)
    hid_lo = sb("hid_lo", [P, KF, TOK], F32R, at=big + KF * TOK * 4)
    rms = sb("rms", [P, 4, TOK], at=big)
    nt = sb("norm_t", [P, 2, TOK], at=big + 16 * TOK)
    nx = sb("norm_x", [P, 2, TOK], at=big + 24 * TOK)
    ada_ring = sb("ada_ring", [P, RING, 2, KD * P], at=big)
    o_hi = sb("o_hi", [P, KD, TOK], F32R, at=big)
    o_lo = sb("o_lo", [P, KD, TOK], F32R, at=big + KD * TOK * 4)
    att = big + 2 * KD * TOK * 4
    m_hi = sb("m_hi", [P, KD, TOK], F32R, at=att)
    m_lo = sb("m_lo", [P, KD, TOK], F32R, at=att + KD * TOK * 4)
    sig = sb("sig", [P, 3, TOK], at=att + 2 * KD * TOK * 4)
    msum = sb("msum", [P, TOK], at=att + (2 * KD + 3) * TOK * 4)
    mtmp = sb("mtmp", [P, TOK], at=att + (2 * KD + 4) * TOK * 4)
    SC = PAST + DEC
    at = [att]

    def sa(name, shape, keep=True):
        t = sb(name, shape, at=at[0])
        if keep:
            at[0] += int(np.prod(shape[1:])) * 4
        return t

    f_rows = sa("f_rows", [B_HEADS, SEQ + SC], keep=False)
    prob = sa("prob", [P, PROBS, SC])
    prob_t = sa("prob_t", [P, 2, TOK])
    sp_at = at[0]
    decay_s = sa("decay_s", [P, 2, SC])
    decay_p = sa("decay_p", [P, 2, SEQ])
    strip = sb("strip", [P, 2, STRIP], at=sp_at)
    v_tok_c = sb("v_tok_c", [P, NT, 256], at=sp_at)
    w_mix = sb("w_mix", [P, C_GROUPS, P], at=sp_at + NT * 1024)
    c_gain = sb("c_gain", [P, 256], at=sp_at + NT * 1024 + 2048)
    c_bias = sb("c_bias", [P, 2, P], at=sp_at + NT * 1024 + 3072)
    fx = sb("fx", [P, 6, NT, B_HEADS], at=sp_at + NT * 1024 + 4096)
    cache_k = sa("cache_k", [P, PAST])
    cache_v = sa("cache_v", [P, 8, P])
    q_st = sa("q_stage", [P, TOK])
    k_st = sa("k_stage", [P, TOK])
    v_st = sa("v_stage", [P, TOK])
    nxt = sa("next", [P, 3, TOK])
    v_tok = sa("v_tok", [P, NT, P])
    o_tok = sa("o_tok", [P, NT, P])
    c_mix = sa("c_mix", [P, 2, TOK])
    cache_f = sa("cache_f", [P, 8, B_HEADS])
    later_f = sa("later_f", [P, 8, B_HEADS])
    earlier_f = sa("earlier_f", [P, 4, B_HEADS])
    logf = sa("logf", [P, NT, B_HEADS])
    b_forget = sa("b_forget", [P, B_HEADS])

    ps = nc.alloc_psum_tensor("ps", [P, 8, 512], F32)
    pair = [ps[:, 0:2, 0:HALF], ps[:, 2:4, 0:HALF]]
    stat = ps[:, 4:6, 0:HALF]
    ada_ps = ps[:, 6, :]
    score = [ps[:, 4, :], ps[:, 5, :]]
    turned = ps[:, 6, :]
    att_out = ps[:, 7, :]
    scratch = nc.dram_tensor("f_scratch", (DEPTH, B_HEADS, SEQ + SC), F32, kind="Internal").ap()

    def two(ap):
        return ap.rearrange("p (b n) -> p b n", b=2)

    def tile(t, k):
        return t[:, bass.ds(k, 1), :].rearrange("p a n -> p (a n)")

    S = lambda *a, **k: Signal(nc, *a, **k)
    raw_full = [S(f"raw_full{s}", SPLIT_N[s], step=16) for s in (0, 1)]
    hi_ready = [S(f"hi_ready{s}", SPLIT_N[s]) for s in (0, 1)]
    lo_ready = [S(f"lo_ready{s}", SPLIT_N[s], 1) for s in (0, 1)]
    chunk_done = [S(f"chunk_done{s}", SPLIT_N[s], 1) for s in (0, 1)]
    acc_free = [S(f"acc_free{s}", GROUP_N[s], 1) for s in (0, 1)]
    first_full = [S(f"first_full{s}", 0, step=16) for s in range(RING)]
    first_used = S("first_used", 0, RING)
    ada_full = [S(f"ada_full{s}", ADA_N[s], step=16) for s in (0, 1)]
    ada_used = [S(f"ada_used{s}", ADA_N[s], 1) for s in (0, 1)]
    prod_hi = S("prod_hi", 2 * KF + KD)
    prod_lo = S("prod_lo", 2 * KF + KD, 1)
    merged = S("merged", KD)
    sq_ready = S("sq_ready", 6 * KD)
    sq_added = S("sq_added", 6 * KD, 2)
    stat_ready = S("stat_ready", 6)
    ms_ready = S("ms_ready", 6)
    est_ready = S("est_ready", 6)
    t_ready = S("t_ready", 3 * KD)
    nx_ready = S("nx_ready", 3 * KD)
    x_ready = S("x_ready", 3 * KD, 2)
    h_ready = S("h_ready", 3 * KD)
    start_in = S("start_in", 4, step=16)
    small_in = S("small_in", 2, step=16)
    roll_out = S("roll_out", 2, step=16)
    small_used = S("small_used", 1, 1)
    mix_in = S("mix_in", 5, step=16)
    cond_ready = S("cond_ready", 1)
    eps_ready = S("eps_ready", 1)
    ada_read = S("ada_read", 1, 1)
    tri_done = S("tri_done", 2 * (NP + 1))
    nxt_full = S("nxt_full", 3 * (NP + 1))
    logits_turned = S("logits_turned", 1)
    f_neg = S("f_neg", 1)
    f_exp = S("f_exp", 1)
    f_sums_in = S("f_sums_in", 1)
    f_sums = S("f_sums", 1)
    f_rows_ready = S("f_rows_ready", 1)
    vc_turned = S("vc_turned", 1)
    vc_copied = S("vc_copied", 1)
    vc_ready = S("vc_ready", 1)
    mixed = S("mixed", 1)
    mix_ready = S("mix_ready", 1)
    strip_in = S("strip_in", A_PAIRS, step=16)
    ck_in = S("ck_in", NP, step=16)
    cv_in = S("cv_in", NP, step=16)
    decay_s_in = S("decay_s_in", B_PAIRS, step=16)
    decay_p_in = S("decay_p_in", B_PAIRS, step=16)
    rows_out = S("rows_out", 1, step=16)
    q_staged = S("q_staged", NP)
    k_staged = S("k_staged", NP)
    v_staged = S("v_staged", NP)
    v_turned = S("v_turned", NP)
    v_ready = S("v_ready", NP)
    scores_ready = S("scores_ready", NSEG)
    scores_taken = S("scores_taken", NSEG, 2)
    shift_ready = S("shift_ready", NP * UNITS)
    exp_ready = S("exp_ready", NP * UNITS)
    inv_ready = S("inv_ready", NP * UNITS)
    prob_turned = S("prob_turned", NP * UNITS, PROBS)
    prob_t_ready = S("prob_t_ready", NP * UNITS, 1)
    o_summed = S("o_summed", NP * UNITS, 2)
    o_taken = S("o_taken", NP * UNITS, 1)
    o_turned = S("o_turned", NP)
    o_high = S("o_high", KD)
    o_ready = S("o_ready", KD, 1)
    oc_made = S("oc_made", 2)
    branch_done = S("branch_done", 2 * KD)
    out_kv = S("out_kv", 2 * NP, step=16)
    kv_free = S("kv_free", NP, 1)
    out_small = S("out_small", 2, step=16)
    out_h = S("out_h", 1, step=16)
    passed = {e: nc.alloc_semaphore(f"passed_{e}") for e in ("sp", "pe", "act", "dve", "pool")}

    def hold(eng, e):
        eng.sem_inc(passed[e], 1)

    def credits(eng, signals):
        for s in signals:
            eng.sem_inc(s.sem, s.slots)

    block_ctx = nc.Block()
    block = block_ctx.__enter__()

    @block.sync
    def _(sp):
        sp.dma_start(cond[:, :, :], ins["cond"]).then_inc(start_in.sem, 16)
        sp.dma_start(const[:, :, :], ins["const"]).then_inc(start_in.sem, 16)
        sp.dma_start(b_ada[:, :], ins["b_ada"]).then_inc(start_in.sem, 16)
        sp.dma_start(h[:, :, :], ins["x"]).then_inc(start_in.sem, 16)
        with sp.Fori(0, ADA_FIRST // (2 * RING)) as i:
            for s in range(RING):
                sp.wait_ge(first_used.sem, i * RING + s + 1)
                hold(sp, "sp")
                sp.dma_start(ada_ring[:, s, :, :], ins["ada"][bass.ds((i * RING + s) * 2, 2), :, :]
                             .rearrange("t p n -> p t n")).then_inc(first_full[s].sem, 16)

        def load(l, ph, s, i, src, index):
            src = src[bass.ds(index, 1), :, :].rearrange("a p n -> p (a n)")
            sp.wait_ge(lo_ready[s].sem, lo_ready[s].free(l, SPLIT_AT[ph][s] + i))
            hold(sp, "sp")
            sp.dma_start(raw[:, s, 0:WIDTH[ph]], src).then_inc(raw_full[s].sem, 16)

        def load_pairs(l, ph, n, src, first):
            with sp.Fori(0, n) as i:
                for s in (0, 1):
                    load(l, ph, s, i, src, first + i * 2 + s)

        with sp.Fori(0, DEPTH) as l:
            sp.wait_ge(small_used.sem, small_used.free(l, 0))
            hold(sp, "sp")
            for dst, name in ((norm_g, "norm_g"), (b_gate, "b_gate")):
                sp.dma_start(dst[:, :, :].rearrange("p a b -> p (a b)"),
                             ins[name][bass.ds(l, 1), :, :].rearrange("a p n -> p (a n)")
                             ).then_inc(small_in.sem, 16)
            load_pairs(l, "f1a", KF, ins["f1"], (l * 2) * 2 * KF)
            for name, out in (("cache_a_k", "roll_k"), ("cache_a_v", "roll_v")):
                sp.dma_start(outs[out][bass.ds(l, 1), :, :],
                             ins[name][bass.ds(l, 1), DEC:A_WIN, :]).then_inc(roll_out.sem, 16)
            load_pairs(l, "f2a", KD, ins["f2"], (l * 2) * 2 * KD)
            load_pairs(l, "tri", NP + 1, ins["tri"], l * 2 * (NP + 1))
            for s in (0, 1):
                load(l, "uc", s, 0, ins["uc"], l * 2 + s)
            load_pairs(l, "gate", 2 * KD, ins["gate"], l * 4 * KD)
            load_pairs(l, "out", KD // 2, ins["wout"], l * KD)
            load_pairs(l, "f1b", KF, ins["f1"], (l * 2 + 1) * 2 * KF)
            load_pairs(l, "f2b", KD, ins["f2"], (l * 2 + 1) * 2 * KD)

    @block.tensor
    def _(pe):
        credits(pe, chunk_done + ada_used + [prob_turned, o_summed, first_used])
        mm, turn_in = nc.tensor.matmul, nc.tensor.transpose

        def split_tile(out, s, t, hi, lo, first, last):
            wh, wl = w_hi[:, s, t * P:(t + 1) * P], w_lo[:, s, t * P:(t + 1) * P]
            for n, (w, xx) in enumerate(((wh, hi), (wh, lo), (wl, hi))):
                for b in (0, 1):
                    r = mm(out[:, b, :], w, xx[:, b * HALF:(b + 1) * HALF],
                           start=first and n == 0, stop=last and n == 2)
            return r

        def chunk_ready(l, ph, s, i):
            pe.wait_ge(lo_ready[s].sem, lo_ready[s].done(l, SPLIT_AT[ph][s] + i))

        def pair_free(l, ph, p, i):
            pe.wait_ge(acc_free[p].sem, acc_free[p].free(l, GROUP_AT[ph][p] + i))

        def whole_chunk(l, ph, s, p, i, group, hi, lo, gate=None):
            chunk_ready(l, ph, s, i)
            pair_free(l, ph, p, group)
            for t in range(KD):
                if gate is not None:
                    gate(t)
                r = split_tile(pair[p], s, t, hi[:, t, :], lo[:, t, :], t == 0, t == KD - 1)
            r.then_inc(chunk_done[s].sem, 1)

        def x_tile(l, n):
            return lambda t: pe.wait_ge(x_ready.sem, x_ready.done(l, n * KD + t))

        def column_sums(l, n):
            pe.wait_ge(sq_added.sem, sq_added.done(l, n * KD + KD - 1))
            for b in (0, 1):
                r = mm(stat[:, b, :], const[:, ONES, :], acc[:, b * HALF:(b + 1) * HALF], start=True, stop=True)
            r.then_inc(stat_ready.sem, 1)

        def sum_squares(l, n):
            for k in range(KD):
                pe.wait_ge(sq_ready.sem, sq_ready.done(l, n * KD + k))
                for b in (0, 1):
                    r = mm(stat[:, b, :], const[:, ONES, :], sq[:, k % 2, b * HALF:(b + 1) * HALF],
                           start=k == 0, stop=k == KD - 1)
                r.then_inc(sq_added.sem if k < KD - 1 else stat_ready.sem, 1)

        def ada_product(w, n):
            for k in range(KD):
                r = mm(ada_ps[:, bass.ds(n * 2, 2)], w[:, k * P:(k + 1) * P], cond_s[:, k, :],
                       start=k == 0, stop=k == KD - 1)
            return r

        def ada_tile(l, s, i, n):
            pe.wait_ge(ada_full[s].sem, ada_full[s].done(l, i))
            ada_product(ada_w[:, s, :], n).then_inc(ada_used[s].sem, 1)

        def ffn(l, ab, n, ada):
            sum_squares(l, 2 * n)
            x_in = x_tile(l, n)
            if ada:
                pe.wait_ge(ada_read.sem, ada_read.done(l, -1) + 1)
                hold(pe, "pe")
            with pe.Fori(0, KF) as i:
                for p in (0, 1):
                    whole_chunk(l, "f1" + ab, p, p, i, i, x_hi, x_lo, gate=x_in if p == 0 else None)
                    if ada:
                        ada_tile(l, p, i, i * 2 + p)
            with pe.Fori(0, KD // 2) as i:
                for p in (0, 1):
                    pair_free(l, "f2" + ab, p, i)
                    for s in (0, 1):
                        chunk_ready(l, "f2" + ab, s, 2 * i + p)
                        for t in range(KF2):
                            k = s * KF2 + t
                            if p == 0:
                                pe.wait_ge(prod_lo.sem, prod_lo.done(l, (0 if ab == "a" else KF + KD) + k))
                            r = split_tile(pair[p], s, t, hid_hi[:, k, :], hid_lo[:, k, :], k == 0, k == KF - 1)
                        r.then_inc(chunk_done[s].sem, 1)
                        a = 2 * p + s
                        if ada and a < ADA_DOWN:
                            ada_tile(l, s, KF + (i if s else 2 * i + p), ADA_UP * KF + i * ADA_DOWN + a)
            column_sums(l, 2 * n + 1)

        def project(l, T, j0, j1):
            for j in range(j0, j1):
                g, k, s = j // KD, j % KD, j // KT
                p = g % 2
                if j % KT == 0:
                    chunk_ready(l, "tri", s, T)
                if k == 0:
                    pair_free(l, "tri", p, T if p else 2 * T + g // 2)
                r = split_tile(pair[p], s, j % KT, x_hi[:, k, :], x_lo[:, k, :], k == 0, k == KD - 1)
                if j in (KD - 1, 2 * KD - 1):
                    r.then_inc(tri_done.sem, 1)
                if j % KT == KT - 1:
                    r.then_inc(chunk_done[s].sem, 1)

        def project_u(l, j0, j1):
            for j in range(j0, min(j1, 2 * KD)):
                s, k = j // KD, j % KD
                if k == 0:
                    chunk_ready(l, "uc", s, 0)
                    pair_free(l, "uc", s, 0)
                r = split_tile(pair[s], s, k, x_hi[:, k, :], x_lo[:, k, :], k == 0, k == KD - 1)
                if k == KD - 1:
                    r.then_inc(chunk_done[s].sem, 1)

        def before_pairs(l):
            x_in = x_tile(l, 1)
            for k in range(KD):
                x_in(k)
                project(l, 0, k, k + 1)
            project(l, 0, KD, TRI)
            project(l, 1, 0, 4)
            pe.wait_ge(nxt_full.sem, nxt_full.done(l, 2))
            hold(pe, "pe")
            for t in range(NT):
                m = P if t < 4 else DEC
                r = turn_in(ps[0:m, 4, t * 8:t * 8 + 8], nxt[0:8, 2, t * P:t * P + m], const[0:8, IDENT, 0:8])
            r.then_inc(logits_turned.sem, 1)
            for t in range(NT):
                m = P if t < 4 else DEC
                for c in (0, 1):
                    at = (t % 2) * 256 + c * P
                    r = turn_in(ps[0:m, 5 + t // 2, at:at + P], nxt[:, c, t * P:t * P + m], const[:, IDENT, :])
            r.then_inc(vc_turned.sem, 1)
            project(l, 1, 4, KT)
            pe.wait_ge(f_sums_in.sem, f_sums_in.done(l, 0))
            for t in range(4):
                o = ps[:, 4, 64 + t * 8:72 + t * 8]
                mm(o, const[:, TRI_LE, :], logf[:, t, :], start=True, stop=t == 0)
                if t:
                    mm(o, const[:, ONES, :], earlier_f[:, t, :], start=False, stop=True)
            mm(ps[0:DEC, 4, 96:104], const[0:DEC, TRI_LE, 0:DEC], logf[0:DEC, 4, :], start=True, stop=True)
            mm(ps[0:B_HEADS, 4, 128:128 + DEC], logf[0:DEC, 4, :], const[0:DEC, TRI_LE, 0:DEC],
               start=True, stop=True)
            pe.wait_ge(vc_copied.sem, vc_copied.done(l, 0))
            for t in range(4):
                o = ps[0:B_HEADS, 7, t * P:(t + 1) * P]
                mm(o, logf[:, t, :], const[:, TRI_LE, :], start=True, stop=t == 0)
                if t:
                    mm(o, earlier_f[:, t, :], const[:, ONES, :], start=False, stop=True)
            for t in range(8):
                o = ps[0:B_HEADS, 5 + t // 4, (t % 4) * P:(t % 4 + 1) * P]
                r = mm(o, cache_f[:, t, :], const[:, TRI_GT, :], start=True, stop=t == 7)
                if t < 7:
                    r = mm(o, later_f[:, t, :], const[:, ONES, :], start=False, stop=True)
            r.then_inc(f_sums.sem, 1)
            project(l, 1, KT, 18)
            pe.wait_ge(vc_ready.sem, vc_ready.done(l, 0))
            pe.wait_ge(f_rows_ready.sem, f_rows_ready.done(l, 0))
            for T in (0, 1):
                for hh in (0, 1):
                    g, rows = 2 * T + hh, slice(HD * hh, HD * hh + HD)
                    for n in range(4):
                        mm(ps[rows, 5 + T, n * P:(n + 1) * P], v_tok_c[:, n, g * HD:(g + 1) * HD],
                           w_mix[:, g, :], start=True, stop=True)
                    r = mm(ps[rows, 7, T * DEC:(T + 1) * DEC], v_tok_c[0:DEC, 4, g * HD:(g + 1) * HD],
                           w_mix[0:DEC, g, 0:DEC], start=True, stop=True)
            r.then_inc(mixed.sem, 1)
            project(l, 1, 18, TRI)

        def stage(l, st, cached, seg0, work):
            base = st * UNITS

            def scores(u):
                hh, i, m, nk, _, segs = unit_shape(u, cached)
                rows, s0 = slice(hh * HD, hh * HD + HD), first_segment(u, cached)
                q = q_st[rows, i * P:i * P + m]
                for e, (c0, c1) in enumerate(segs):
                    pe.wait_ge(scores_taken.sem, scores_taken.free(l, seg0 + s0 + e))
                    if u == 0 and e == 0:
                        pe.wait_ge(ck_in.sem, ck_in.done(l, st))
                    if i == 4:
                        hold(pe, "pe")
                    if i == 4 and c0 >= cached:
                        k = k_st[rows, SEQ:TOK]
                    else:
                        k = cache_k[rows, c0:c1] if i == 4 else k_st[rows, c0:c1]
                    mm(score[(s0 + e) % 2][0:m, 0:c1 - c0], q, k, start=True, stop=True
                       ).then_inc(scores_ready.sem, 1)

            def turn(u):
                hh, i, m, nk, nb, _ = unit_shape(u, cached)
                n = base + u
                pe.wait_ge(exp_ready.sem, exp_ready.done(l, n))
                pe.wait_ge(prob_t_ready.sem, prob_t_ready.free(l, n))
                if nb > 8:
                    pe.wait_ge(o_taken.sem, o_taken.free(l, n))
                if i == 4:
                    hold(pe, "pe")
                for b in range(nb):
                    w = min(P, nk - b * P)
                    out = turned[0:w, b * m:(b + 1) * m] if b < 8 else att_out[0:w, 256:256 + m]
                    r = turn_in(out, prob[0:m, u % PROBS, b * P:b * P + w], const[0:m, IDENT, 0:m])
                r.then_inc(prob_turned.sem, 1)

            def weigh(u):
                hh, i, m, nk, nb, _ = unit_shape(u, cached)
                n, cols = base + u, slice(hh * HD, hh * HD + HD)
                pe.wait_ge(prob_t_ready.sem, prob_t_ready.done(l, n))
                pe.wait_ge(o_taken.sem, o_taken.free(l, n))
                if u == 0:
                    pe.wait_ge(cv_in.sem, cv_in.done(l, st))
                if i == 4:
                    hold(pe, "pe")
                for b in range(nb):
                    w = min(P, nk - b * P)
                    if i < 4:
                        v = v_tok[:, b, cols]
                    else:
                        v = cache_v[:, b, cols] if b < nb - 1 else v_tok[0:w, 4, cols]
                    r = mm(att_out[0:m, 0:HD], prob_t[0:w, u % 2, b * m:(b + 1) * m], v,
                           start=b == 0, stop=b == nb - 1)
                r.then_inc(o_summed.sem, 1)

            pe.wait_ge(v_staged.sem, v_staged.done(l, st))
            for t in range(NT):
                m = P if t < 4 else DEC
                out = turned[:, t * P:(t + 1) * P] if t < 4 else att_out[0:m, 0:P]
                r = turn_in(out, v_st[:, t * P:t * P + m], const[:, IDENT, :])
            r.then_inc(v_turned.sem, 1)
            work(0, 2)
            pe.wait_ge(q_staged.sem, q_staged.done(l, st))
            pe.wait_ge(k_staged.sem, k_staged.done(l, st))
            pe.wait_ge(o_ready.sem, o_ready.free(l, st))
            scores(0)
            work(2, 3)
            scores(1)
            work(3, 4)
            pe.wait_ge(v_ready.sem, v_ready.done(l, st))
            for u in range(UNITS):
                if u + 2 < UNITS:
                    scores(u + 2)
                work(4 + 2 * u, 5 + 2 * u)
                turn(u)
                work(5 + 2 * u, 6 + 2 * u)
                weigh(u)
            pe.wait_ge(o_taken.sem, o_taken.done(l, base + UNITS - 1))
            hold(pe, "pe")
            for t in range(NT):
                m = P if t < 4 else DEC
                out = score[0][:, t * P:(t + 1) * P] if t < 4 else score[1][:, 0:m]
                r = turn_in(out, o_tok[0:m, t, :], const[0:m, IDENT, 0:m])
            r.then_inc(o_turned.sem, 1)

        def merge(l):
            with pe.Fori(0, KD) as m:
                whole_chunk(l, "gate", 0, 0, 2 * m, 3 * m, x_hi, x_lo)
                whole_chunk(l, "gate", 1, 1, 2 * m, 3 * m, x_hi, x_lo)
                whole_chunk(l, "gate", 0, 0, 2 * m + 1, 3 * m + 1, x_hi, x_lo)
                chunk_ready(l, "gate", 1, 2 * m + 1)
                for t0, t1, p, group in ((0, 2, 1, 1), (2, 6, 0, 2), (6, 8, 1, 2)):
                    pair_free(l, "gate", p, 3 * m + group)
                    for t in range(t0, t1):
                        pe.wait_ge(o_ready.sem, o_ready.done(l, KD - 1))
                        r = split_tile(pair[p], 1, t, o_hi[:, t, :], o_lo[:, t, :], t == t0, t == t1 - 1)
                    r.then_inc(branch_done.sem if t1 < KD else chunk_done[1].sem, 1)

        pe.wait_ge(start_in.sem, start_in.done(0, 3))
        pe.wait_ge(cond_ready.sem, cond_ready.done(0, 0))
        with pe.Fori(0, ADA_FIRST // (2 * RING)) as i:
            for s in range(RING):
                pe.wait_ge(first_full[s].sem, (i + 1) * 16)
                for t in (0, 1):
                    r = ada_product(ada_ring[:, s, t, :], (i * RING + s) * 2 + t)
                r.then_inc(first_used.sem, 1)
        with pe.Fori(0, DEPTH) as l:
            ffn(l, "a", 0, True)
            sum_squares(l, 2)
            before_pairs(l)
            pe.wait_ge(mix_ready.sem, mix_ready.done(l, 0))
            hold(pe, "pe")
            with pe.Fori(0, B_PAIRS) as b:
                stage(l, b, PAST, b * SEGS_B, lambda j0, j1: project(l, b + 2, j0, j1))
            seg0 = B_PAIRS * SEGS_B
            stage(l, B_PAIRS, A_WIN, seg0, lambda j0, j1: project(l, NP, j0, j1))
            stage(l, B_PAIRS + 1, A_WIN, seg0 + SEGS_A, lambda j0, j1: project_u(l, j0, j1))
            merge(l)
            with pe.Fori(0, KD // 2) as i:
                for p in (0, 1):
                    whole_chunk(l, "out", p, p, i, i, m_hi, m_lo,
                                gate=(lambda t: pe.wait_ge(prod_lo.sem, prod_lo.done(l, KF + t))) if p == 0 else None)
            column_sums(l, 3)
            ffn(l, "b", 2, False)

    @block.scalar
    def _(act):
        credits(act, [prob_t_ready, o_taken, acc_free[0]])
        A, copy = nc.scalar.activation, nc.scalar.copy

        def split_hi(l, ph, s, i):
            act.wait_ge(raw_full[s].sem, raw_full[s].done(l, SPLIT_AT[ph][s] + i))
            act.wait_ge(chunk_done[s].sem, chunk_done[s].free(l, SPLIT_AT[ph][s] + i))
            copy(w_hi[:, s, 0:WIDTH[ph]], raw[:, s, 0:WIDTH[ph]]).then_inc(hi_ready[s].sem, 1)

        def chunk_over(l, ph, s, i):
            act.wait_ge(chunk_done[s].sem, chunk_done[s].done(l, SPLIT_AT[ph][s] + i))

        def pairs(n, body, following):
            with act.Fori(0, n - 1) as i:
                body(i, None)
            body(n - 1, following)

        def ffn_up(l, ab, following):
            ph, at = "f1" + ab, (0 if ab == "a" else KF + KD)
            hold(act, "act")
            act.preload_act_table(ACT.Silu)

            def body(i, nxt_split):
                split_hi(l, ph, 1, i)
                chunk_over(l, ph, 0, i)
                act.wait_ge(acc_free[1].sem, acc_free[1].free(l, GROUP_AT[ph][1] + i))
                A(two(sil[:, :]), pair[0], ACT.Silu).then_inc(acc_free[0].sem, 1)
                nxt_split() if nxt_split else split_hi(l, ph, 0, i + 1)
                act.wait_ge(acc_free[1].sem, acc_free[1].done(l, GROUP_AT[ph][1] + i))
                copy(tile(hid_hi, i), hid[:, :]).then_inc(prod_hi.sem, 1)
            pairs(KF, body, following)

        def keep_and_square(l, ph, n, p, s, i, m):
            chunk_over(l, ph, s, i)
            act.wait_ge(sq_added.sem, sq_added.free(l, n * KD + m))
            A(two(sq[:, p, :]), pair[p], ACT.Square).then_inc(sq_ready.sem, 1)
            copy(two(tile(y, m)), pair[p]).then_inc(acc_free[p].sem, 1)

        def ffn_down(l, ab, n, following):
            ph = "f2" + ab

            def body(i, nxt_split):
                for p in (0, 1):
                    split_hi(l, ph, 1, 2 * i + p)
                    if p == 0 or not nxt_split:
                        split_hi(l, ph, 0, 2 * i + p + 1)
                    else:
                        nxt_split()
                    keep_and_square(l, ph, n, p, 1, 2 * i + p, 2 * i + p)
            pairs(KD // 2, body, following)

        def square_h(l, n, h_tile):
            for k in range(KD):
                h_tile(k)
                act.wait_ge(sq_added.sem, sq_added.free(l, n * KD + k))
                A(sq[:, k % 2, :], h[:, k, :], ACT.Square).then_inc(sq_ready.sem, 1)

        def estimate(l, n):
            act.preload_act_table_set("natural_log_exp_and_others")
            act.wait_ge(ms_ready.sem, ms_ready.done(l, n))
            A(rms[:, 1, :], rms[:, 0, :], ACT.Ln)
            act.drain()
            A(rms[:, 1, :], rms[:, 1, :], ACT.Exp, scale=-0.5).then_inc(est_ready.sem, 1)

        def make_x(l, n):
            for k in range(KD):
                act.wait_ge(t_ready.sem, t_ready.done(l, n * KD + k))
                act.wait_ge(x_ready.sem, x_ready.free(l, n * KD + k))
                for g, cols in ((0, slice(0, SEQ)), (1, slice(SEQ, TOK))):
                    A(nx[:, k % 2, cols], nt[:, k % 2, cols], ACT.Identity,
                      bias=mods[:, 3 * n, k, g:g + 1], scale=pre_scale[:, n, k, g:g + 1])
                act.drain()
                copy(x_hi[:, k, :], nx[:, k % 2, :]).then_inc(nx_ready.sem, 1)

        def before_pairs(l):
            act.wait_ge(tri_done.sem, tri_done.done(l, 0))
            copy(two(nxt[:, 0, :]), pair[0]).then_inc(acc_free[0].sem, 1)
            split_hi(l, "tri", 0, 1)
            chunk_over(l, "tri", 1, 0)
            copy(two(nxt[:, 2, :]), pair[0]).then_inc(acc_free[0].sem, 1)
            act.drain()
            act.sem_inc(nxt_full.sem, 2)
            split_hi(l, "tri", 1, 1)
            act.preload_act_table(ACT.Exp)
            act.wait_ge(f_neg.sem, f_neg.done(l, 0))
            A(fx[:, 2, :, :], fx[:, 1, :, :], ACT.Exp).then_inc(f_exp.sem, 1)
            act.wait_ge(vc_turned.sem, vc_turned.done(l, 0))
            for t in range(NT):
                m = P if t < 4 else DEC
                src = ps[0:m, 5 + t // 2, (t % 2) * 256:(t % 2) * 256 + 256]
                A(v_tok_c[0:m, t, :], src, ACT.Square, accum_out=c_stat[0:m, 0, t:t + 1])
            act.drain()
            for t in range(NT):
                m = P if t < 4 else DEC
                src = ps[0:m, 5 + t // 2, (t % 2) * 256:(t % 2) * 256 + 256]
                copy(v_tok_c[0:m, t, :], src)
            act.drain()
            A(c_stat[:, 1, :], c_stat[:, 0, :], ACT.Sqrt, scale=1.0 / 256, bias=eps_t[:, 0:1]
              ).then_inc(vc_copied.sem, 1)
            take_q(l, 1)
            split_hi(l, "tri", 0, 2)
            act.wait_ge(f_sums.sem, f_sums.done(l, 0))
            nc.scalar.mul(f_rows[:, 0:SEQ], ps[0:B_HEADS, 7, :], -1.0)
            copy(f_rows[:, SEQ:SEQ + PAST].rearrange("p (b n) -> p b n", b=2), ps[0:B_HEADS, 5:7, :])
            nc.scalar.mul(f_rows[:, SEQ + PAST:SEQ + SC], ps[0:B_HEADS, 4, 128:128 + DEC], -1.0)
            copy(f_query[:, 0:4, :].rearrange("p t h -> p (t h)"), ps[:, 4, 64:96])
            copy(f_query[0:DEC, 4, :], ps[0:DEC, 4, 96:104]).then_inc(f_rows_ready.sem, 1)
            take_v(l, 1)
            act.preload_act_table(ACT.Exp)

        def take_q(l, T):
            act.wait_ge(tri_done.sem, tri_done.done(l, 2 * T))
            nc.scalar.mul(two(nxt[:, 0, :]), pair[0], HD ** -0.5).then_inc(acc_free[0].sem, 1)

        def take_v(l, T):
            chunk_over(l, "tri", 1, T)
            copy(two(nxt[:, 2, :]), pair[0]).then_inc(acc_free[0].sem, 1)
            act.drain()
            act.sem_inc(nxt_full.sem, 2)

        def stage(l, st, cached, o_tile, second, third, last):
            base = st * UNITS
            act.wait_ge(nxt_full.sem, nxt_full.done(l, 3 * (st + 1) + 2))
            act.wait_ge(kv_free.sem, kv_free.free(l, st))
            hold(act, "act")
            copy(v_st[:, :], nxt[:, 2, :]).then_inc(v_staged.sem, 1)
            copy(q_st[:, :], nxt[:, 0, :]).then_inc(q_staged.sem, 1)
            second()
            act.wait_ge(v_turned.sem, v_turned.done(l, st))
            copy(v_tok[:, 0:4, :].rearrange("p t n -> p (t n)"), turned)
            copy(v_tok[0:DEC, 4, :], att_out[0:DEC, 0:P]).then_inc(v_ready.sem, 1)

            def expo(u):
                hh, i, m, nk, nb, _ = unit_shape(u, cached)
                p = u % PROBS
                act.wait_ge(shift_ready.sem, shift_ready.done(l, base + u))
                A(prob[0:m, p, 0:nk], prob[0:m, p, 0:nk], ACT.Exp, bias=row[0:m, 1, p:p + 1],
                  accum_out=row[0:m, 2, p:p + 1]).then_inc(exp_ready.sem, 1)

            def take_turned(u):
                hh, i, m, nk, nb, _ = unit_shape(u, cached)
                n = base + u
                act.wait_ge(prob_turned.sem, prob_turned.done(l, n))
                act.wait_ge(o_summed.sem, o_summed.free(l, n))
                part = nk % P
                full = nb - 1 if part else nb
                r = copy(prob_t[:, u % 2, 0:full * m], turned[:, 0:full * m])
                if part:
                    src = turned[0:part, full * m:nb * m] if full < 8 else att_out[0:part, 256:256 + m]
                    r = copy(prob_t[0:part, u % 2, full * m:nb * m], src)
                r.then_inc(prob_t_ready.sem, 1)

            def take_o(u):
                hh, i, m, nk, nb, _ = unit_shape(u, cached)
                n = base + u
                act.wait_ge(inv_ready.sem, inv_ready.done(l, n))
                act.wait_ge(o_summed.sem, o_summed.done(l, n))
                A(o_tok[0:m, i, hh * HD:hh * HD + HD], att_out[0:m, 0:HD], ACT.Copy,
                  scale=row[0:m, 3, u % PROBS:u % PROBS + 1]).then_inc(o_taken.sem, 1)

            expo(0)
            expo(1)
            for u in range(UNITS):
                take_turned(u)
                if u + 2 < UNITS:
                    expo(u + 2)
                take_o(u)
                if u == 2 and last:
                    take_q(l, st + 2)
                if u == 4:
                    third()
            if last:
                take_v(l, st + 2)
            act.wait_ge(o_turned.sem, o_turned.done(l, st))
            hold(act, "act")
            copy(o_hi[:, bass.ds(o_tile, 1), 0:SEQ].rearrange("p a n -> p (a n)"), score[0])
            copy(o_hi[:, bass.ds(o_tile, 1), SEQ:TOK].rearrange("p a n -> p (a n)"), score[1][:, 0:DEC]
                 ).then_inc(o_high.sem, 1)

        def merge(l):
            act.preload_act_table(ACT.Sigmoid)

            def body(m, nxt_split):
                g0, g1 = GROUP_AT["gate"]
                for br, (s, i, used, group) in enumerate(((0, 2 * m, 1, g1 + 3 * m - 2), (1, 2 * m, 0, g0 + 3 * m - 1),
                                                          (0, 2 * m + 1, 1, g1 + 3 * m - 1))):
                    if br == 0:
                        split_hi(l, "gate", 1, 2 * m)
                    elif br == 1:
                        split_hi(l, "gate", 0, 2 * m + 1)
                    else:
                        split_hi(l, "gate", 1, 2 * m + 1)
                    chunk_over(l, "gate", s, i)
                    act.wait_ge(acc_free[used].sem, acc_free[used].done(l, group))
                    A(two(sig[:, br, :]), pair[s], ACT.Sigmoid, bias=b_gate[:, br, bass.ds(m, 1)]
                      ).then_inc(acc_free[s].sem, 1)
                nxt_split() if nxt_split else split_hi(l, "gate", 0, 2 * m + 2)
                act.wait_ge(merged.sem, merged.done(l, m))
                copy(tile(m_hi, m), msum[:, :]).then_inc(prod_hi.sem, 1)
            pairs(KD, body, lambda: split_hi(l, "out", 0, 0))

        act.wait_ge(start_in.sem, start_in.done(0, 3))
        A(cond_s[:, :, :], cond[:, :, :], ACT.Silu).then_inc(cond_ready.sem, 1)
        act.wait_ge(eps_ready.sem, eps_ready.done(0, 0))
        with act.Fori(0, DEPTH) as l:
            square_h(l, 0, lambda k: act.wait_ge(h_ready.sem, l * h_ready.per_layer + k + 1))
            split_hi(l, "f1a", 0, 0)
            estimate(l, 0)
            make_x(l, 0)
            ffn_up(l, "a", lambda: split_hi(l, "f2a", 0, 0))
            ffn_down(l, "a", 1, lambda: split_hi(l, "tri", 0, 0))
            split_hi(l, "tri", 1, 0)
            estimate(l, 1)
            square_h(l, 2, lambda k: act.wait_ge(h_ready.sem, h_ready.done(l, k) + KD))
            estimate(l, 2)
            make_x(l, 1)
            before_pairs(l)
            with act.Fori(0, B_PAIRS) as b:
                stage(l, b, PAST, b + A_PAIRS, lambda: split_hi(l, "tri", 1, b + 2),
                      lambda: split_hi(l, "tri", 0, b + 3), True)
            stage(l, B_PAIRS, A_WIN, 0, lambda: split_hi(l, "tri", 1, NP), lambda: split_hi(l, "uc", 0, 0), True)
            stage(l, B_PAIRS + 1, A_WIN, 1, lambda: split_hi(l, "uc", 1, 0), lambda: split_hi(l, "gate", 0, 0), False)
            for c in (0, 1):
                act.wait_ge(oc_made.sem, oc_made.done(l, c))
                copy(o_hi[:, NP + c, :], nxt[:, c, :]).then_inc(o_high.sem, 1)
            act.wait_ge(kv_free.sem, kv_free.done(l, NP - 1))
            hold(act, "act")
            merge(l)

            def out_pair(i, nxt_split):
                split_hi(l, "out", 1, i)
                keep_and_square(l, "out", 3, 0, 0, i, 2 * i)
                nxt_split() if nxt_split else split_hi(l, "out", 0, i + 1)
                keep_and_square(l, "out", 3, 1, 1, i, 2 * i + 1)
            pairs(KD // 2, out_pair, lambda: split_hi(l, "f1b", 0, 0))
            estimate(l, 3)
            square_h(l, 4, lambda k: act.wait_ge(h_ready.sem, h_ready.done(l, KD + k) + KD))
            estimate(l, 4)
            make_x(l, 2)
            ffn_up(l, "b", lambda: split_hi(l, "f2b", 0, 0))
            ffn_down(l, "b", 5, lambda: None)
            estimate(l, 5)

    @block.vector
    def _(dve):
        credits(dve, lo_ready + [acc_free[1], prod_lo, sq_added, x_ready, scores_taken, ada_read, small_used, o_ready])
        V = nc.vector

        def split_lo(l, ph, s, i):
            w = WIDTH[ph]
            dve.wait_ge(hi_ready[s].sem, hi_ready[s].done(l, SPLIT_AT[ph][s] + i))
            V.tensor_tensor(w_lo[:, s, 0:w], raw[:, s, 0:w], w_hi[:, s, 0:w], ALU.subtract
                            ).then_inc(lo_ready[s].sem, 1)

        def pairs(n, body, following):
            with dve.Fori(0, n - 1) as i:
                body(i, None)
            body(n - 1, following)

        def ffn_up(l, ab, following):
            ph, at = "f1" + ab, (0 if ab == "a" else KF + KD)

            def body(i, nxt_split):
                split_lo(l, ph, 1, i)
                nxt_split() if nxt_split else split_lo(l, ph, 0, i + 1)
                dve.wait_ge(acc_free[0].sem, acc_free[0].done(l, GROUP_AT[ph][0] + i))
                dve.wait_ge(chunk_done[1].sem, chunk_done[1].done(l, SPLIT_AT[ph][1] + i))
                dve.wait_ge(prod_lo.sem, prod_lo.free(l, at + i))
                V.tensor_tensor(two(hid[:, :]), two(sil[:, :]), pair[1], ALU.mult).then_inc(acc_free[1].sem, 1)
                dve.wait_ge(prod_hi.sem, prod_hi.done(l, at + i))
                V.tensor_tensor(tile(hid_lo, i), hid[:, :], tile(hid_hi, i), ALU.subtract
                                ).then_inc(prod_lo.sem, 1)
            pairs(KF, body, following)

        def add_squares(l, n, p, m):
            dve.wait_ge(sq_ready.sem, sq_ready.done(l, n * KD + m))
            dve.wait_ge(sq_added.sem, sq_added.done(l, n * KD + m - 1))
            V.tensor_tensor(acc[:, :], acc[:, :], sq[:, p, :], ALU.add).then_inc(sq_added.sem, 1)

        def clear_acc():
            V.memset(acc[:, :], 0.0)
            dve.drain()

        def ffn_down(l, ab, n, following):
            ph = "f2" + ab

            def body(i, nxt_split):
                for p in (0, 1):
                    split_lo(l, ph, 1, 2 * i + p)
                    if p == 0 or not nxt_split:
                        split_lo(l, ph, 0, 2 * i + p + 1)
                    else:
                        nxt_split()
                    add_squares(l, n, p, 2 * i + p)
            clear_acc()
            pairs(KD // 2, body, following)

        def inverse_rms(l, n):
            dve.wait_ge(stat_ready.sem, stat_ready.done(l, n))
            if n % 2 == 0:
                dve.sem_inc(sq_added.sem, 1)
            V.tensor_scalar(two(rms[:, 0, :]), stat, 1.0 / D_MODEL, EPS, ALU.mult, ALU.add
                            ).then_inc(ms_ready.sem, 1)
            dve.wait_ge(est_ready.sem, est_ready.done(l, n))
            V.scalar_tensor_tensor(out=rms[:, 2, :], in0=rms[:, 0, :], scalar=-0.5, in1=rms[:, 1, :],
                                   op0=ALU.mult, op1=ALU.mult)
            dve.drain()
            V.tensor_tensor(rms[:, 2, :], rms[:, 2, :], rms[:, 1, :], ALU.mult)
            dve.drain()
            V.scalar_tensor_tensor(out=rms[:, 3, :], in0=rms[:, 2, :], scalar=1.5, in1=rms[:, 1, :],
                                   op0=ALU.add, op1=ALU.mult)
            dve.drain()

        def x_low(l, n, k):
            dve.wait_ge(nx_ready.sem, nx_ready.done(l, n * KD + k))
            V.tensor_tensor(x_lo[:, k, :], nx[:, k % 2, :], x_hi[:, k, :], ALU.subtract
                            ).then_inc(x_ready.sem, 1)

        def make_x(l, n):
            for k in range(KD):
                V.tensor_tensor(nt[:, k % 2, :], h[:, k, :], rms[:, 3, :], ALU.mult).then_inc(t_ready.sem, 1)
                if k:
                    x_low(l, n, k - 1)
            x_low(l, n, KD - 1)

        def residual(l, n):
            for k in range(KD):
                V.tensor_tensor(nt[:, k % 2, :], y[:, k, :], rms[:, 3, :], ALU.mult)
                dve.drain()
                for g, cols in ((0, slice(0, SEQ)), (1, slice(SEQ, TOK))):
                    r = V.scalar_tensor_tensor(out=h[:, k, cols], in0=nt[:, k % 2, cols],
                                               scalar=post_gate[:, n, k, g:g + 1], in1=h[:, k, cols],
                                               op0=ALU.mult, op1=ALU.add)
                r.then_inc(h_ready.sem, 1)

        def take_ada(first, n):
            bias = b_ada[:, bass.ds(first, n)].rearrange("p (n a) -> p n a", a=1).to_broadcast((P, n, 2))
            V.tensor_tensor(ada_all[:, bass.ds(first, n), :], ada_ps[:, 0:2 * n].rearrange("p (n g) -> p n g", g=2),
                            bias, ALU.add)
            dve.drain()
            dve.sem_inc(ada_read.sem, 1)

        def fold_mods(l, parts):
            for j0, j1 in ((0, 2),) if parts == "first" else ((2, N_MOD),):
                V.tensor_copy(mods[:, j0:j1, :, :].rearrange("p m k g -> p (m k g)"),
                              ada_all[:, bass.ds(l * N_ADA + j0 * KD, (j1 - j0) * KD), :]
                              .rearrange("p n g -> p (n g)"))
            dve.drain()
            for n in ([0] if parts == "first" else [1, 2]):
                for g in (0, 1):
                    V.scalar_tensor_tensor(out=pre_scale[:, n, :, g], in0=mods[:, 3 * n + 1, :, g], scalar=1.0,
                                           in1=norm_g[:, 2 * n, :], op0=ALU.add, op1=ALU.mult)
            if parts != "first":
                for n in range(3):
                    for g in (0, 1):
                        V.scalar_tensor_tensor(out=post_gate[:, n, :, g], in0=mods[:, 3 * n + 2, :, g],
                                               scalar=1.0 if n == 1 else 0.5,
                                               in1=norm_g[:, 2 * n + 1, :], op0=ALU.mult, op1=ALU.mult)
            dve.drain()

        def forget(l):
            dve.wait_ge(mix_in.sem, mix_in.done(l, 4))
            V.memset(fx[:, 0, :, :], 0.0)
            dve.drain()
            dve.wait_ge(logits_turned.sem, logits_turned.done(l, 0))
            V.tensor_copy(fx[:, 0, 0:4, :].rearrange("p t h -> p (t h)"), ps[:, 4, 0:32])
            V.tensor_copy(fx[0:DEC, 0, 4, :], ps[0:DEC, 4, 32:40])
            dve.drain()
            bias = b_forget[:, :].rearrange("p (a h) -> p a h", a=1).to_broadcast((P, NT, B_HEADS))
            x, na, e, z, z2, pl = (fx[:, k, :, :] for k in range(6))
            V.tensor_tensor(x, x, bias, ALU.add)
            dve.drain()
            V.tensor_scalar(z, x, -1.0, None, ALU.mult)
            dve.drain()
            V.tensor_tensor(na, x, z, ALU.min).then_inc(f_neg.sem, 1)
            dve.wait_ge(f_exp.sem, f_exp.done(l, 0))
            V.tensor_scalar(z2, e, 2.0, None, ALU.add)
            dve.drain()
            V.reciprocal(z2, z2)
            dve.drain()
            V.tensor_tensor(z, e, z2, ALU.mult)
            dve.drain()
            V.tensor_tensor(z2, z, z, ALU.mult)
            dve.drain()
            V.tensor_scalar(pl, z2, 1.0 / 17, None, ALU.mult)
            for odd in (15, 13, 11, 9, 7, 5, 3):
                dve.drain()
                V.scalar_tensor_tensor(out=pl, in0=pl, scalar=1.0 / odd, in1=z2, op0=ALU.add, op1=ALU.mult)
            dve.drain()
            V.scalar_tensor_tensor(out=pl, in0=pl, scalar=1.0, in1=z, op0=ALU.add, op1=ALU.mult)
            V.tensor_scalar(x, x, 0.0, None, ALU.min)
            dve.drain()
            V.scalar_tensor_tensor(out=logf[:, :, :], in0=pl, scalar=-2.0, in1=x, op0=ALU.mult, op1=ALU.add)
            dve.drain()
            V.tensor_copy(earlier_f[:, 1, :], logf[:, 0, :])
            V.tensor_copy(later_f[:, 6, :], cache_f[:, 7, :])
            for t in range(2, 4):
                dve.drain()
                V.tensor_tensor(earlier_f[:, t, :], earlier_f[:, t - 1, :], logf[:, t - 1, :], ALU.add)
            for t in range(5, -1, -1):
                dve.drain()
                r = V.tensor_tensor(later_f[:, t, :], later_f[:, t + 1, :], cache_f[:, t + 1, :], ALU.add)
            r.then_inc(f_sums_in.sem, 1)

        def before_pairs(l):
            dve.wait_ge(tri_done.sem, tri_done.done(l, 1))
            V.tensor_copy(two(nxt[:, 1, :]), pair[1]).then_inc(acc_free[1].sem, 1)
            dve.drain()
            dve.sem_inc(nxt_full.sem, 1)
            split_lo(l, "tri", 0, 1)
            split_lo(l, "tri", 1, 1)
            forget(l)
            mask = const[:, TRI_LE:TRI_LE + 1, :].to_broadcast((P, C_GROUPS, P))
            V.tensor_tensor(w_mix[:, :, :], w_mix[:, :, :], mask, ALU.mult)
            dve.wait_ge(vc_copied.sem, vc_copied.done(l, 0))
            V.reciprocal(c_stat[:, 2, :], c_stat[:, 1, :])
            dve.drain()
            for t in range(NT):
                m = P if t < 4 else DEC
                r = V.scalar_tensor_tensor(out=v_tok_c[0:m, t, :], in0=v_tok_c[0:m, t, :],
                                           scalar=c_stat[0:m, 2, t:t + 1], in1=c_gain[0:m, :],
                                           op0=ALU.mult, op1=ALU.mult)
            r.then_inc(vc_ready.sem, 1)
            split_lo(l, "tri", 0, 2)
            take_k(l, 1)
            dve.wait_ge(mixed.sem, mixed.done(l, 0))
            for T in (0, 1):
                V.tensor_tensor(c_mix[:, T, 0:SEQ].rearrange("p (t n) -> p t n", t=4),
                                ps[:, 5 + T, :].rearrange("p (t n) -> p t n", t=4),
                                c_bias[:, T:T + 1, :].to_broadcast((P, 4, P)), ALU.add)
                r = V.tensor_tensor(c_mix[:, T, SEQ:TOK], ps[:, 7, T * DEC:(T + 1) * DEC], c_bias[:, T, 0:DEC],
                                    ALU.add)
            r.then_inc(mix_ready.sem, 1)

        def take_k(l, T):
            dve.wait_ge(tri_done.sem, tri_done.done(l, 2 * T + 1))
            V.tensor_copy(two(nxt[:, 1, :]), pair[1]).then_inc(acc_free[1].sem, 1)
            dve.drain()
            dve.sem_inc(nxt_full.sem, 1)

        def stage(l, st, cached, seg0, o_tile, second, third, last):
            base = st * UNITS
            is_b = cached == PAST
            dve.wait_ge(o_summed.sem, o_summed.done(l, base - 1))
            dve.wait_ge(kv_free.sem, kv_free.free(l, st))
            dve.wait_ge(nxt_full.sem, nxt_full.done(l, 3 * (st + 1) + 2))
            hold(dve, "dve")
            V.tensor_copy(k_st[:, :], nxt[:, 1, :]).then_inc(k_staged.sem, 1)
            second()

            def logits(u):
                hh, i, m, nk, nb, segs = unit_shape(u, cached)
                n, p, s0 = base + u, u % PROBS, first_segment(u, cached)
                dve.wait_ge(prob_turned.sem, prob_turned.done(l, base + last_user(u)))
                if is_b and u in (0, 2):
                    sem = decay_p_in if u else decay_s_in
                    dve.wait_ge(sem.sem, sem.done(l, st))
                if not is_b and u == 0:
                    dve.wait_ge(strip_in.sem, strip_in.done(l, st - B_PAIRS))
                for e, (c0, c1) in enumerate(segs):
                    out, bank = prob[0:m, p, c0:c1], score[(s0 + e) % 2][0:m, 0:c1 - c0]
                    dve.wait_ge(scores_ready.sem, scores_ready.done(l, seg0 + s0 + e))
                    if is_b:
                        d = (decay_p if i < 4 else decay_s)[0:m, hh, c0:c1]
                        V.scalar_tensor_tensor(out=out, in0=d, scalar=f_query[0:m, i, bass.ds(st * 2 + hh, 1)],
                                               in1=bank, op0=ALU.add, op1=ALU.add).then_inc(scores_taken.sem, 1)
                    else:
                        c = c0 + (512 - P * i if i < 4 else 0)
                        V.tensor_tensor(out, bank, strip[0:m, hh, c:c + c1 - c0], ALU.add
                                        ).then_inc(scores_taken.sem, 1)
                dve.drain()
                if is_b:
                    diag = prob[0:m, p, nk - m:nk]
                    V.tensor_tensor(diag, diag, const[0:m, CAUSAL, 0:m], ALU.add)
                    dve.drain()
                V.reduce_max(row[0:m, 0, p:p + 1], prob[0:m, p, 0:nk], AXX)
                dve.drain()
                V.tensor_scalar(row[0:m, 1, p:p + 1], row[0:m, 0, p:p + 1], -1.0, None, ALU.mult
                                ).then_inc(shift_ready.sem, 1)

            def inverse(u):
                m, p = unit_shape(u, cached)[2], u % PROBS
                dve.wait_ge(exp_ready.sem, exp_ready.done(l, base + u))
                V.reciprocal(row[0:m, 3, p:p + 1], row[0:m, 2, p:p + 1]).then_inc(inv_ready.sem, 1)

            logits(0)
            logits(1)
            for u in range(UNITS):
                inverse(u)
                if u + 2 < UNITS:
                    logits(u + 2)
                if u == 4:
                    third()
                if u == 6 and last:
                    take_k(l, st + 2)
            dve.wait_ge(o_high.sem, o_high.done(l, st))
            hold(dve, "dve")
            for bank, cols in ((score[0], slice(0, SEQ)), (score[1][:, 0:DEC], slice(SEQ, TOK))):
                o = [t[:, bass.ds(o_tile, 1), cols].rearrange("p a n -> p (a n)") for t in (o_hi, o_lo)]
                r = V.tensor_tensor(o[1], bank, o[0], ALU.subtract)
            r.then_inc(o_ready.sem, 1)

        def merge(l):
            def body(m, nxt_split):
                g0, g1 = GROUP_AT["gate"]
                split_lo(l, "gate", 1, 2 * m)
                split_lo(l, "gate", 0, 2 * m + 1)
                split_lo(l, "gate", 1, 2 * m + 1)
                nxt_split() if nxt_split else split_lo(l, "gate", 0, 2 * m + 2)
                dve.wait_ge(acc_free[0].sem, acc_free[0].done(l, g0 + 3 * m))
                dve.wait_ge(branch_done.sem, branch_done.done(l, 2 * m))
                dve.wait_ge(prod_lo.sem, prod_lo.free(l, KF + m))
                V.tensor_tensor(two(msum[:, :]), two(sig[:, 0, :]), pair[1], ALU.mult).then_inc(acc_free[1].sem, 1)
                dve.wait_ge(acc_free[1].sem, acc_free[1].done(l, g1 + 3 * m))
                dve.wait_ge(branch_done.sem, branch_done.done(l, 2 * m + 1))
                V.tensor_tensor(two(mtmp[:, :]), two(sig[:, 1, :]), pair[0], ALU.mult).then_inc(acc_free[0].sem, 1)
                dve.drain()
                V.tensor_tensor(msum[:, :], msum[:, :], mtmp[:, :], ALU.add)
                dve.drain()
                dve.wait_ge(acc_free[0].sem, acc_free[0].done(l, g0 + 3 * m + 1))
                dve.wait_ge(chunk_done[1].sem, chunk_done[1].done(l, SPLIT_AT["gate"][1] + 2 * m + 1))
                V.tensor_tensor(two(mtmp[:, :]), two(sig[:, 2, :]), pair[1], ALU.mult).then_inc(acc_free[1].sem, 1)
                dve.drain()
                V.tensor_tensor(msum[:, :], msum[:, :], mtmp[:, :], ALU.add).then_inc(merged.sem, 1)
                dve.wait_ge(prod_hi.sem, prod_hi.done(l, KF + m))
                V.tensor_tensor(tile(m_lo, m), msum[:, :], tile(m_hi, m), ALU.subtract).then_inc(prod_lo.sem, 1)
            pairs(KD, body, lambda: split_lo(l, "out", 0, 0))

        V.memset(c_stat[:, :, :], 1.0)
        dve.drain()
        V.memset(eps_t[:, :], EPS).then_inc(eps_ready.sem, 1)
        dve.wait_ge(start_in.sem, start_in.done(0, 3))
        dve.sem_inc(h_ready.sem, KD)
        dve.wait_ge(first_used.sem, ADA_FIRST // 2 + RING)
        take_ada(0, ADA_FIRST)
        with dve.Fori(0, DEPTH) as l:
            dve.wait_ge(small_in.sem, small_in.done(l, 1))
            hold(dve, "dve")
            fold_mods(l, "first")
            inverse_rms(l, 0)
            split_lo(l, "f1a", 0, 0)
            make_x(l, 0)
            ffn_up(l, "a", lambda: split_lo(l, "f2a", 0, 0))
            ffn_down(l, "a", 1, lambda: split_lo(l, "tri", 0, 0))
            split_lo(l, "tri", 1, 0)
            for s in (0, 1):
                dve.wait_ge(ada_used[s].sem, ada_used[s].done(l, ADA_N[s] - 1))
            hold(dve, "dve")
            take_ada(l * ADA_LAYER + ADA_FIRST, ADA_LAYER)
            fold_mods(l, "rest")
            inverse_rms(l, 1)
            residual(l, 0)
            inverse_rms(l, 2)
            make_x(l, 1)
            before_pairs(l)
            with dve.Fori(0, B_PAIRS) as b:
                stage(l, b, PAST, b * SEGS_B, b + A_PAIRS, lambda: split_lo(l, "tri", 1, b + 2),
                      lambda: split_lo(l, "tri", 0, b + 3), True)
            seg0 = B_PAIRS * SEGS_B
            stage(l, B_PAIRS, A_WIN, seg0, 0, lambda: split_lo(l, "tri", 1, NP), lambda: split_lo(l, "uc", 0, 0), True)
            stage(l, B_PAIRS + 1, A_WIN, seg0 + SEGS_A, 1, lambda: split_lo(l, "uc", 1, 0),
                  lambda: split_lo(l, "gate", 0, 0), False)
            for c in (0, 1):
                dve.wait_ge(chunk_done[c].sem, chunk_done[c].done(l, SPLIT_AT["uc"][c]))
                V.tensor_tensor(two(nxt[:, c, :]), two(c_mix[:, c, :]), pair[c], ALU.mult
                                ).then_inc(acc_free[c].sem, 1)
            dve.drain()
            dve.sem_inc(oc_made.sem, 2)
            for c in (0, 1):
                dve.wait_ge(o_high.sem, o_high.done(l, NP + c))
                V.tensor_tensor(o_lo[:, NP + c, :], nxt[:, c, :], o_hi[:, NP + c, :], ALU.subtract
                                ).then_inc(o_ready.sem, 1)
            dve.wait_ge(kv_free.sem, kv_free.done(l, NP - 1))
            hold(dve, "dve")
            merge(l)
            clear_acc()

            def out_pair(i, nxt_split):
                split_lo(l, "out", 1, i)
                add_squares(l, 3, 0, 2 * i)
                nxt_split() if nxt_split else split_lo(l, "out", 0, i + 1)
                add_squares(l, 3, 1, 2 * i + 1)
            pairs(KD // 2, out_pair, lambda: split_lo(l, "f1b", 0, 0))
            inverse_rms(l, 3)
            residual(l, 1)
            inverse_rms(l, 4)
            make_x(l, 2)
            ffn_up(l, "b", lambda: split_lo(l, "f2b", 0, 0))
            ffn_down(l, "b", 5, lambda: None)
            inverse_rms(l, 5)
            residual(l, 2)
            dve.drain()
            dve.sem_inc(small_used.sem, 1)

    @block.gpsimd
    def _(pool):
        pool.sem_inc(kv_free.sem, kv_free.slots)

        def dma(dst, src, signal):
            hold(pool, "pool")
            nc.gpsimd.dma_start(dst, src).then_inc(signal.sem, 16)

        def row_of(name, index):
            return ins[name][bass.ds(index, 1), :, :].rearrange("a p n -> (a p) n")

        def ada_load(l, s, i, n):
            pool.wait_ge(ada_used[s].sem, ada_used[s].free(l, i))
            dma(ada_w[:, s, :], row_of("ada", l * ADA_LAYER + ADA_FIRST + n), ada_full[s])

        def caches(l, ab, index):
            n = PAST if ab == "b" else A_WIN
            dma(cache_k[:, 0:n], row_of("ck_" + ab, index), ck_in)
            dma(cache_v[:, 0:n // P, :].rearrange("p t n -> p (t n)"), row_of("cv_" + ab, index), cv_in)

        def strip_rows(l, a):
            dma(strip[:, :, :].rearrange("p a n -> p (a n)"), row_of("strip", l * A_PAIRS + a), strip_in)

        def decay_rows(l, b, dst, c0, c1, signal):
            src = scratch[bass.ds(l, 1), bass.ds(b * 2, 2), c0:c1].rearrange("a h n -> (a h) n")
            dma(dst[:, :, :], src.partition_broadcast(P), signal)

        def mixer_inputs(l):
            pool.wait_ge(chunk_done[1].sem, chunk_done[1].done(l, SPLIT_AT["f2a"][1] + KD - 1))
            dma(w_mix[:, :, :].rearrange("p g n -> p (g n)"), row_of("c_spatial", l), mix_in)
            dma(cache_f[:, :, :].rearrange("p t h -> p (t h)"), row_of("cache_f", l), mix_in)
            dma(b_forget[:, :], row_of("b_forget", l), mix_in)
            dma(c_gain[:, :], row_of("c_gain", l), mix_in)
            dma(c_bias[:, :, :].rearrange("p t n -> p (t n)"), row_of("c_bias", l), mix_in)
            caches(l, "b", l * B_PAIRS)
            pool.wait_ge(f_sums_in.sem, f_sums_in.done(l, 0))
            dma(outs["logf"][bass.ds(l, 1), :, :].rearrange("a p n -> (a p) n"),
                logf[:, :, :].rearrange("p t h -> p (t h)"), out_small)
            pool.wait_ge(f_rows_ready.sem, f_rows_ready.done(l, 0))
            dma(scratch[bass.ds(l, 1), :, :].rearrange("a h n -> (a h) n"), f_rows[:, :], rows_out)
            pool.wait_ge(vc_ready.sem, vc_ready.done(l, 0))
            dma(outs["vc"][bass.ds(l, 1), :, :].rearrange("a p n -> (a p) n"), v_tok_c[0:DEC, 4, :], out_small)
            pool.wait_ge(rows_out.sem, rows_out.done(l, 0))
            pool.wait_ge(mix_ready.sem, mix_ready.done(l, 0))
            pool.wait_ge(out_small.sem, out_small.done(l, 1))
            decay_rows(l, 0, decay_s, SEQ, SEQ + SC, decay_s_in)
            decay_rows(l, 0, decay_p, 0, SEQ, decay_p_in)

        def stage(l, st, k_tile, v_tile, after):
            for staged, src, t in ((k_staged, k_st, k_tile), (v_staged, v_st, v_tile)):
                pool.wait_ge(staged.sem, staged.done(l, st))
                dma(outs["kv"][bass.ds(l, 1), :, bass.ds(t, 1), :].rearrange("a p t n -> (a p) (t n)"), src[:, :],
                    out_kv)
            pool.wait_ge(out_kv.sem, out_kv.done(l, 2 * st + 1))
            pool.sem_inc(kv_free.sem, 1)
            if after is None:
                return
            pool.wait_ge(o_summed.sem, o_summed.done(l, st * UNITS + 1))
            if after == "b":
                pool.wait_ge(shift_ready.sem, shift_ready.done(l, st * UNITS + 1))
                caches(l, "b", l * B_PAIRS + st + 1)
                decay_rows(l, st + 1, decay_s, SEQ, SEQ + SC, decay_s_in)
            else:
                caches(l, "a", l * A_PAIRS + st + 1 - B_PAIRS)
            pool.wait_ge(shift_ready.sem, shift_ready.done(l, st * UNITS + UNITS - 1))
            if after == "b":
                decay_rows(l, st + 1, decay_p, 0, SEQ, decay_p_in)
            else:
                strip_rows(l, st + 1 - B_PAIRS)

        with pool.Fori(0, DEPTH) as l:
            with pool.Fori(0, KF) as i:
                for s in (0, 1):
                    ada_load(l, s, i, i * ADA_UP + s)
            with pool.Fori(0, KD // 2) as i:
                for a, (s, nth) in enumerate(((0, KF + 2 * i), (1, KF + i), (0, KF + 2 * i + 1))):
                    ada_load(l, s, nth, ADA_UP * KF + i * ADA_DOWN + a)
            mixer_inputs(l)
            with pool.Fori(0, B_PAIRS - 1) as b:
                stage(l, b, b + 4, b + 8, "b")
            stage(l, B_PAIRS - 1, B_PAIRS + 3, B_PAIRS + 7, "a")
            stage(l, B_PAIRS, 0, 2, "a")
            stage(l, B_PAIRS + 1, 1, 3, None)
        pool.wait_ge(h_ready.sem, h_ready.done(DEPTH - 1, 3 * KD - 1) + KD)
        dma(outs["h"], h[:, :, :], out_h)
        pool.wait_ge(out_h.sem, 16)
        pool.wait_ge(out_kv.sem, DEPTH * out_kv.per_layer * 16)
        pool.wait_ge(out_small.sem, out_small.done(DEPTH - 1, 1))
        pool.wait_ge(roll_out.sem, roll_out.done(DEPTH - 1, 1))

    block_ctx.__exit__(None, None, None)


def constants():
    j, k = np.arange(P)[:, None], np.arange(P)[None, :]
    out = np.zeros((P, NCONST, P), np.float32)
    out[:, IDENT] = j == k
    out[:, ONES] = 1.0
    out[:, TRI_LE] = j <= k
    out[:, TRI_GT] = j > k
    out[:, CAUSAL] = np.where(k > j, np.float32(NEG), np.float32(0))
    return out


def tiles(w, k_tiles, chunks):
    n, rows, cols = w.shape
    kt = k_tiles // chunks
    w = w.reshape(n, chunks, kt, P, cols // P, P)
    return np.ascontiguousarray(w.transpose(0, 4, 1, 3, 2, 5)).reshape(n * (cols // P) * chunks, P, kt * P)


def layout(v):
    f = {k: np.asarray(x) for k, x in v.items()}
    g = {}
    x = np.concatenate([f["x_prompt"][0], f["x_sample"][0]], 0).T
    g["x"] = x.reshape(KD, P, TOK).transpose(1, 0, 2)
    c = np.concatenate([f["c_prompt"], f["c_sample"]], 0).T
    g["cond"] = c.reshape(KD, P, 2).transpose(1, 0, 2)
    g["const"] = constants()
    g["ada"] = tiles(f["w_ada"], KD, 1)
    g["b_ada"] = f["b_ada"].reshape(DEPTH * N_ADA, P).T
    g["norm_g"] = f["norm_g"].reshape(DEPTH, 6 * KD, P).transpose(0, 2, 1)
    w1 = f["ffn_w1"].reshape(DEPTH * 2, D_MODEL, 2, D_FF)
    w1 = np.pad(w1, ((0, 0), (0, 0), (0, 0), (0, KF * P - D_FF)))
    w1 = w1.reshape(DEPTH * 2, D_MODEL, 2, KF, P).transpose(0, 1, 3, 2, 4).reshape(DEPTH * 2, D_MODEL, 2 * KF * P)
    g["f1"] = tiles(w1, KD, 1)
    w2 = f["ffn_w2"].reshape(DEPTH * 2, D_FF, D_MODEL)
    g["f2"] = tiles(np.pad(w2, ((0, 0), (0, KF * P - D_FF), (0, 0))), KF, 2)
    w = f["w_in"]
    fb0 = 3 * A_HEADS * HD + 3 * B_HEADS * HD
    uc0 = fb0 + B_HEADS
    gl0 = uc0 + 512
    fb = np.pad(w[:, :, fb0:uc0], ((0, 0), (0, 0), (0, P - B_HEADS)))

    def column_tile(c):
        return w[:, :, c:c + P]

    triples = [column_tile(uc0 + 256), column_tile(uc0 + 384), fb]
    for first, heads in ((3 * A_HEADS * HD, B_HEADS), (0, A_HEADS)):
        for pr in range(heads // 2):
            triples += [column_tile(first + part * heads * HD + pr * P) for part in range(3)]
    tri = tiles(np.concatenate(triples, 2), KD, 1).reshape(DEPTH * (NP + 1), 3, P, KD * P)
    tri = tri.transpose(0, 2, 1, 3).reshape(DEPTH * (NP + 1), P, 2, SLOT).transpose(0, 2, 1, 3)
    g["tri"] = tri.reshape(-1, P, SLOT)
    g["uc"] = tiles(w[:, :, uc0:uc0 + 256], KD, 1)
    gl = w[:, :, gl0:].reshape(DEPTH, D_MODEL, 3, KD, P)
    br = np.concatenate([f["w_br_a"], f["w_br_b"], f["w_br_c"]], 1).reshape(DEPTH, D_MODEL, 1, KD, P)
    g["gate"] = tiles(np.concatenate([gl, br], 2).transpose(0, 1, 3, 2, 4).reshape(DEPTH, D_MODEL, -1), KD, 1)
    g["wout"] = tiles(f["w_out"], KD, 1)
    g["b_gate"] = f["b_gate"].reshape(DEPTH, 3 * KD, P).transpose(0, 2, 1)
    g["b_forget"] = np.broadcast_to(f["b_forget"][:, None, :], (DEPTH, P, B_HEADS))
    g["c_gain"] = np.broadcast_to(f["c_vnorm_g"][:, None, :], (DEPTH, P, 256))
    cb = f["c_spatial_b"].reshape(DEPTH, 2, 2, 1, P)
    g["c_bias"] = np.broadcast_to(cb, (DEPTH, 2, 2, HD, P)).transpose(0, 2, 3, 1, 4).reshape(DEPTH, P, 2 * P)
    g["cache_f"] = f["cache_b_logf"][:, 0].reshape(DEPTH, 8, P, B_HEADS).transpose(0, 2, 1, 3).reshape(DEPTH, P, 64)
    g["c_spatial"] = f["c_spatial_w"].transpose(0, 3, 1, 2).reshape(DEPTH, P, C_GROUPS * P)
    for name in ("cache_a_k", "cache_a_v"):
        g[name] = f[name].reshape(DEPTH, A_WIN, A_HEADS * HD)
    p, c = np.arange(P)[:, None], np.arange(STRIP)[None, :]
    rel = np.clip(p - (c - 512), -(CHUNK - 1), REL_MAX) + CHUNK - 1
    strip = f["a_rel_bias"][:, :, rel].transpose(0, 2, 1, 3)
    strip = np.where(((p < CHUNK) & (c >= 512 + CHUNK))[None, :, None, :], np.float32(NEG), strip)
    g["strip"] = strip.reshape(DEPTH, P, A_PAIRS, 2 * STRIP).transpose(0, 2, 1, 3).reshape(-1, P, 2 * STRIP)
    for ab, heads, n in (("a", A_HEADS, A_WIN), ("b", B_HEADS, PAST)):
        k = f[f"cache_{ab}_k"][:, 0].reshape(DEPTH, n, heads // 2, P)
        g["ck_" + ab] = k.transpose(0, 2, 3, 1).reshape(-1, P, n)
        vv = f[f"cache_{ab}_v"][:, 0].reshape(DEPTH, n // P, P, heads // 2, P)
        g["cv_" + ab] = vv.transpose(0, 3, 2, 1, 4).reshape(-1, P, n)
    return {k: np.ascontiguousarray(x) for k, x in g.items()}


OUTS = {"h": (P, KD, TOK), "kv": (DEPTH, P, 12, TOK), "logf": (DEPTH, P, NT * B_HEADS), "vc": (DEPTH, DEC, 256),
        "roll_k": (DEPTH, A_WIN - DEC, A_HEADS * HD), "roll_v": (DEPTH, A_WIN - DEC, A_HEADS * HD)}


def kernel(**inputs):
    import concourse.bacc as bacc
    from concourse.bass_utils import run_bass_kernel_spmd

    nc = bacc.Bacc("TRN2", target_bir_lowering=False, num_devices=1)
    arrays = layout(inputs)
    ins = {k: nc.dram_tensor(f"in_{k}", a.shape, mybir.dt.from_np(a.dtype), kind="ExternalInput").ap()
           for k, a in arrays.items()}
    outs = {k: nc.dram_tensor(f"out_{k}", s, F32, kind="ExternalOutput").ap() for k, s in OUTS.items()}
    build_program(nc, ins, outs)
    r = run_bass_kernel_spmd(nc, [{f"in_{k}": a for k, a in arrays.items()}], core_ids=[0]).results[0]
    r = {k: np.asarray(r[f"out_{k}"]) for k in OUTS}

    h = r["h"].transpose(2, 1, 0).reshape(TOK, D_MODEL)
    kv = r["kv"].transpose(0, 3, 2, 1).reshape(DEPTH, TOK, 12 * P)
    ka, va, kb, vb = np.split(kv, [256, 512, 1024], axis=2)
    logf = r["logf"].reshape(DEPTH, P, NT, B_HEADS).transpose(0, 2, 1, 3).reshape(DEPTH, NT * P, B_HEADS)

    def prompt(t, heads):
        return np.ascontiguousarray(t[:, :SEQ]).reshape(DEPTH, 1, SEQ, heads, HD)

    def sample(t, heads, before=None):
        t = t[:, SEQ:TOK]
        if before is not None:
            t = np.concatenate([before, t], 1)
        return np.ascontiguousarray(t).reshape(DEPTH, 1, -1, heads, HD)

    return (np.ascontiguousarray(h[:SEQ])[None], np.ascontiguousarray(h[SEQ:])[None],
            prompt(ka, A_HEADS), prompt(va, A_HEADS), prompt(kb, B_HEADS), prompt(vb, B_HEADS),
            np.ascontiguousarray(logf[:, :SEQ])[:, None],
            sample(ka, A_HEADS, r["roll_k"]), sample(va, A_HEADS, r["roll_v"]),
            sample(kb, B_HEADS), sample(vb, B_HEADS),
            np.ascontiguousarray(logf[:, SEQ:TOK])[:, None], r["vc"][:, None])
```

```python
import numpy as np
import concourse.bass as bass
from concourse import mybir

F32 = mybir.dt.float32
F32R = mybir.dt.float32r
ACT = mybir.ActivationFunctionType
ALU = mybir.AluOpType
AXX = mybir.AxisListType.X

P = 128
D_MODEL = 1024
SEQ = 512
DEC = 64
TOK = SEQ + DEC
HALF = TOK // 2
DEPTH = 2
PAST = 1024
A_WIN = 512
HD = 64
A_HEADS, B_HEADS = 4, 8
CHUNK = 64
REL_MAX = 128
C_GROUPS = 4
D_FF = 2752
KD = D_MODEL // P
KF = -(-D_FF // P)
KF2 = KF // 2
N_MOD = 9
N_ADA = N_MOD * KD
NT = 5
EPS = 1e-6
NEG = -1e30

A_PAIRS, B_PAIRS = A_HEADS // 2, B_HEADS // 2
NP = A_PAIRS + B_PAIRS
UNITS = 10
SEGS_A, SEGS_B = 12, 14
NSEG = B_PAIRS * SEGS_B + A_PAIRS * SEGS_A
PROBS = 3
STRIP = 640
NCONST, NMASK = 3, 2
IDENT, ONES, TRI_LE = range(NCONST)
TRI_GT, CAUSAL = range(NMASK)
TRI = 3 * KD
KT = TRI // 2
SLOT = KT * P

ADA_FIRST, ADA_UP, ADA_DOWN = 32, 2, 3
ADA_LAYER = ADA_UP * KF + ADA_DOWN * (KD // 2)
ADA_N = (KF + KD, KF + KD // 2)
RING = 4
assert sum(ADA_N) == ADA_LAYER and ADA_FIRST % (2 * RING) == 0
assert ADA_FIRST + DEPTH * ADA_LAYER == DEPTH * N_ADA and ADA_FIRST + ADA_LAYER >= N_ADA + 2 * KD

PHASES = [("f1a", KF, KF), ("f2a", KD, KD), ("tri", NP + 1, NP + 1), ("uc", 1, 1), ("gate", 2 * KD, 2 * KD),
          ("out", KD // 2, KD // 2), ("f1b", KF, KF), ("f2b", KD, KD)]
GROUPS = [("f1a", KF, KF), ("f2a", KD // 2, KD // 2), ("tri", 2 * (NP + 1), NP + 1), ("uc", 1, 1),
          ("gate", 3 * KD, 3 * KD), ("out", KD // 2, KD // 2), ("f1b", KF, KF), ("f2b", KD // 2, KD // 2)]


def running(counts):
    at, base = [0, 0], {}
    for name, a, b in counts:
        base[name] = tuple(at)
        at[0] += a
        at[1] += b
    return base, tuple(at)


SPLIT_AT, SPLIT_N = running(PHASES)
GROUP_AT, GROUP_N = running(GROUPS)
WIDTH = {"f1a": KD * P, "f2a": KF2 * P, "tri": SLOT, "uc": KD * P, "gate": KD * P, "out": KD * P, "f1b": KD * P,
         "f2b": KF2 * P}


class Signal:

    def __init__(self, nc, name, per_layer, slots=0, step=1):
        self.sem = nc.alloc_semaphore(name)
        self.per_layer, self.slots, self.step = per_layer, slots, step

    def done(self, l, n):
        return (l * self.per_layer + n + 1) * self.step + self.slots

    def free(self, l, n):
        return l * self.per_layer + n + 1


UNIT = [(hh, i) for i in (0, 4, 3, 2, 1) for hh in (0, 1)]
SAMPLE = 3

LEAD = 3
WORK = (1, 1, 2, 2, 1, 1, 1, 1, 1, 1, 1, 1, 1, 0, 1, 0, 1, 1, 1, 1, 1, 0, 0, 1, 2)
WORK_U = (1, 1, 1, 1, 1, 0, 1, 0, 1, 0, 1, 0, 1, 0, 1, 0, 1, 0, 1, 0, 1, 0, 0, 0, 0)

assert sum(WORK) == TRI and sum(WORK_U) == 2 * KD - LEAD


def unit_shape(u, cached):
    hh, i = UNIT[u]
    if i < 4:
        return hh, i, P, P * (i + 1), i + 1, [(0, P * (i + 1))]
    nk = cached + DEC
    return hh, i, DEC, nk, cached // P + 1, [(c, min(c + 512, nk)) for c in range(0, nk, 512)]


def first_segment(u, cached):
    return sum(len(unit_shape(v, cached)[5]) for v in range(u))


def last_user(u):
    return u - PROBS if u >= PROBS else max(v for v in range(UNITS) if v % PROBS == u) - UNITS


def build_program(nc, ins, outs):
    arena = [(nc.sbuf_base + 31) // 32 * 32]

    def sb(name, shape, dt=F32, at=None):
        n = int(np.prod(shape[1:])) * 4
        if at is None:
            at = arena[0]
            arena[0] += (n + 31) // 32 * 32
        assert at + n <= nc.sbuf_usable_end, (name, at + n, nc.sbuf_usable_end)
        return nc.alloc_sbuf_tensor_at(name, shape, dt, offset=at)

    h = sb("h", [P, KD, TOK])
    x_at = arena[0]
    x_hi = sb("x_hi", [P, KD, TOK], F32R)
    x_lo = sb("x_lo", [P, KD, TOK], F32R)
    y = sb("y", [P, KD, TOK], at=x_at)
    acc = sb("acc", [P, TOK], at=x_at + KD * TOK * 4)
    raw = sb("w_raw", [P, 2, SLOT])
    w_hi = sb("w_hi", [P, 2, SLOT], F32R)
    w_lo = sb("w_lo", [P, 2, SLOT], F32R)
    ada_w = sb("ada_w", [P, 2, KD * P])
    const = sb("const", [P, NCONST, P])
    ada_part = sb("ada_part", [P, 2, P])
    cond_s = sb("cond_silu", [P, KD, 2])
    eps_t = sb("eps", [P, 1])
    ada_all = sb("ada_all", [P, DEPTH * N_ADA, 2])
    mods = sb("mods", [P, N_MOD, KD, 2])
    norm_g = sb("norm_g", [P, 6, KD])
    pre_scale = sb("pre_scale", [P, 3, KD, 2])
    post_gate = sb("post_gate", [P, 3, KD, 2])
    b_gate = sb("b_gate", [P, 3, KD])
    f_query = sb("f_query", [P, NT, B_HEADS])
    c_stat = sb("c_stat", [P, 3, NT])
    row = sb("row", [P, 4, PROBS])
    tmp_at = arena[0]
    sil = sb("sil", [P, TOK])
    hid = sb("hid", [P, TOK])
    cond = sb("cond", [P, KD, 2], at=tmp_at)
    sq = sb("sq", [P, 2, TOK], at=tmp_at)
    big = arena[0]
    hid_hi = sb("hid_hi", [P, KF, TOK], F32R, at=big)
    hid_lo = sb("hid_lo", [P, KF, TOK], F32R, at=big + KF * TOK * 4)
    rms = sb("rms", [P, 4, TOK], at=big)
    nt = sb("norm_t", [P, 2, TOK], at=big + 16 * TOK)
    nx = sb("norm_x", [P, 2, TOK], at=big + 24 * TOK)
    ada_ring = sb("ada_ring", [P, RING, 2, KD * P], at=big)
    first_part = sb("first_part", [P, RING - 1, 2, P], at=big + RING * 2 * KD * P * 4)
    o_hi = sb("o_hi", [P, KD, TOK], F32R, at=big)
    o_lo = sb("o_lo", [P, KD, TOK], F32R, at=big + KD * TOK * 4)
    att = big + 2 * KD * TOK * 4
    m_hi = sb("m_hi", [P, KD, TOK], F32R, at=att)
    m_lo = sb("m_lo", [P, KD, TOK], F32R, at=att + KD * TOK * 4)
    sig = sb("sig", [P, 3, TOK], at=att + 2 * KD * TOK * 4)
    msum = sb("msum", [P, TOK], at=att + (2 * KD + 3) * TOK * 4)
    mtmp = sb("mtmp", [P, TOK], at=att + (2 * KD + 4) * TOK * 4)
    SC = PAST + DEC
    at = [att]

    def sa(name, shape, keep=True):
        t = sb(name, shape, at=at[0])
        if keep:
            at[0] += int(np.prod(shape[1:])) * 4
        return t

    f_rows = sa("f_rows", [B_HEADS, SEQ + SC], keep=False)
    prob = sa("prob", [P, PROBS, SC])
    prob_t = sa("prob_t", [P, 2, TOK])
    sp_at = at[0]
    decay_s = sa("decay_s", [P, 2, SC])
    decay_p = sa("decay_p", [P, 2, SEQ])
    strip = sb("strip", [P, 2, STRIP], at=sp_at)
    v_tok_c = sb("v_tok_c", [P, NT, 256], at=sp_at)
    w_mix = sb("w_mix", [P, C_GROUPS, P], at=sp_at + NT * 1024)
    c_gain = sb("c_gain", [P, 256], at=sp_at + NT * 1024 + 2048)
    c_bias = sb("c_bias", [P, 2, P], at=sp_at + NT * 1024 + 3072)
    fx = sb("fx", [P, 6, NT, B_HEADS], at=sp_at + NT * 1024 + 4096)
    cache_k = sa("cache_k", [P, PAST])
    cache_v = sa("cache_v", [P, 8, P])
    q_st = sa("q_stage", [P, TOK])
    k_st = sa("k_stage", [P, TOK])
    v_st = sa("v_stage", [P, TOK])
    nxt = sa("next", [P, 3, TOK])
    v_tok = sa("v_tok", [P, NT, P])
    o_tok = sa("o_tok", [P, NT, P])
    c_mix = sa("c_mix", [P, 2, TOK])
    cache_f = sa("cache_f", [P, 8, B_HEADS])
    later_f = sa("later_f", [P, 8, B_HEADS])
    earlier_f = sa("earlier_f", [P, 4, B_HEADS])
    logf = sa("logf", [P, NT, B_HEADS])
    b_forget = sa("b_forget", [P, B_HEADS])
    mask = sa("mask", [P, NMASK, P])

    ps = nc.alloc_psum_tensor("ps", [P, 8, 512], F32)
    pair = [ps[:, 0:2, 0:HALF], ps[:, 2:4, 0:HALF]]
    stat = ps[:, 4:6, 0:HALF]
    ada_ps = ps[:, 6, :]
    score = [ps[:, 4, :], ps[:, 5, :]]
    turned = ps[:, 6, :]
    att_out = ps[:, 7, :]
    scratch = nc.dram_tensor("f_scratch", (DEPTH, B_HEADS, SEQ + SC), F32, kind="Internal").ap()

    def two(ap):
        return ap.rearrange("p (b n) -> p b n", b=2)

    def tile(t, k):
        return t[:, bass.ds(k, 1), :].rearrange("p a n -> p (a n)")

    S = lambda *a, **k: Signal(nc, *a, **k)
    raw_full = [S(f"raw_full{s}", SPLIT_N[s], step=16) for s in (0, 1)]
    hi_ready = [S(f"hi_ready{s}", SPLIT_N[s]) for s in (0, 1)]
    lo_ready = [S(f"lo_ready{s}", SPLIT_N[s], 1) for s in (0, 1)]
    chunk_done = [S(f"chunk_done{s}", SPLIT_N[s], 1) for s in (0, 1)]
    acc_free = [S(f"acc_free{s}", GROUP_N[s], 1) for s in (0, 1)]
    first_full = [S(f"first_full{s}", 0, step=16) for s in range(RING)]
    first_sums = S("first_sums", 0)
    first_used = S("first_used", 0, RING - 1)
    last_used = S("last_used", 0, 1)
    ada_full = [S(f"ada_full{s}", ADA_N[s], step=16) for s in (0, 1)]
    ada_sums = S("ada_sums", ADA_N[1])
    ada_used = [S(f"ada_used{s}", ADA_N[s], 1) for s in (0, 1)]
    prod_hi = S("prod_hi", 2 * KF + KD)
    prod_lo = S("prod_lo", 2 * KF + KD, 1)
    merged = S("merged", KD)
    sq_ready = S("sq_ready", 6 * KD)
    sq_added = S("sq_added", 6 * KD, 2)
    stat_ready = S("stat_ready", 6)
    log_ready = S("log_ready", 6)
    est_ready = S("est_ready", 6)
    t_ready = S("t_ready", 3 * KD)
    nx_ready = S("nx_ready", 3 * KD)
    x_ready = S("x_ready", 3 * KD, 2)
    h_ready = S("h_ready", 3 * KD)
    start_in = S("start_in", 4, step=16)
    small_in = S("small_in", 2, step=16)
    roll_out = S("roll_out", 2, step=16)
    small_used = S("small_used", 1, 1)
    mix_in = S("mix_in", 6, step=16)
    cond_ready = S("cond_ready", 1)
    eps_ready = S("eps_ready", 1)
    ada_read = S("ada_read", 1, 1)
    tri_done = S("tri_done", 2 * (NP + 1))
    nxt_full = S("nxt_full", 3)
    logits_turned = S("logits_turned", 1)
    f_neg = S("f_neg", 1)
    f_exp = S("f_exp", 1)
    f_sums_in = S("f_sums_in", 1)
    f_sums = S("f_sums", 1)
    f_rows_ready = S("f_rows_ready", 1)
    vc_turned = S("vc_turned", 1)
    vc_copied = S("vc_copied", 1)
    vc_ready = S("vc_ready", 1)
    mixed = S("mixed", 1)
    mix_ready = S("mix_ready", 1)
    strip_in = S("strip_in", A_PAIRS, step=16)
    ck_in = S("ck_in", NP, step=16)
    cv_in = S("cv_in", NP, step=16)
    decay_s_in = S("decay_s_in", B_PAIRS, step=16)
    decay_p_in = S("decay_p_in", B_PAIRS, step=16)
    rows_out = S("rows_out", 1, step=16)
    q_staged = S("q_staged", NP)
    k_staged = S("k_staged", NP)
    v_staged = S("v_staged", NP)
    v_turned = S("v_turned", NP)
    v_ready = S("v_ready", NP)
    scores_ready = S("scores_ready", NSEG)
    scores_taken = S("scores_taken", NSEG, 2)
    shift_ready = S("shift_ready", NP * UNITS)
    exp_ready = S("exp_ready", NP * UNITS)
    inv_ready = S("inv_ready", NP * UNITS)
    prob_turned = S("prob_turned", NP * UNITS, PROBS)
    prob_t_ready = S("prob_t_ready", NP * UNITS, 1)
    o_summed = S("o_summed", NP * UNITS, 2)
    o_taken = S("o_taken", NP * UNITS, 1)
    o_turned = S("o_turned", NP)
    o_high = S("o_high", KD)
    o_ready = S("o_ready", KD, 1)
    oc_made = S("oc_made", 2)
    branch_done = S("branch_done", 2 * KD)
    out_kv = S("out_kv", 2 * NP, step=16)
    kv_free = S("kv_free", NP, 1)
    out_small = S("out_small", 2, step=16)
    out_h = S("out_h", 1, step=16)
    passed = {e: nc.alloc_semaphore(f"passed_{e}") for e in ("sp", "pe", "act", "dve", "pool")}

    def hold(eng, e):
        eng.sem_inc(passed[e], 1)

    def credits(eng, signals):
        for s in signals:
            eng.sem_inc(s.sem, s.slots)

    block_ctx = nc.Block()
    block = block_ctx.__enter__()

    @block.sync
    def _(sp):
        sp.dma_start(cond[:, :, :], ins["cond"]).then_inc(start_in.sem, 16)
        sp.dma_start(const[:, :, :], ins["const"]).then_inc(start_in.sem, 16)
        sp.dma_start(ada_all[:, :, :], ins["b_ada"]).then_inc(start_in.sem, 16)
        sp.dma_start(h[:, :, :], ins["x"]).then_inc(start_in.sem, 16)
        with sp.Fori(0, ADA_FIRST // (2 * RING)) as i:
            for s in range(RING):
                if s < RING - 1:
                    sp.wait_ge(first_used.sem, i * (RING - 1) + s + 1)
                else:
                    sp.wait_ge(last_used.sem, i + 1)
                hold(sp, "sp")
                sp.dma_start(ada_ring[:, s, :, :], ins["ada"][bass.ds((i * RING + s) * 2, 2), :, :]
                             .rearrange("t p n -> p t n")).then_inc(first_full[s].sem, 16)

        def load(l, ph, s, i, src, index):
            src = src[bass.ds(index, 1), :, :].rearrange("a p n -> p (a n)")
            sp.wait_ge(lo_ready[s].sem, lo_ready[s].free(l, SPLIT_AT[ph][s] + i))
            hold(sp, "sp")
            sp.dma_start(raw[:, s, 0:WIDTH[ph]], src).then_inc(raw_full[s].sem, 16)

        def ada_load(l, i, n):
            sp.wait_ge(ada_used[1].sem, ada_used[1].free(l, i))
            hold(sp, "sp")
            sp.dma_start(ada_w[:, 1, :], ins["ada"][bass.ds(l * ADA_LAYER + ADA_FIRST + n, 1), :, :]
                         .rearrange("a p n -> p (a n)")).then_inc(ada_full[1].sem, 16)

        def load_pairs(l, ph, n, src, first):
            with sp.Fori(0, n) as i:
                for s in (0, 1):
                    load(l, ph, s, i, src, first + i * 2 + s)

        with sp.Fori(0, DEPTH) as l:
            for s in (0, 1):
                load(l, "f1a", s, 0, ins["f1"], (l * 2) * 2 * KF + s)
            sp.wait_ge(small_used.sem, small_used.free(l, 0))
            hold(sp, "sp")
            for dst, name in ((norm_g, "norm_g"), (b_gate, "b_gate")):
                sp.dma_start(dst[:, :, :].rearrange("p a b -> p (a b)"),
                             ins[name][bass.ds(l, 1), :, :].rearrange("a p n -> p (a n)")
                             ).then_inc(small_in.sem, 16)
            with sp.Fori(1, KF) as i:
                load(l, "f1a", 0, i, ins["f1"], (l * 2) * 2 * KF + i * 2)
                ada_load(l, i - 1, (i - 1) * ADA_UP + 1)
                load(l, "f1a", 1, i, ins["f1"], (l * 2) * 2 * KF + i * 2 + 1)
            ada_load(l, KF - 1, (KF - 1) * ADA_UP + 1)
            for name, out in (("cache_a_k", "roll_k"), ("cache_a_v", "roll_v")):
                sp.dma_start(outs[out][bass.ds(l, 1), :, :],
                             ins[name][bass.ds(l, 1), DEC:A_WIN, :]).then_inc(roll_out.sem, 16)
            with sp.Fori(0, KD // 2) as i:
                for p in (0, 1):
                    for s in (0, 1):
                        load(l, "f2a", s, i * 2 + p, ins["f2"], (l * 2) * 2 * KD + i * 4 + p * 2 + s)
                    if p == 0:
                        ada_load(l, i + KF, i * ADA_DOWN + ADA_UP * KF + 1)
            load_pairs(l, "tri", NP + 1, ins["tri"], l * 2 * (NP + 1))
            for s in (0, 1):
                load(l, "uc", s, 0, ins["uc"], l * 2 + s)
            load_pairs(l, "gate", 2 * KD, ins["gate"], l * 4 * KD)
            load_pairs(l, "out", KD // 2, ins["wout"], l * KD)
            load_pairs(l, "f1b", KF, ins["f1"], (l * 2 + 1) * 2 * KF)
            load_pairs(l, "f2b", KD, ins["f2"], (l * 2 + 1) * 2 * KD)

    @block.tensor
    def _(pe):
        credits(pe, chunk_done + ada_used + [prob_turned, o_summed, first_used, last_used])
        mm, turn_in = nc.tensor.matmul, nc.tensor.transpose

        def split_tile(out, s, t, hi, lo, first, last):
            wh, wl = w_hi[:, s, t * P:(t + 1) * P], w_lo[:, s, t * P:(t + 1) * P]
            for n, (w, xx) in enumerate(((wh, hi), (wh, lo), (wl, hi))):
                for b in (0, 1):
                    r = mm(out[:, b, :], w, xx[:, b * HALF:(b + 1) * HALF],
                           start=first and n == 0, stop=last and n == 2)
            return r

        def chunk_ready(l, ph, s, i):
            pe.wait_ge(lo_ready[s].sem, lo_ready[s].done(l, SPLIT_AT[ph][s] + i))

        def pair_free(l, ph, p, i):
            pe.wait_ge(acc_free[p].sem, acc_free[p].free(l, GROUP_AT[ph][p] + i))

        def whole_chunk(l, ph, s, p, i, group, hi, lo, gate=None):
            chunk_ready(l, ph, s, i)
            pair_free(l, ph, p, group)
            for t in range(KD):
                if gate is not None:
                    gate(t)
                r = split_tile(pair[p], s, t, hi[:, t, :], lo[:, t, :], t == 0, t == KD - 1)
            r.then_inc(chunk_done[s].sem, 1)

        def first_pair(l, ph, hi, lo, gate):
            for s in (0, 1):
                chunk_ready(l, ph, s, 0)
                pair_free(l, ph, s, 0)
            for t in range(KD + 2):
                if t < KD:
                    gate(t)
                for s, k in ((0, t), (1, t - 2)):
                    if 0 <= k < KD:
                        r = split_tile(pair[s], s, k, hi[:, k, :], lo[:, k, :], k == 0, k == KD - 1)
                        if k == KD - 1:
                            r.then_inc(chunk_done[s].sem, 1)

        def x_tile(l, n):
            return lambda t: pe.wait_ge(x_ready.sem, x_ready.done(l, n * KD + t))

        def column_sums(l, n):
            pe.wait_ge(sq_added.sem, sq_added.done(l, n * KD + KD - 1))
            for b in (0, 1):
                r = mm(stat[:, b, :], const[:, ONES, :], acc[:, b * HALF:(b + 1) * HALF], start=True, stop=True)
            r.then_inc(stat_ready.sem, 1)

        def sum_squares(l, n):
            for k in range(KD):
                pe.wait_ge(sq_ready.sem, sq_ready.done(l, n * KD + k))
                for b in (0, 1):
                    r = mm(stat[:, b, :], const[:, ONES, :], sq[:, k % 2, b * HALF:(b + 1) * HALF],
                           start=k == 0, stop=k == KD - 1)
                r.then_inc(sq_added.sem if k < KD - 1 else stat_ready.sem, 1)

        def ada_product(w, n):
            for k in range(KD):
                r = mm(ada_ps[:, bass.ds(n * 2, 2)], w[:, k * P:(k + 1) * P], cond_s[:, k, :],
                       start=k == 0, stop=k == KD - 1)
            return r

        def ada_sum(part, n):
            for g in (0, 1):
                r = mm(ada_ps[:, bass.ds(n * 2 + g, 1)], part[:, g, :], const[:, ONES, 0:1], start=True, stop=True)
            return r

        def ada_tile(l, s, i, n):
            if s == 0:
                pe.wait_ge(ada_full[0].sem, ada_full[0].done(l, i))
                r = ada_product(ada_w[:, 0, :], n)
            else:
                pe.wait_ge(ada_sums.sem, ada_sums.done(l, i))
                r = ada_sum(ada_part, n)
            r.then_inc(ada_used[s].sem, 1)

        def ffn(l, ab, n, ada):
            sum_squares(l, 2 * n)
            x_in = x_tile(l, n)
            if ada:
                pe.wait_ge(ada_read.sem, ada_read.done(l, -1) + 1)
                hold(pe, "pe")
            first_pair(l, "f1" + ab, x_hi, x_lo, x_in)
            if ada:
                for p in (0, 1):
                    ada_tile(l, p, 0, p)
            with pe.Fori(1, KF) as i:
                for p in (0, 1):
                    whole_chunk(l, "f1" + ab, p, p, i, i, x_hi, x_lo)
                    if ada:
                        ada_tile(l, p, i, i * 2 + p)
            with pe.Fori(0, KD // 2) as i:
                for p in (0, 1):
                    pair_free(l, "f2" + ab, p, i)
                    for s in (0, 1):
                        chunk_ready(l, "f2" + ab, s, 2 * i + p)
                        for t in range(KF2):
                            k = s * KF2 + t
                            if p == 0:
                                pe.wait_ge(prod_lo.sem, prod_lo.done(l, (0 if ab == "a" else KF + KD) + k))
                            r = split_tile(pair[p], s, t, hid_hi[:, k, :], hid_lo[:, k, :], k == 0, k == KF - 1)
                        r.then_inc(chunk_done[s].sem, 1)
                        a = 2 * p + s
                        if ada and a < ADA_DOWN:
                            ada_tile(l, s, KF + (i if s else 2 * i + p), ADA_UP * KF + i * ADA_DOWN + a)
            column_sums(l, 2 * n + 1)

        def project(l, T, j0, j1):
            for j in range(j0, j1):
                project_tile(l, T, j, KT - 1)

        def project_tile(l, T, j, last):
            g, k, s = j // KD, j % KD, j // KT
            p = g % 2
            if j % KT == 0:
                chunk_ready(l, "tri", s, T)
            if k == 0:
                pair_free(l, "tri", p, T if p else 2 * T + g // 2)
            r = split_tile(pair[p], s, j % KT, x_hi[:, k, :], x_lo[:, k, :], k == 0, k == KD - 1)
            if j in (KD - 1, 2 * KD - 1):
                r.then_inc(tri_done.sem, 1)
            elif j == TRI - 1:
                r.then_inc(chunk_done[1].sem, 1)
            if j == last:
                if j == KD - 1:
                    pe.drain()
                    pe.sem_inc(chunk_done[0].sem, 1)
                else:
                    r.then_inc(chunk_done[0].sem, 1)

        def project_u(l, j0, j1):
            for j in range(j0, min(j1, 2 * KD)):
                s, k = j // KD, j % KD
                if k == 0:
                    chunk_ready(l, "uc", s, 0)
                    pair_free(l, "uc", s, 0)
                r = split_tile(pair[s], s, k, x_hi[:, k, :], x_lo[:, k, :], k == 0, k == KD - 1)
                if k == KD - 1:
                    r.then_inc(chunk_done[s].sem, 1)

        def projected(steps, project_part):
            at, left = [0], list(steps)

            def work():
                j = at[0]
                at[0] += left.pop(0)
                if at[0] > j:
                    project_part(j, at[0])
            return work

        def triple(l, T, following):
            def part(j0, j1):
                n = TRI - LEAD
                if j0 < n:
                    project(l, T, j0 + LEAD, min(j1, n) + LEAD)
                if j1 > n:
                    following(max(j0, n) - n, j1 - n)
            return projected(WORK, part)

        def before_pairs(l):
            x_in = x_tile(l, 1)
            for k in range(KD + 1):
                if k < KD:
                    x_in(k)
                    project_tile(l, 0, k, KD - 1)
                if k:
                    project_tile(l, 0, KD + k - 1, KD - 1)
            for j in range(2 * KD, TRI):
                project_tile(l, 0, j, KD - 1)
            project(l, 1, 0, 4)
            pe.wait_ge(nxt_full.sem, nxt_full.done(l, 2))
            hold(pe, "pe")
            for t in range(NT):
                m = P if t < 4 else DEC
                r = turn_in(ps[0:m, 4, t * 8:t * 8 + 8], nxt[0:8, 2, t * P:t * P + m], const[0:8, IDENT, 0:8])
            r.then_inc(logits_turned.sem, 1)
            for t in range(NT):
                m = P if t < 4 else DEC
                for c in (0, 1):
                    at = (t % 2) * 256 + c * P
                    r = turn_in(ps[0:m, 5 + t // 2, at:at + P], nxt[:, c, t * P:t * P + m], const[:, IDENT, :])
            r.then_inc(vc_turned.sem, 1)
            project(l, 1, 4, KT)
            pe.wait_ge(f_sums_in.sem, f_sums_in.done(l, 0))
            for t in range(4):
                o = ps[:, 4, 64 + t * 8:72 + t * 8]
                mm(o, const[:, TRI_LE, :], logf[:, t, :], start=True, stop=t == 0)
                if t:
                    mm(o, const[:, ONES, :], earlier_f[:, t, :], start=False, stop=True)
            mm(ps[0:DEC, 4, 96:104], const[0:DEC, TRI_LE, 0:DEC], logf[0:DEC, 4, :], start=True, stop=True)
            mm(ps[0:B_HEADS, 4, 128:128 + DEC], logf[0:DEC, 4, :], const[0:DEC, TRI_LE, 0:DEC],
               start=True, stop=True)
            pe.wait_ge(vc_copied.sem, vc_copied.done(l, 0))
            for t in range(4):
                o = ps[0:B_HEADS, 7, t * P:(t + 1) * P]
                mm(o, logf[:, t, :], const[:, TRI_LE, :], start=True, stop=t == 0)
                if t:
                    mm(o, earlier_f[:, t, :], const[:, ONES, :], start=False, stop=True)
            for t in range(8):
                o = ps[0:B_HEADS, 5 + t // 4, (t % 4) * P:(t % 4 + 1) * P]
                r = mm(o, cache_f[:, t, :], mask[:, TRI_GT, :], start=True, stop=t == 7)
                if t < 7:
                    r = mm(o, later_f[:, t, :], const[:, ONES, :], start=False, stop=True)
            r.then_inc(f_sums.sem, 1)
            project(l, 1, KT, 18)
            pe.wait_ge(vc_ready.sem, vc_ready.done(l, 0))
            pe.wait_ge(f_rows_ready.sem, f_rows_ready.done(l, 0))
            for T in (0, 1):
                for hh in (0, 1):
                    g, rows = 2 * T + hh, slice(HD * hh, HD * hh + HD)
                    for n in range(4):
                        mm(ps[rows, 5 + T, n * P:(n + 1) * P], v_tok_c[:, n, g * HD:(g + 1) * HD],
                           w_mix[:, g, :], start=True, stop=True)
                    r = mm(ps[rows, 7, T * DEC:(T + 1) * DEC], v_tok_c[0:DEC, 4, g * HD:(g + 1) * HD],
                           w_mix[0:DEC, g, 0:DEC], start=True, stop=True)
            r.then_inc(mixed.sem, 1)
            project(l, 1, 18, TRI)
            project(l, 2, 0, LEAD)

        def stage(l, st, cached, seg0, work):
            base = st * UNITS

            def scores(u):
                hh, i, m, nk, _, segs = unit_shape(u, cached)
                rows, s0 = slice(hh * HD, hh * HD + HD), first_segment(u, cached)
                q = q_st[rows, i * P:i * P + m]
                for e, (c0, c1) in enumerate(segs):
                    pe.wait_ge(scores_taken.sem, scores_taken.free(l, seg0 + s0 + e))
                    if i == 4 and hh == 0 and e == 0:
                        pe.wait_ge(ck_in.sem, ck_in.done(l, st))
                    if i == 4:
                        hold(pe, "pe")
                    if i == 4 and c0 >= cached:
                        k = k_st[rows, SEQ:TOK]
                    else:
                        k = cache_k[rows, c0:c1] if i == 4 else k_st[rows, c0:c1]
                    mm(score[(s0 + e) % 2][0:m, 0:c1 - c0], q, k, start=True, stop=True
                       ).then_inc(scores_ready.sem, 1)

            def turn(u):
                hh, i, m, nk, nb, _ = unit_shape(u, cached)
                n = base + u
                pe.wait_ge(exp_ready.sem, exp_ready.done(l, n))
                pe.wait_ge(prob_t_ready.sem, prob_t_ready.free(l, n))
                if nb > 8:
                    pe.wait_ge(o_taken.sem, o_taken.free(l, n))
                if i == 4:
                    hold(pe, "pe")
                for b in range(nb):
                    w = min(P, nk - b * P)
                    out = turned[0:w, b * m:(b + 1) * m] if b < 8 else att_out[0:w, 256:256 + m]
                    r = turn_in(out, prob[0:m, u % PROBS, b * P:b * P + w], const[0:m, IDENT, 0:m])
                r.then_inc(prob_turned.sem, 1)

            def weigh(u):
                hh, i, m, nk, nb, _ = unit_shape(u, cached)
                n, cols = base + u, slice(hh * HD, hh * HD + HD)
                pe.wait_ge(prob_t_ready.sem, prob_t_ready.done(l, n))
                pe.wait_ge(o_taken.sem, o_taken.free(l, n))
                if i == 4 and hh == 0:
                    pe.wait_ge(cv_in.sem, cv_in.done(l, st))
                if i == 4:
                    hold(pe, "pe")
                for b in range(nb):
                    w = min(P, nk - b * P)
                    if i < 4:
                        v = v_tok[:, b, cols]
                    else:
                        v = cache_v[:, b, cols] if b < nb - 1 else v_tok[0:w, 4, cols]
                    r = mm(att_out[0:m, 0:HD], prob_t[0:w, u % 2, b * m:(b + 1) * m], v,
                           start=b == 0, stop=b == nb - 1)
                r.then_inc(o_summed.sem, 1)

            work()
            pe.wait_ge(v_staged.sem, v_staged.done(l, st))
            for t in range(NT):
                m = P if t < 4 else DEC
                out = turned[:, t * P:(t + 1) * P] if t < 4 else att_out[0:m, 0:P]
                r = turn_in(out, v_st[:, t * P:t * P + m], const[:, IDENT, :])
            r.then_inc(v_turned.sem, 1)
            work()
            pe.wait_ge(q_staged.sem, q_staged.done(l, st))
            pe.wait_ge(k_staged.sem, k_staged.done(l, st))
            pe.wait_ge(o_ready.sem, o_ready.free(l, st))
            scores(0)
            work()
            scores(1)
            work()
            pe.wait_ge(v_ready.sem, v_ready.done(l, st))
            for u in range(UNITS):
                if u + 2 < UNITS:
                    scores(u + 2)
                work()
                turn(u)
                work()
                weigh(u)
            work()
            pe.wait_ge(o_taken.sem, o_taken.done(l, base + UNITS - 1))
            hold(pe, "pe")
            for t in range(NT):
                m = P if t < 4 else DEC
                out = score[0][:, t * P:(t + 1) * P] if t < 4 else score[1][:, 0:m]
                r = turn_in(out, o_tok[0:m, t, :], const[0:m, IDENT, 0:m])
            r.then_inc(o_turned.sem, 1)

        def merge(l):
            with pe.Fori(0, KD) as m:
                whole_chunk(l, "gate", 0, 0, 2 * m, 3 * m, x_hi, x_lo)
                whole_chunk(l, "gate", 1, 1, 2 * m, 3 * m, x_hi, x_lo)
                whole_chunk(l, "gate", 0, 0, 2 * m + 1, 3 * m + 1, x_hi, x_lo)
                chunk_ready(l, "gate", 1, 2 * m + 1)
                for t0, t1, p, group in ((0, 2, 1, 1), (2, 6, 0, 2), (6, 8, 1, 2)):
                    pair_free(l, "gate", p, 3 * m + group)
                    for t in range(t0, t1):
                        pe.wait_ge(o_ready.sem, o_ready.done(l, KD - 1))
                        r = split_tile(pair[p], 1, t, o_hi[:, t, :], o_lo[:, t, :], t == t0, t == t1 - 1)
                    r.then_inc(branch_done.sem if t1 < KD else chunk_done[1].sem, 1)

        pe.wait_ge(start_in.sem, start_in.done(0, 3))
        pe.wait_ge(cond_ready.sem, cond_ready.done(0, 0))
        with pe.Fori(0, ADA_FIRST // (2 * RING)) as i:
            def weighed(s):
                pe.wait_ge(first_sums.sem, i * (RING - 1) + s + 1)
                ada_sum(first_part[:, s, :, :], (i * RING + s) * 2 + 1).then_inc(first_used.sem, 1)

            for s in range(RING):
                pe.wait_ge(first_full[s].sem, (i + 1) * 16)
                ada_product(ada_ring[:, s, 0, :], (i * RING + s) * 2)
                if s and s < RING - 1:
                    weighed(s - 1)
            ada_product(ada_ring[:, RING - 1, 1, :], i * RING * 2 + RING * 2 - 1).then_inc(last_used.sem, 1)
            weighed(RING - 2)
        with pe.Fori(0, DEPTH) as l:
            ffn(l, "a", 0, True)
            sum_squares(l, 2)
            before_pairs(l)
            pe.wait_ge(mix_ready.sem, mix_ready.done(l, 0))
            hold(pe, "pe")
            with pe.Fori(0, B_PAIRS) as b:
                stage(l, b, PAST, b * SEGS_B, triple(l, b + 2, lambda j0, j1: project(l, b + 3, j0, j1)))
            seg0 = B_PAIRS * SEGS_B
            stage(l, B_PAIRS, A_WIN, seg0, triple(l, NP, lambda j0, j1: project_u(l, j0, j1)))
            stage(l, B_PAIRS + 1, A_WIN, seg0 + SEGS_A,
                  projected(WORK_U, lambda j0, j1: project_u(l, j0 + LEAD, j1 + LEAD)))
            merge(l)
            with pe.Fori(0, KD // 2) as i:
                for p in (0, 1):
                    whole_chunk(l, "out", p, p, i, i, m_hi, m_lo,
                                gate=(lambda t: pe.wait_ge(prod_lo.sem, prod_lo.done(l, KF + t))) if p == 0 else None)
            column_sums(l, 3)
            ffn(l, "b", 2, False)

    @block.scalar
    def _(act):
        credits(act, [prob_t_ready, o_taken, acc_free[0]])
        A, copy = nc.scalar.activation, nc.scalar.copy

        def split_hi(l, ph, s, i):
            act.wait_ge(raw_full[s].sem, raw_full[s].done(l, SPLIT_AT[ph][s] + i))
            act.wait_ge(chunk_done[s].sem, chunk_done[s].free(l, SPLIT_AT[ph][s] + i))
            copy(w_hi[:, s, 0:WIDTH[ph]], raw[:, s, 0:WIDTH[ph]]).then_inc(hi_ready[s].sem, 1)

        def chunk_over(l, ph, s, i):
            act.wait_ge(chunk_done[s].sem, chunk_done[s].done(l, SPLIT_AT[ph][s] + i))

        def pairs(n, body, following):
            with act.Fori(0, n - 1) as i:
                body(i, None)
            body(n - 1, following)

        def ffn_up(l, ab, following):
            ph, at = "f1" + ab, (0 if ab == "a" else KF + KD)
            hold(act, "act")
            act.preload_act_table(ACT.Silu)

            def body(i, nxt_split):
                chunk_over(l, ph, 0, i)
                act.wait_ge(acc_free[1].sem, acc_free[1].free(l, GROUP_AT[ph][1] + i))
                A(two(sil[:, :]), pair[0], ACT.Silu).then_inc(acc_free[0].sem, 1)
                nxt_split() if nxt_split else split_hi(l, ph, 0, i + 1)
                act.wait_ge(acc_free[1].sem, acc_free[1].done(l, GROUP_AT[ph][1] + i))
                copy(tile(hid_hi, i), hid[:, :]).then_inc(prod_hi.sem, 1)
                if not nxt_split:
                    split_hi(l, ph, 1, i + 1)
            pairs(KF, body, following)

        def keep_and_square(l, ph, n, p, s, i, m):
            chunk_over(l, ph, s, i)
            act.wait_ge(sq_added.sem, sq_added.free(l, n * KD + m))
            A(two(sq[:, p, :]), pair[p], ACT.Square).then_inc(sq_ready.sem, 1)
            copy(two(tile(y, m)), pair[p]).then_inc(acc_free[p].sem, 1)

        def ffn_down(l, ab, n, following):
            ph = "f2" + ab

            def body(i, nxt_split):
                for p in (0, 1):
                    split_hi(l, ph, 1, 2 * i + p)
                    if p == 0 or not nxt_split:
                        split_hi(l, ph, 0, 2 * i + p + 1)
                    else:
                        nxt_split()
                    keep_and_square(l, ph, n, p, 1, 2 * i + p, 2 * i + p)
            pairs(KD // 2, body, following)

        def square_h(l, n, h_tile):
            for k in range(KD):
                h_tile(k)
                act.wait_ge(sq_added.sem, sq_added.free(l, n * KD + k))
                A(sq[:, k % 2, :], h[:, k, :], ACT.Square).then_inc(sq_ready.sem, 1)

        def estimate(l, n):
            act.preload_act_table_set("natural_log_exp_and_others")
            act.wait_ge(stat_ready.sem, stat_ready.done(l, n))
            A(two(rms[:, 1, :]), stat, ACT.Ln, scale=1.0 / D_MODEL, bias=eps_t[:, 0:1]).then_inc(log_ready.sem, 1)
            act.drain()
            A(rms[:, 1, :], rms[:, 1, :], ACT.Exp, scale=-0.5).then_inc(est_ready.sem, 1)

        def make_x(l, n):
            for k in range(KD):
                act.wait_ge(t_ready.sem, t_ready.done(l, n * KD + k))
                act.wait_ge(x_ready.sem, x_ready.free(l, n * KD + k))
                for g, cols in ((0, slice(0, SEQ)), (1, slice(SEQ, TOK))):
                    A(nx[:, k % 2, cols], nt[:, k % 2, cols], ACT.Identity,
                      bias=mods[:, 3 * n, k, g:g + 1], scale=pre_scale[:, n, k, g:g + 1])
                act.drain()
                copy(x_hi[:, k, :], nx[:, k % 2, :]).then_inc(nx_ready.sem, 1)

        def before_pairs(l):
            act.wait_ge(tri_done.sem, tri_done.done(l, 0))
            copy(two(nxt[:, 0, :]), pair[0]).then_inc(acc_free[0].sem, 1)
            split_hi(l, "tri", 0, 1)
            chunk_over(l, "tri", 1, 0)
            copy(two(nxt[:, 2, :]), pair[0]).then_inc(acc_free[0].sem, 1)
            act.drain()
            act.sem_inc(nxt_full.sem, 2)
            split_hi(l, "tri", 1, 1)
            act.preload_act_table(ACT.Exp)
            act.wait_ge(f_neg.sem, f_neg.done(l, 0))
            A(fx[:, 2, :, :], fx[:, 1, :, :], ACT.Exp).then_inc(f_exp.sem, 1)
            act.wait_ge(vc_turned.sem, vc_turned.done(l, 0))
            for t in range(NT):
                m = P if t < 4 else DEC
                src = ps[0:m, 5 + t // 2, (t % 2) * 256:(t % 2) * 256 + 256]
                A(v_tok_c[0:m, t, :], src, ACT.Square, accum_out=c_stat[0:m, 0, t:t + 1])
            act.drain()
            for t in range(NT):
                m = P if t < 4 else DEC
                src = ps[0:m, 5 + t // 2, (t % 2) * 256:(t % 2) * 256 + 256]
                copy(v_tok_c[0:m, t, :], src)
            act.drain()
            A(c_stat[:, 1, :], c_stat[:, 0, :], ACT.Sqrt, scale=1.0 / 256, bias=eps_t[:, 0:1]
              ).then_inc(vc_copied.sem, 1)
            take_q(l, 1)
            split_hi(l, "tri", 0, 2)
            act.wait_ge(f_sums.sem, f_sums.done(l, 0))
            nc.scalar.mul(f_rows[:, 0:SEQ], ps[0:B_HEADS, 7, :], -1.0)
            copy(f_rows[:, SEQ:SEQ + PAST].rearrange("p (b n) -> p b n", b=2), ps[0:B_HEADS, 5:7, :])
            nc.scalar.mul(f_rows[:, SEQ + PAST:SEQ + SC], ps[0:B_HEADS, 4, 128:128 + DEC], -1.0)
            copy(f_query[:, 0:4, :].rearrange("p t h -> p (t h)"), ps[:, 4, 64:96])
            copy(f_query[0:DEC, 4, :], ps[0:DEC, 4, 96:104]).then_inc(f_rows_ready.sem, 1)
            take_v(l, 1)
            stage_q(l, 0)
            act.preload_act_table(ACT.Exp)

        def take_q(l, T):
            act.wait_ge(tri_done.sem, tri_done.done(l, 2 * T))
            nc.scalar.mul(two(nxt[:, 0, :]), pair[0], HD ** -0.5).then_inc(acc_free[0].sem, 1)

        def take_v(l, T):
            chunk_over(l, "tri", 1, T)
            act.wait_ge(kv_free.sem, kv_free.free(l, T - 1))
            hold(act, "act")
            copy(two(v_st[:, :]), pair[0]).then_inc(acc_free[0].sem, 1)
            act.drain()
            act.sem_inc(v_staged.sem, 1)

        def stage_q(l, st):
            copy(q_st[:, :], nxt[:, 0, :]).then_inc(q_staged.sem, 1)

        def stage(l, st, cached, o_tile, second, third, last):
            base = st * UNITS
            second()
            act.wait_ge(v_turned.sem, v_turned.done(l, st))
            copy(v_tok[:, 0:4, :].rearrange("p t n -> p (t n)"), turned)
            copy(v_tok[0:DEC, 4, :], att_out[0:DEC, 0:P]).then_inc(v_ready.sem, 1)

            def expo(u):
                hh, i, m, nk, nb, _ = unit_shape(u, cached)
                p = u % PROBS
                act.wait_ge(shift_ready.sem, shift_ready.done(l, base + u))
                A(prob[0:m, p, 0:nk], prob[0:m, p, 0:nk], ACT.Exp, bias=row[0:m, 1, p:p + 1],
                  accum_out=row[0:m, 2, p:p + 1]).then_inc(exp_ready.sem, 1)

            def take_turned(u):
                hh, i, m, nk, nb, _ = unit_shape(u, cached)
                n = base + u
                act.wait_ge(prob_turned.sem, prob_turned.done(l, n))
                act.wait_ge(o_summed.sem, o_summed.free(l, n))
                part = nk % P
                full = nb - 1 if part else nb
                r = copy(prob_t[:, u % 2, 0:full * m], turned[:, 0:full * m])
                if part:
                    src = turned[0:part, full * m:nb * m] if full < 8 else att_out[0:part, 256:256 + m]
                    r = copy(prob_t[0:part, u % 2, full * m:nb * m], src)
                r.then_inc(prob_t_ready.sem, 1)

            def take_o(u):
                hh, i, m, nk, nb, _ = unit_shape(u, cached)
                n = base + u
                act.wait_ge(inv_ready.sem, inv_ready.done(l, n))
                act.wait_ge(o_summed.sem, o_summed.done(l, n))
                A(o_tok[0:m, i, hh * HD:hh * HD + HD], att_out[0:m, 0:HD], ACT.Copy,
                  scale=row[0:m, 3, u % PROBS:u % PROBS + 1]).then_inc(o_taken.sem, 1)

            expo(0)
            expo(1)
            for u in range(UNITS):
                take_turned(u)
                if u + 2 < UNITS:
                    expo(u + 2)
                if u == UNITS - 2 and last:
                    take_v(l, st + 2)
                take_o(u)
                if u == 1 and last:
                    take_q(l, st + 2)
                if u == 4:
                    third()
            if last:
                stage_q(l, st + 1)
            act.wait_ge(o_turned.sem, o_turned.done(l, st))
            hold(act, "act")
            copy(o_hi[:, bass.ds(o_tile, 1), 0:SEQ].rearrange("p a n -> p (a n)"), score[0])
            copy(o_hi[:, bass.ds(o_tile, 1), SEQ:TOK].rearrange("p a n -> p (a n)"), score[1][:, 0:DEC]
                 ).then_inc(o_high.sem, 1)

        def merge(l):
            act.preload_act_table(ACT.Sigmoid)

            def body(m, nxt_split):
                g0, g1 = GROUP_AT["gate"]
                for br, (s, i, used, group) in enumerate(((0, 2 * m, 1, g1 + 3 * m - 2), (1, 2 * m, 0, g0 + 3 * m - 1),
                                                          (0, 2 * m + 1, 1, g1 + 3 * m - 1))):
                    if br == 0:
                        split_hi(l, "gate", 1, 2 * m)
                    elif br == 1:
                        split_hi(l, "gate", 0, 2 * m + 1)
                    else:
                        split_hi(l, "gate", 1, 2 * m + 1)
                    chunk_over(l, "gate", s, i)
                    act.wait_ge(acc_free[used].sem, acc_free[used].done(l, group))
                    A(two(sig[:, br, :]), pair[s], ACT.Sigmoid, bias=b_gate[:, br, bass.ds(m, 1)]
                      ).then_inc(acc_free[s].sem, 1)
                nxt_split() if nxt_split else split_hi(l, "gate", 0, 2 * m + 2)
                act.wait_ge(merged.sem, merged.done(l, m))
                copy(tile(m_hi, m), msum[:, :]).then_inc(prod_hi.sem, 1)
            pairs(KD, body, lambda: split_hi(l, "out", 0, 0))

        act.wait_ge(start_in.sem, start_in.done(0, 3))
        A(cond_s[:, :, :], cond[:, :, :], ACT.Silu).then_inc(cond_ready.sem, 1)
        act.drain()
        act.wait_ge(eps_ready.sem, eps_ready.done(0, 0))
        with act.Fori(0, DEPTH) as l:
            for s in (0, 1):
                split_hi(l, "f1a", s, 0)
            square_h(l, 0, lambda k: act.wait_ge(h_ready.sem, l * h_ready.per_layer + k + 1))
            estimate(l, 0)
            make_x(l, 0)
            ffn_up(l, "a", lambda: split_hi(l, "f2a", 0, 0))
            ffn_down(l, "a", 1, lambda: split_hi(l, "tri", 0, 0))
            split_hi(l, "tri", 1, 0)
            estimate(l, 1)
            square_h(l, 2, lambda k: act.wait_ge(h_ready.sem, h_ready.done(l, k) + KD))
            estimate(l, 2)
            make_x(l, 1)
            before_pairs(l)
            with act.Fori(0, B_PAIRS) as b:
                stage(l, b, PAST, b + A_PAIRS, lambda: split_hi(l, "tri", 1, b + 2),
                      lambda: split_hi(l, "tri", 0, b + 3), True)
            stage(l, B_PAIRS, A_WIN, 0, lambda: split_hi(l, "tri", 1, NP), lambda: split_hi(l, "uc", 0, 0), True)
            stage(l, B_PAIRS + 1, A_WIN, 1, lambda: split_hi(l, "uc", 1, 0), lambda: split_hi(l, "gate", 0, 0), False)
            for c in (0, 1):
                act.wait_ge(oc_made.sem, oc_made.done(l, c))
                copy(o_hi[:, NP + c, :], nxt[:, c, :]).then_inc(o_high.sem, 1)
            act.wait_ge(kv_free.sem, kv_free.done(l, NP - 1))
            hold(act, "act")
            merge(l)

            def out_pair(i, nxt_split):
                split_hi(l, "out", 1, i)
                keep_and_square(l, "out", 3, 0, 0, i, 2 * i)
                nxt_split() if nxt_split else split_hi(l, "out", 0, i + 1)
                keep_and_square(l, "out", 3, 1, 1, i, 2 * i + 1)
            pairs(KD // 2, out_pair, lambda: split_hi(l, "f1b", 0, 0))
            estimate(l, 3)
            split_hi(l, "f1b", 1, 0)
            square_h(l, 4, lambda k: act.wait_ge(h_ready.sem, h_ready.done(l, KD + k) + KD))
            estimate(l, 4)
            make_x(l, 2)
            ffn_up(l, "b", lambda: split_hi(l, "f2b", 0, 0))
            ffn_down(l, "b", 5, lambda: None)
            estimate(l, 5)

    @block.vector
    def _(dve):
        credits(dve, lo_ready + [acc_free[1], prod_lo, sq_added, x_ready, scores_taken, ada_read, small_used, o_ready])
        V = nc.vector

        def split_lo(l, ph, s, i):
            w = WIDTH[ph]
            dve.wait_ge(hi_ready[s].sem, hi_ready[s].done(l, SPLIT_AT[ph][s] + i))
            V.tensor_tensor(w_lo[:, s, 0:w], raw[:, s, 0:w], w_hi[:, s, 0:w], ALU.subtract
                            ).then_inc(lo_ready[s].sem, 1)

        def pairs(n, body, following):
            with dve.Fori(0, n - 1) as i:
                body(i, None)
            body(n - 1, following)

        def ffn_up(l, ab, following):
            ph, at = "f1" + ab, (0 if ab == "a" else KF + KD)

            def body(i, nxt_split):
                if ab == "a":
                    weigh_ada(l, i)
                nxt_split() if nxt_split else split_lo(l, ph, 0, i + 1)
                dve.wait_ge(acc_free[0].sem, acc_free[0].done(l, GROUP_AT[ph][0] + i))
                dve.wait_ge(chunk_done[1].sem, chunk_done[1].done(l, SPLIT_AT[ph][1] + i))
                dve.wait_ge(prod_lo.sem, prod_lo.free(l, at + i))
                V.tensor_tensor(two(hid[:, :]), two(sil[:, :]), pair[1], ALU.mult).then_inc(acc_free[1].sem, 1)
                dve.wait_ge(prod_hi.sem, prod_hi.done(l, at + i))
                V.tensor_tensor(tile(hid_lo, i), hid[:, :], tile(hid_hi, i), ALU.subtract
                                ).then_inc(prod_lo.sem, 1)
                if not nxt_split:
                    split_lo(l, ph, 1, i + 1)
            pairs(KF, body, following)

        def add_squares(l, n, p, m):
            dve.wait_ge(sq_ready.sem, sq_ready.done(l, n * KD + m))
            dve.wait_ge(sq_added.sem, sq_added.done(l, n * KD + m - 1))
            V.tensor_tensor(acc[:, :], acc[:, :], sq[:, p, :], ALU.add).then_inc(sq_added.sem, 1)

        def clear_acc():
            V.memset(acc[:, :], 0.0)
            dve.drain()

        def ffn_down(l, ab, n, following):
            ph = "f2" + ab

            def body(i, nxt_split):
                for p in (0, 1):
                    split_lo(l, ph, 1, 2 * i + p)
                    if p == 0 and ab == "a":
                        weigh_ada(l, i + KF)
                    if p == 0 or not nxt_split:
                        split_lo(l, ph, 0, 2 * i + p + 1)
                    else:
                        nxt_split()
                    add_squares(l, n, p, 2 * i + p)
            clear_acc()
            pairs(KD // 2, body, following)

        def inverse_rms(l, n):
            dve.wait_ge(stat_ready.sem, stat_ready.done(l, n))
            if n % 2 == 0:
                dve.sem_inc(sq_added.sem, 1)
            dve.wait_ge(log_ready.sem, log_ready.done(l, n))
            V.tensor_scalar(two(rms[:, 0, :]), stat, 1.0 / D_MODEL, EPS, ALU.mult, ALU.add)
            dve.drain()
            dve.wait_ge(est_ready.sem, est_ready.done(l, n))
            V.scalar_tensor_tensor(out=rms[:, 2, :], in0=rms[:, 0, :], scalar=-0.5, in1=rms[:, 1, :],
                                   op0=ALU.mult, op1=ALU.mult)
            dve.drain()
            V.tensor_tensor(rms[:, 2, :], rms[:, 2, :], rms[:, 1, :], ALU.mult)
            dve.drain()
            V.scalar_tensor_tensor(out=rms[:, 3, :], in0=rms[:, 2, :], scalar=1.5, in1=rms[:, 1, :],
                                   op0=ALU.add, op1=ALU.mult)
            dve.drain()

        def x_low(l, n, k):
            dve.wait_ge(nx_ready.sem, nx_ready.done(l, n * KD + k))
            V.tensor_tensor(x_lo[:, k, :], nx[:, k % 2, :], x_hi[:, k, :], ALU.subtract
                            ).then_inc(x_ready.sem, 1)

        def make_x(l, n):
            for k in range(KD):
                V.tensor_tensor(nt[:, k % 2, :], h[:, k, :], rms[:, 3, :], ALU.mult).then_inc(t_ready.sem, 1)
                if k:
                    x_low(l, n, k - 1)
            x_low(l, n, KD - 1)

        def residual(l, n):
            for k in range(KD):
                V.tensor_tensor(nt[:, k % 2, :], y[:, k, :], rms[:, 3, :], ALU.mult)
                dve.drain()
                for g, cols in ((0, slice(0, SEQ)), (1, slice(SEQ, TOK))):
                    r = V.scalar_tensor_tensor(out=h[:, k, cols], in0=nt[:, k % 2, cols],
                                               scalar=post_gate[:, n, k, g:g + 1], in1=h[:, k, cols],
                                               op0=ALU.mult, op1=ALU.add)
                r.then_inc(h_ready.sem, 1)

        def weigh(tile_in, part, done):
            for k in range(KD):
                w = tile_in[:, k * P:(k + 1) * P]
                for g in (0, 1):
                    out, c = part[:, g, :], cond_s[:, k, g:g + 1]
                    if k:
                        V.scalar_tensor_tensor(out=out, in0=w, scalar=c, in1=out, op0=ALU.mult, op1=ALU.add)
                    else:
                        V.tensor_scalar(out, w, c, None, ALU.mult)
                dve.drain()
            dve.sem_inc(done.sem, 1)

        def weigh_ada(l, i):
            dve.wait_ge(ada_full[1].sem, ada_full[1].done(l, i))
            hold(dve, "dve")
            weigh(ada_w[:, 1, :], ada_part, ada_sums)

        def take_ada(first, n):
            mine = ada_all[:, bass.ds(first, n), :]
            V.tensor_tensor(mine, ada_ps[:, 0:2 * n].rearrange("p (n g) -> p n g", g=2), mine, ALU.add)
            dve.drain()
            dve.sem_inc(ada_read.sem, 1)

        def fold_mods(l, parts):
            for j0, j1 in ((0, 2),) if parts == "first" else ((2, N_MOD),):
                V.tensor_copy(mods[:, j0:j1, :, :].rearrange("p m k g -> p (m k g)"),
                              ada_all[:, bass.ds(l * N_ADA + j0 * KD, (j1 - j0) * KD), :]
                              .rearrange("p n g -> p (n g)"))
            dve.drain()
            for n in ([0] if parts == "first" else [1, 2]):
                for g in (0, 1):
                    V.scalar_tensor_tensor(out=pre_scale[:, n, :, g], in0=mods[:, 3 * n + 1, :, g], scalar=1.0,
                                           in1=norm_g[:, 2 * n, :], op0=ALU.add, op1=ALU.mult)
            if parts != "first":
                for n in range(3):
                    for g in (0, 1):
                        V.scalar_tensor_tensor(out=post_gate[:, n, :, g], in0=mods[:, 3 * n + 2, :, g],
                                               scalar=1.0 if n == 1 else 0.5,
                                               in1=norm_g[:, 2 * n + 1, :], op0=ALU.mult, op1=ALU.mult)
            dve.drain()

        def forget(l):
            dve.wait_ge(mix_in.sem, mix_in.done(l, 5))
            V.memset(fx[:, 0, :, :], 0.0)
            dve.drain()
            dve.wait_ge(logits_turned.sem, logits_turned.done(l, 0))
            V.tensor_copy(fx[:, 0, 0:4, :].rearrange("p t h -> p (t h)"), ps[:, 4, 0:32])
            V.tensor_copy(fx[0:DEC, 0, 4, :], ps[0:DEC, 4, 32:40])
            dve.drain()
            bias = b_forget[:, :].rearrange("p (a h) -> p a h", a=1).to_broadcast((P, NT, B_HEADS))
            x, na, e, z, z2, pl = (fx[:, k, :, :] for k in range(6))
            V.tensor_tensor(x, x, bias, ALU.add)
            dve.drain()
            V.tensor_scalar(z, x, -1.0, None, ALU.mult)
            dve.drain()
            V.tensor_tensor(na, x, z, ALU.min).then_inc(f_neg.sem, 1)
            dve.wait_ge(f_exp.sem, f_exp.done(l, 0))
            V.tensor_scalar(z2, e, 2.0, None, ALU.add)
            dve.drain()
            V.reciprocal(z2, z2)
            dve.drain()
            V.tensor_tensor(z, e, z2, ALU.mult)
            dve.drain()
            V.tensor_tensor(z2, z, z, ALU.mult)
            dve.drain()
            V.tensor_scalar(pl, z2, 1.0 / 17, None, ALU.mult)
            for odd in (15, 13, 11, 9, 7, 5, 3):
                dve.drain()
                V.scalar_tensor_tensor(out=pl, in0=pl, scalar=1.0 / odd, in1=z2, op0=ALU.add, op1=ALU.mult)
            dve.drain()
            V.scalar_tensor_tensor(out=pl, in0=pl, scalar=1.0, in1=z, op0=ALU.add, op1=ALU.mult)
            V.tensor_scalar(x, x, 0.0, None, ALU.min)
            dve.drain()
            V.scalar_tensor_tensor(out=logf[:, :, :], in0=pl, scalar=-2.0, in1=x, op0=ALU.mult, op1=ALU.add)
            dve.drain()
            V.tensor_copy(earlier_f[:, 1, :], logf[:, 0, :])
            V.tensor_copy(later_f[:, 6, :], cache_f[:, 7, :])
            for t in range(2, 4):
                dve.drain()
                V.tensor_tensor(earlier_f[:, t, :], earlier_f[:, t - 1, :], logf[:, t - 1, :], ALU.add)
            for t in range(5, -1, -1):
                dve.drain()
                r = V.tensor_tensor(later_f[:, t, :], later_f[:, t + 1, :], cache_f[:, t + 1, :], ALU.add)
            r.then_inc(f_sums_in.sem, 1)

        def before_pairs(l):
            dve.wait_ge(tri_done.sem, tri_done.done(l, 1))
            V.tensor_copy(two(nxt[:, 1, :]), pair[1]).then_inc(acc_free[1].sem, 1)
            dve.drain()
            dve.sem_inc(nxt_full.sem, 1)
            split_lo(l, "tri", 0, 1)
            split_lo(l, "tri", 1, 1)
            forget(l)
            mask = const[:, TRI_LE:TRI_LE + 1, :].to_broadcast((P, C_GROUPS, P))
            V.tensor_tensor(w_mix[:, :, :], w_mix[:, :, :], mask, ALU.mult)
            dve.wait_ge(vc_copied.sem, vc_copied.done(l, 0))
            V.reciprocal(c_stat[:, 2, :], c_stat[:, 1, :])
            dve.drain()
            for t in range(NT):
                m = P if t < 4 else DEC
                r = V.scalar_tensor_tensor(out=v_tok_c[0:m, t, :], in0=v_tok_c[0:m, t, :],
                                           scalar=c_stat[0:m, 2, t:t + 1], in1=c_gain[0:m, :],
                                           op0=ALU.mult, op1=ALU.mult)
            r.then_inc(vc_ready.sem, 1)
            split_lo(l, "tri", 0, 2)
            take_k(l, 1)
            dve.wait_ge(mixed.sem, mixed.done(l, 0))
            for T in (0, 1):
                V.tensor_tensor(c_mix[:, T, 0:SEQ].rearrange("p (t n) -> p t n", t=4),
                                ps[:, 5 + T, :].rearrange("p (t n) -> p t n", t=4),
                                c_bias[:, T:T + 1, :].to_broadcast((P, 4, P)), ALU.add)
                r = V.tensor_tensor(c_mix[:, T, SEQ:TOK], ps[:, 7, T * DEC:(T + 1) * DEC], c_bias[:, T, 0:DEC],
                                    ALU.add)
            r.then_inc(mix_ready.sem, 1)
            stage_k(l, 0)

        def take_k(l, T):
            dve.wait_ge(tri_done.sem, tri_done.done(l, 2 * T + 1))
            V.tensor_copy(two(nxt[:, 1, :]), pair[1]).then_inc(acc_free[1].sem, 1)
            dve.drain()

        def stage_k(l, st):
            dve.wait_ge(o_summed.sem, o_summed.done(l, st * UNITS - 1))
            dve.wait_ge(kv_free.sem, kv_free.free(l, st))
            hold(dve, "dve")
            V.tensor_copy(k_st[:, :], nxt[:, 1, :]).then_inc(k_staged.sem, 1)

        def stage(l, st, cached, seg0, o_tile, second, third, last):
            base = st * UNITS
            is_b = cached == PAST
            def logits(u):
                hh, i, m, nk, nb, segs = unit_shape(u, cached)
                n, p, s0 = base + u, u % PROBS, first_segment(u, cached)
                dve.wait_ge(prob_turned.sem, prob_turned.done(l, base + last_user(u)))
                if is_b and hh == 0 and i in (0, 4):
                    sem = decay_s_in if i else decay_p_in
                    dve.wait_ge(sem.sem, sem.done(l, st))
                if not is_b and u == 0:
                    dve.wait_ge(strip_in.sem, strip_in.done(l, st - B_PAIRS))
                for e, (c0, c1) in enumerate(segs):
                    out, bank = prob[0:m, p, c0:c1], score[(s0 + e) % 2][0:m, 0:c1 - c0]
                    dve.wait_ge(scores_ready.sem, scores_ready.done(l, seg0 + s0 + e))
                    if is_b:
                        d = (decay_p if i < 4 else decay_s)[0:m, hh, c0:c1]
                        V.scalar_tensor_tensor(out=out, in0=d, scalar=f_query[0:m, i, bass.ds(st * 2 + hh, 1)],
                                               in1=bank, op0=ALU.add, op1=ALU.add).then_inc(scores_taken.sem, 1)
                    else:
                        c = c0 + (512 - P * i if i < 4 else 0)
                        V.tensor_tensor(out, bank, strip[0:m, hh, c:c + c1 - c0], ALU.add
                                        ).then_inc(scores_taken.sem, 1)
                dve.drain()
                if is_b:
                    diag = prob[0:m, p, nk - m:nk]
                    V.tensor_tensor(diag, diag, mask[0:m, CAUSAL, 0:m], ALU.add)
                    dve.drain()
                V.reduce_max(row[0:m, 0, p:p + 1], prob[0:m, p, 0:nk], AXX)
                dve.drain()
                V.tensor_scalar(row[0:m, 1, p:p + 1], row[0:m, 0, p:p + 1], -1.0, None, ALU.mult
                                ).then_inc(shift_ready.sem, 1)

            def inverse(u):
                m, p = unit_shape(u, cached)[2], u % PROBS
                dve.wait_ge(exp_ready.sem, exp_ready.done(l, base + u))
                V.reciprocal(row[0:m, 3, p:p + 1], row[0:m, 2, p:p + 1]).then_inc(inv_ready.sem, 1)

            logits(0)
            logits(1)
            second()
            for u in range(UNITS):
                inverse(u)
                if u + 2 < UNITS:
                    logits(u + 2)
                if u == 5:
                    third()
                if u == 6 and last:
                    take_k(l, st + 2)
            if last:
                stage_k(l, st + 1)
            dve.wait_ge(o_high.sem, o_high.done(l, st))
            hold(dve, "dve")
            for bank, cols in ((score[0], slice(0, SEQ)), (score[1][:, 0:DEC], slice(SEQ, TOK))):
                o = [t[:, bass.ds(o_tile, 1), cols].rearrange("p a n -> p (a n)") for t in (o_hi, o_lo)]
                r = V.tensor_tensor(o[1], bank, o[0], ALU.subtract)
            r.then_inc(o_ready.sem, 1)

        def merge(l):
            def body(m, nxt_split):
                g0, g1 = GROUP_AT["gate"]
                split_lo(l, "gate", 1, 2 * m)
                split_lo(l, "gate", 0, 2 * m + 1)
                split_lo(l, "gate", 1, 2 * m + 1)
                nxt_split() if nxt_split else split_lo(l, "gate", 0, 2 * m + 2)
                dve.wait_ge(acc_free[0].sem, acc_free[0].done(l, g0 + 3 * m))
                dve.wait_ge(branch_done.sem, branch_done.done(l, 2 * m))
                dve.wait_ge(prod_lo.sem, prod_lo.free(l, KF + m))
                V.tensor_tensor(two(msum[:, :]), two(sig[:, 0, :]), pair[1], ALU.mult).then_inc(acc_free[1].sem, 1)
                dve.wait_ge(acc_free[1].sem, acc_free[1].done(l, g1 + 3 * m))
                dve.wait_ge(branch_done.sem, branch_done.done(l, 2 * m + 1))
                V.tensor_tensor(two(mtmp[:, :]), two(sig[:, 1, :]), pair[0], ALU.mult).then_inc(acc_free[0].sem, 1)
                dve.drain()
                V.tensor_tensor(msum[:, :], msum[:, :], mtmp[:, :], ALU.add)
                dve.drain()
                dve.wait_ge(acc_free[0].sem, acc_free[0].done(l, g0 + 3 * m + 1))
                dve.wait_ge(chunk_done[1].sem, chunk_done[1].done(l, SPLIT_AT["gate"][1] + 2 * m + 1))
                V.tensor_tensor(two(mtmp[:, :]), two(sig[:, 2, :]), pair[1], ALU.mult).then_inc(acc_free[1].sem, 1)
                dve.drain()
                V.tensor_tensor(msum[:, :], msum[:, :], mtmp[:, :], ALU.add).then_inc(merged.sem, 1)
                dve.wait_ge(prod_hi.sem, prod_hi.done(l, KF + m))
                V.tensor_tensor(tile(m_lo, m), msum[:, :], tile(m_hi, m), ALU.subtract).then_inc(prod_lo.sem, 1)
            pairs(KD, body, lambda: split_lo(l, "out", 0, 0))

        V.memset(c_stat[:, :, :], 1.0)
        dve.drain()
        V.memset(eps_t[:, :], EPS).then_inc(eps_ready.sem, 1)
        dve.wait_ge(start_in.sem, start_in.done(0, 3))
        dve.sem_inc(h_ready.sem, KD)
        dve.wait_ge(cond_ready.sem, cond_ready.done(0, 0))
        hold(dve, "dve")
        with dve.Fori(0, ADA_FIRST // (2 * RING)) as i:
            for s in range(RING - 1):
                dve.wait_ge(first_full[s].sem, (i + 1) * 16)
                hold(dve, "dve")
                weigh(ada_ring[:, s, 1, :], first_part[:, s, :, :], first_sums)
        dve.wait_ge(first_used.sem, ADA_FIRST // (2 * RING) * (RING - 1) + first_used.slots)
        dve.wait_ge(last_used.sem, ADA_FIRST // (2 * RING) + last_used.slots)
        take_ada(0, ADA_FIRST)
        with dve.Fori(0, DEPTH) as l:
            dve.wait_ge(small_in.sem, small_in.done(l, 1))
            hold(dve, "dve")
            fold_mods(l, "first")
            for s in (0, 1):
                split_lo(l, "f1a", s, 0)
            inverse_rms(l, 0)
            make_x(l, 0)
            ffn_up(l, "a", lambda: split_lo(l, "f2a", 0, 0))
            ffn_down(l, "a", 1, lambda: split_lo(l, "tri", 0, 0))
            split_lo(l, "tri", 1, 0)
            for s in (0, 1):
                dve.wait_ge(ada_used[s].sem, ada_used[s].done(l, ADA_N[s] - 1))
            hold(dve, "dve")
            take_ada(l * ADA_LAYER + ADA_FIRST, ADA_LAYER)
            fold_mods(l, "rest")
            inverse_rms(l, 1)
            residual(l, 0)
            inverse_rms(l, 2)
            make_x(l, 1)
            before_pairs(l)
            with dve.Fori(0, B_PAIRS) as b:
                stage(l, b, PAST, b * SEGS_B, b + A_PAIRS, lambda: split_lo(l, "tri", 1, b + 2),
                      lambda: split_lo(l, "tri", 0, b + 3), True)
            seg0 = B_PAIRS * SEGS_B
            stage(l, B_PAIRS, A_WIN, seg0, 0, lambda: split_lo(l, "tri", 1, NP), lambda: split_lo(l, "uc", 0, 0), True)
            stage(l, B_PAIRS + 1, A_WIN, seg0 + SEGS_A, 1, lambda: split_lo(l, "uc", 1, 0),
                  lambda: split_lo(l, "gate", 0, 0), False)
            for c in (0, 1):
                dve.wait_ge(chunk_done[c].sem, chunk_done[c].done(l, SPLIT_AT["uc"][c]))
                V.tensor_tensor(two(nxt[:, c, :]), two(c_mix[:, c, :]), pair[c], ALU.mult
                                ).then_inc(acc_free[c].sem, 1)
            dve.drain()
            dve.sem_inc(oc_made.sem, 2)
            for c in (0, 1):
                dve.wait_ge(o_high.sem, o_high.done(l, NP + c))
                V.tensor_tensor(o_lo[:, NP + c, :], nxt[:, c, :], o_hi[:, NP + c, :], ALU.subtract
                                ).then_inc(o_ready.sem, 1)
            dve.wait_ge(kv_free.sem, kv_free.done(l, NP - 1))
            hold(dve, "dve")
            merge(l)
            clear_acc()

            def out_pair(i, nxt_split):
                split_lo(l, "out", 1, i)
                add_squares(l, 3, 0, 2 * i)
                nxt_split() if nxt_split else split_lo(l, "out", 0, i + 1)
                add_squares(l, 3, 1, 2 * i + 1)
            pairs(KD // 2, out_pair, lambda: split_lo(l, "f1b", 0, 0))
            inverse_rms(l, 3)
            residual(l, 1)
            split_lo(l, "f1b", 1, 0)
            inverse_rms(l, 4)
            make_x(l, 2)
            ffn_up(l, "b", lambda: split_lo(l, "f2b", 0, 0))
            ffn_down(l, "b", 5, lambda: None)
            inverse_rms(l, 5)
            residual(l, 2)
            dve.drain()
            dve.sem_inc(small_used.sem, 1)

    @block.gpsimd
    def _(pool):
        pool.sem_inc(kv_free.sem, kv_free.slots)

        def dma(dst, src, signal):
            hold(pool, "pool")
            nc.gpsimd.dma_start(dst, src).then_inc(signal.sem, 16)

        def row_of(name, index):
            return ins[name][bass.ds(index, 1), :, :].rearrange("a p n -> (a p) n")

        def ada_load(l, i, n):
            pool.wait_ge(ada_used[0].sem, ada_used[0].free(l, i))
            dma(ada_w[:, 0, :], row_of("ada", l * ADA_LAYER + ADA_FIRST + n), ada_full[0])

        def caches(l, ab, index):
            n = PAST if ab == "b" else A_WIN
            dma(cache_k[:, 0:n], row_of("ck_" + ab, index), ck_in)
            dma(cache_v[:, 0:n // P, :].rearrange("p t n -> p (t n)"), row_of("cv_" + ab, index), cv_in)

        def strip_rows(l, a):
            dma(strip[:, :, :].rearrange("p a n -> p (a n)"), row_of("strip", l * A_PAIRS + a), strip_in)

        def decay_rows(l, b, dst, c0, c1, signal):
            src = scratch[bass.ds(l, 1), bass.ds(b * 2, 2), c0:c1].rearrange("a h n -> (a h) n")
            dma(dst[:, :, :], src.partition_broadcast(P), signal)

        def mixer_inputs(l):
            pool.wait_ge(chunk_done[1].sem, chunk_done[1].done(l, SPLIT_AT["f2a"][1] + KD - 1))
            dma(w_mix[:, :, :].rearrange("p g n -> p (g n)"), row_of("c_spatial", l), mix_in)
            dma(cache_f[:, :, :].rearrange("p t h -> p (t h)"), row_of("cache_f", l), mix_in)
            dma(b_forget[:, :], row_of("b_forget", l), mix_in)
            dma(c_gain[:, :], row_of("c_gain", l), mix_in)
            dma(c_bias[:, :, :].rearrange("p t n -> p (t n)"), row_of("c_bias", l), mix_in)
            dma(mask[:, :, :], ins["mask"], mix_in)
            caches(l, "b", l * B_PAIRS)
            pool.wait_ge(f_sums_in.sem, f_sums_in.done(l, 0))
            dma(outs["logf"][bass.ds(l, 1), :, :].rearrange("a p n -> (a p) n"),
                logf[:, :, :].rearrange("p t h -> p (t h)"), out_small)
            pool.wait_ge(f_rows_ready.sem, f_rows_ready.done(l, 0))
            dma(scratch[bass.ds(l, 1), :, :].rearrange("a h n -> (a h) n"), f_rows[:, :], rows_out)
            pool.wait_ge(vc_ready.sem, vc_ready.done(l, 0))
            dma(outs["vc"][bass.ds(l, 1), :, :].rearrange("a p n -> (a p) n"), v_tok_c[0:DEC, 4, :], out_small)
            pool.wait_ge(rows_out.sem, rows_out.done(l, 0))
            pool.wait_ge(mix_ready.sem, mix_ready.done(l, 0))
            pool.wait_ge(out_small.sem, out_small.done(l, 1))
            decay_rows(l, 0, decay_s, SEQ, SEQ + SC, decay_s_in)
            decay_rows(l, 0, decay_p, 0, SEQ, decay_p_in)

        def stage(l, st, k_tile, v_tile, after):
            for staged, src, t in ((k_staged, k_st, k_tile), (v_staged, v_st, v_tile)):
                pool.wait_ge(staged.sem, staged.done(l, st))
                dma(outs["kv"][bass.ds(l, 1), :, bass.ds(t, 1), :].rearrange("a p t n -> (a p) (t n)"), src[:, :],
                    out_kv)
            pool.wait_ge(out_kv.sem, out_kv.done(l, 2 * st + 1))
            pool.sem_inc(kv_free.sem, 1)
            if after is None:
                return
            pool.wait_ge(o_summed.sem, o_summed.done(l, st * UNITS + SAMPLE))
            if after == "b":
                pool.wait_ge(shift_ready.sem, shift_ready.done(l, st * UNITS + SAMPLE))
                caches(l, "b", l * B_PAIRS + st + 1)
                decay_rows(l, st + 1, decay_s, SEQ, SEQ + SC, decay_s_in)
            else:
                caches(l, "a", l * A_PAIRS + st + 1 - B_PAIRS)
            pool.wait_ge(shift_ready.sem, shift_ready.done(l, st * UNITS + UNITS - 1))
            if after == "b":
                decay_rows(l, st + 1, decay_p, 0, SEQ, decay_p_in)
            else:
                strip_rows(l, st + 1 - B_PAIRS)

        with pool.Fori(0, DEPTH) as l:
            with pool.Fori(0, KF) as i:
                ada_load(l, i, i * ADA_UP)
            with pool.Fori(0, KD // 2) as i:
                for p in (0, 1):
                    ada_load(l, i * 2 + p + KF, i * ADA_DOWN + ADA_UP * KF + 2 * p)
            mixer_inputs(l)
            with pool.Fori(0, B_PAIRS - 1) as b:
                stage(l, b, b + 4, b + 8, "b")
            stage(l, B_PAIRS - 1, B_PAIRS + 3, B_PAIRS + 7, "a")
            stage(l, B_PAIRS, 0, 2, "a")
            stage(l, B_PAIRS + 1, 1, 3, None)
        pool.wait_ge(h_ready.sem, h_ready.done(DEPTH - 1, 3 * KD - 1) + KD)
        dma(outs["h"], h[:, :, :], out_h)
        pool.wait_ge(out_h.sem, 16)
        pool.wait_ge(out_kv.sem, DEPTH * out_kv.per_layer * 16)
        pool.wait_ge(out_small.sem, out_small.done(DEPTH - 1, 1))
        pool.wait_ge(roll_out.sem, roll_out.done(DEPTH - 1, 1))

    block_ctx.__exit__(None, None, None)


def constants():
    j, k = np.arange(P)[:, None], np.arange(P)[None, :]
    out = np.zeros((P, NCONST, P), np.float32)
    out[:, IDENT] = j == k
    out[:, ONES] = 1.0
    out[:, TRI_LE] = j <= k
    mask = np.zeros((P, NMASK, P), np.float32)
    mask[:, TRI_GT] = j > k
    mask[:, CAUSAL] = np.where(k > j, np.float32(NEG), np.float32(0))
    return out, mask


def tiles(w, k_tiles, chunks):
    n, rows, cols = w.shape
    kt = k_tiles // chunks
    w = w.reshape(n, chunks, kt, P, cols // P, P)
    return np.ascontiguousarray(w.transpose(0, 4, 1, 3, 2, 5)).reshape(n * (cols // P) * chunks, P, kt * P)


def layout(v):
    f = {k: np.asarray(x) for k, x in v.items()}
    g = {}
    x = np.concatenate([f["x_prompt"][0], f["x_sample"][0]], 0).T
    g["x"] = x.reshape(KD, P, TOK).transpose(1, 0, 2)
    c = np.concatenate([f["c_prompt"], f["c_sample"]], 0).T
    g["cond"] = c.reshape(KD, P, 2).transpose(1, 0, 2)
    g["const"], g["mask"] = constants()
    g["ada"] = tiles(f["w_ada"], KD, 1)
    g["b_ada"] = np.repeat(f["b_ada"].reshape(DEPTH * N_ADA, P, 1), 2, axis=2).transpose(1, 0, 2)
    g["norm_g"] = f["norm_g"].reshape(DEPTH, 6 * KD, P).transpose(0, 2, 1)
    w1 = f["ffn_w1"].reshape(DEPTH * 2, D_MODEL, 2, D_FF)
    w1 = np.pad(w1, ((0, 0), (0, 0), (0, 0), (0, KF * P - D_FF)))
    w1 = w1.reshape(DEPTH * 2, D_MODEL, 2, KF, P).transpose(0, 1, 3, 2, 4).reshape(DEPTH * 2, D_MODEL, 2 * KF * P)
    g["f1"] = tiles(w1, KD, 1)
    w2 = f["ffn_w2"].reshape(DEPTH * 2, D_FF, D_MODEL)
    g["f2"] = tiles(np.pad(w2, ((0, 0), (0, KF * P - D_FF), (0, 0))), KF, 2)
    w = f["w_in"]
    fb0 = 3 * A_HEADS * HD + 3 * B_HEADS * HD
    uc0 = fb0 + B_HEADS
    gl0 = uc0 + 512
    fb = np.pad(w[:, :, fb0:uc0], ((0, 0), (0, 0), (0, P - B_HEADS)))

    def column_tile(c):
        return w[:, :, c:c + P]

    triples = [column_tile(uc0 + 256), column_tile(uc0 + 384), fb]
    for first, heads in ((3 * A_HEADS * HD, B_HEADS), (0, A_HEADS)):
        for pr in range(heads // 2):
            triples += [column_tile(first + part * heads * HD + pr * P) for part in range(3)]
    tri = tiles(np.concatenate(triples, 2), KD, 1).reshape(DEPTH * (NP + 1), 3, P, KD * P)
    tri = tri.transpose(0, 2, 1, 3).reshape(DEPTH * (NP + 1), P, 2, SLOT).transpose(0, 2, 1, 3)
    g["tri"] = tri.reshape(-1, P, SLOT)
    g["uc"] = tiles(w[:, :, uc0:uc0 + 256], KD, 1)
    gl = w[:, :, gl0:].reshape(DEPTH, D_MODEL, 3, KD, P)
    br = np.concatenate([f["w_br_a"], f["w_br_b"], f["w_br_c"]], 1).reshape(DEPTH, D_MODEL, 1, KD, P)
    g["gate"] = tiles(np.concatenate([gl, br], 2).transpose(0, 1, 3, 2, 4).reshape(DEPTH, D_MODEL, -1), KD, 1)
    g["wout"] = tiles(f["w_out"], KD, 1)
    g["b_gate"] = f["b_gate"].reshape(DEPTH, 3 * KD, P).transpose(0, 2, 1)
    g["b_forget"] = np.broadcast_to(f["b_forget"][:, None, :], (DEPTH, P, B_HEADS))
    g["c_gain"] = np.broadcast_to(f["c_vnorm_g"][:, None, :], (DEPTH, P, 256))
    cb = f["c_spatial_b"].reshape(DEPTH, 2, 2, 1, P)
    g["c_bias"] = np.broadcast_to(cb, (DEPTH, 2, 2, HD, P)).transpose(0, 2, 3, 1, 4).reshape(DEPTH, P, 2 * P)
    g["cache_f"] = f["cache_b_logf"][:, 0].reshape(DEPTH, 8, P, B_HEADS).transpose(0, 2, 1, 3).reshape(DEPTH, P, 64)
    g["c_spatial"] = f["c_spatial_w"].transpose(0, 3, 1, 2).reshape(DEPTH, P, C_GROUPS * P)
    for name in ("cache_a_k", "cache_a_v"):
        g[name] = f[name].reshape(DEPTH, A_WIN, A_HEADS * HD)
    p, c = np.arange(P)[:, None], np.arange(STRIP)[None, :]
    rel = np.clip(p - (c - 512), -(CHUNK - 1), REL_MAX) + CHUNK - 1
    strip = f["a_rel_bias"][:, :, rel].transpose(0, 2, 1, 3)
    strip = np.where(((p < CHUNK) & (c >= 512 + CHUNK))[None, :, None, :], np.float32(NEG), strip)
    g["strip"] = strip.reshape(DEPTH, P, A_PAIRS, 2 * STRIP).transpose(0, 2, 1, 3).reshape(-1, P, 2 * STRIP)
    for ab, heads, n in (("a", A_HEADS, A_WIN), ("b", B_HEADS, PAST)):
        k = f[f"cache_{ab}_k"][:, 0].reshape(DEPTH, n, heads // 2, P)
        g["ck_" + ab] = k.transpose(0, 2, 3, 1).reshape(-1, P, n)
        vv = f[f"cache_{ab}_v"][:, 0].reshape(DEPTH, n // P, P, heads // 2, P)
        g["cv_" + ab] = vv.transpose(0, 3, 2, 1, 4).reshape(-1, P, n)
    return {k: np.ascontiguousarray(x) for k, x in g.items()}


OUTS = {"h": (P, KD, TOK), "kv": (DEPTH, P, 12, TOK), "logf": (DEPTH, P, NT * B_HEADS), "vc": (DEPTH, DEC, 256),
        "roll_k": (DEPTH, A_WIN - DEC, A_HEADS * HD), "roll_v": (DEPTH, A_WIN - DEC, A_HEADS * HD)}


def kernel(**inputs):
    import concourse.bacc as bacc
    from concourse.bass_utils import run_bass_kernel_spmd

    nc = bacc.Bacc("TRN2", target_bir_lowering=False, num_devices=1)
    arrays = layout(inputs)
    ins = {k: nc.dram_tensor(f"in_{k}", a.shape, mybir.dt.from_np(a.dtype), kind="ExternalInput").ap()
           for k, a in arrays.items()}
    outs = {k: nc.dram_tensor(f"out_{k}", s, F32, kind="ExternalOutput").ap() for k, s in OUTS.items()}
    build_program(nc, ins, outs)
    r = run_bass_kernel_spmd(nc, [{f"in_{k}": a for k, a in arrays.items()}], core_ids=[0]).results[0]
    r = {k: np.asarray(r[f"out_{k}"]) for k in OUTS}

    h = r["h"].transpose(2, 1, 0).reshape(TOK, D_MODEL)
    kv = r["kv"].transpose(0, 3, 2, 1).reshape(DEPTH, TOK, 12 * P)
    ka, va, kb, vb = np.split(kv, [256, 512, 1024], axis=2)
    logf = r["logf"].reshape(DEPTH, P, NT, B_HEADS).transpose(0, 2, 1, 3).reshape(DEPTH, NT * P, B_HEADS)

    def prompt(t, heads):
        return np.ascontiguousarray(t[:, :SEQ]).reshape(DEPTH, 1, SEQ, heads, HD)

    def sample(t, heads, before=None):
        t = t[:, SEQ:TOK]
        if before is not None:
            t = np.concatenate([before, t], 1)
        return np.ascontiguousarray(t).reshape(DEPTH, 1, -1, heads, HD)

    return (np.ascontiguousarray(h[:SEQ])[None], np.ascontiguousarray(h[SEQ:])[None],
            prompt(ka, A_HEADS), prompt(va, A_HEADS), prompt(kb, B_HEADS), prompt(vb, B_HEADS),
            np.ascontiguousarray(logf[:, :SEQ])[:, None],
            sample(ka, A_HEADS, r["roll_k"]), sample(va, A_HEADS, r["roll_v"]),
            sample(kb, B_HEADS), sample(vb, B_HEADS),
            np.ascontiguousarray(logf[:, SEQ:TOK])[:, None], r["vc"][:, None])
```
